# Optimizing a Trainium2 kernel written in Bass

```python
import jax, jax.numpy as jnp
from jax import lax
import numpy as np
import math

D_MODEL = 1024
BATCH = 1
SEQ = 256
DEPTH = 2

GRID_W = 64
CTX_LEN = 256
EPS = 1e-6
NEG_INF = -1e30

NA_HEADS = 8
NA_HEAD_DIM = 64
NA_WIDTH = NA_HEADS * NA_HEAD_DIM
NA_KH = 8
NA_KW = 16
SGU_GROUPS = 8
SGU_WIDTH = D_MODEL - NA_WIDTH
SGU_GROUP_DIM = SGU_WIDTH // SGU_GROUPS
SGU_CHUNK = 128
HYB_IN = 3 * NA_WIDTH + 2 * SGU_WIDTH

RET_HEADS = 8
RET_QK_DIM = D_MODEL // RET_HEADS
RET_V_DIM = 2 * RET_QK_DIM
RET_QK_WIDTH = RET_HEADS * RET_QK_DIM
RET_V_WIDTH = RET_HEADS * RET_V_DIM
RET_CHUNK = 128
RET_IN = 2 * RET_QK_WIDTH + 2 * RET_V_WIDTH
ROPE_BASE = 10000.0

D_FF = 2816
CONV_W = 3

N_EVEN = (DEPTH + 1) // 2
N_ODD = DEPTH // 2


def rmsnorm(x, g):
    xf = x.astype(jnp.float32)
    y = xf * lax.rsqrt(jnp.mean(xf * xf, axis=-1, keepdims=True) + EPS)
    return (y * g.astype(jnp.float32)).astype(x.dtype)

def modulate(x, shift, scale):
    return x * (1 + scale) + shift

def axial_rope(n_tokens, head_dim):
    t = jnp.arange(n_tokens)
    row = (t // GRID_W).astype(jnp.float32)
    col = (t % GRID_W).astype(jnp.float32)
    n_freq = head_dim // 4
    inv = ROPE_BASE ** (-jnp.arange(n_freq, dtype=jnp.float32) / n_freq)
    ang = jnp.concatenate([row[:, None] * inv, col[:, None] * inv], axis=-1)
    return jnp.cos(ang), jnp.sin(ang)

def apply_rope(x, cos, sin):
    x1, x2 = jnp.split(x, 2, axis=-1)
    c = cos[None, :, None, :]
    s = sin[None, :, None, :]
    return jnp.concatenate([x1 * c - x2 * s, x1 * s + x2 * c], axis=-1).astype(x.dtype)

def neighbourhood_attention(q, k, v, k_ctx, v_ctx, rpb):
    B, T, H, dh = q.shape
    rows = T // GRID_W
    kh = min(NA_KH, rows)
    kw = NA_KW
    scale = dh ** -0.5
    qg = q.reshape(B, rows, GRID_W, H, dh)
    kg = k.reshape(B, rows, GRID_W, H, dh)
    vg = v.reshape(B, rows, GRID_W, H, dh)
    r = jnp.arange(rows)
    r0 = jnp.clip(r - kh // 2, 0, rows - kh)
    key_rows = r0[:, None] + jnp.arange(kh)[None, :]
    k_blk = kg[:, key_rows].reshape(B, rows, kh * GRID_W, H, dh)
    v_blk = vg[:, key_rows].reshape(B, rows, kh * GRID_W, H, dh)
    s_nb = jnp.einsum('brqhd,brkhd->bhrqk', qg, k_blk,
                      preferred_element_type=jnp.float32) * scale
    cidx = jnp.arange(GRID_W)
    c0 = jnp.clip(cidx - kw // 2, 0, GRID_W - kw)
    in_win = (cidx[None, :] >= c0[:, None]) & (cidx[None, :] < c0[:, None] + kw)
    mask = jnp.broadcast_to(in_win[:, None, :], (GRID_W, kh, GRID_W)).reshape(GRID_W, kh * GRID_W)
    dr = key_rows - r[:, None] + (NA_KH - 1)
    dc = jnp.clip(cidx[None, :] - cidx[:, None], -(kw - 1), kw - 1) + (kw - 1)
    bias = rpb[:, dr[:, None, :, None], dc[None, :, None, :]]
    bias = bias.reshape(H, rows, GRID_W, kh * GRID_W).astype(jnp.float32)
    s_nb = jnp.where(mask, s_nb + bias[None], NEG_INF)
    s_cx = jnp.einsum('brqhd,bchd->bhrqc', qg, k_ctx,
                      preferred_element_type=jnp.float32) * scale
    p = jax.nn.softmax(jnp.concatenate([s_nb, s_cx], axis=-1), axis=-1)
    n_nb = kh * GRID_W
    p_nb = p[..., :n_nb].astype(v.dtype)
    p_cx = p[..., n_nb:].astype(v.dtype)
    o = (jnp.einsum('bhrqk,brkhd->brqhd', p_nb, v_blk)
         + jnp.einsum('bhrqc,bchd->brqhd', p_cx, v_ctx))
    return o.reshape(B, T, H * dh).astype(q.dtype)

def context_attention(q, k, v):
    B, L, H, dh = q.shape
    s = jnp.einsum('bqhd,bkhd->bhqk', q, k, preferred_element_type=jnp.float32) * dh ** -0.5
    p = jax.nn.softmax(s, axis=-1).astype(v.dtype)
    return jnp.einsum('bhqk,bkhd->bqhd', p, v).reshape(B, L, H * dh).astype(q.dtype)

def spatial_gating(u, v, w_s, b_s):
    B, N, _ = v.shape
    vf = v.astype(jnp.float32)
    mu = jnp.mean(vf, axis=-1, keepdims=True)
    var = jnp.mean(jnp.square(vf - mu), axis=-1, keepdims=True)
    vn = ((vf - mu) * lax.rsqrt(var + EPS)).astype(v.dtype)
    vc = vn.reshape(B, N // SGU_CHUNK, SGU_CHUNK, SGU_GROUPS, SGU_GROUP_DIM)
    mixed = jnp.einsum('gpq,bnqgc->bnpgc', w_s, vc) + b_s.T[None, None, :, :, None]
    return u * mixed.reshape(B, N, SGU_WIDTH)

def hybrid_na_sgu(h_ctx, h_lat, w_in, rpb, w_s, b_s, w_out, ctx_out):
    heads = lambda a: a.reshape(a.shape[0], a.shape[1], NA_HEADS, NA_HEAD_DIM)
    splits = [NA_WIDTH, 2 * NA_WIDTH, 3 * NA_WIDTH, 3 * NA_WIDTH + SGU_WIDTH]
    q, k, v, u, g = jnp.split(h_lat @ w_in, splits, axis=-1)
    if ctx_out:
        qc, kc, vc, uc, gc = jnp.split(h_ctx @ w_in, splits, axis=-1)
    else:
        kc, vc = jnp.split(h_ctx @ w_in[:, NA_WIDTH:3 * NA_WIDTH], 2, axis=-1)
    a_lat = neighbourhood_attention(heads(q), heads(k), heads(v), heads(kc), heads(vc), rpb)
    s_lat = spatial_gating(jax.nn.gelu(u), jax.nn.gelu(g), w_s, b_s)
    y_lat = jnp.concatenate([a_lat, s_lat], axis=-1) @ w_out
    y_ctx = None
    if ctx_out:
        a_ctx = context_attention(heads(qc), heads(kc), heads(vc))
        s_ctx = spatial_gating(jax.nn.gelu(uc), jax.nn.gelu(gc), w_s, b_s)
        y_ctx = jnp.concatenate([a_ctx, s_ctx], axis=-1) @ w_out
    return y_ctx, y_lat

def retention_chunked(q, k, v, lg, state0):
    B, N, H, dk = q.shape
    dv = v.shape[-1]
    C = RET_CHUNK
    n = N // C
    to_chunks = lambda a: a.reshape(B, n, C, H, a.shape[-1]).transpose(1, 0, 3, 2, 4)
    pos = jnp.arange(C, dtype=jnp.float32)
    diff = pos[:, None] - pos[None, :]
    lower = diff >= 0
    decay_intra = jnp.where(lower[None], jnp.exp(lg[:, None, None] * jnp.where(lower, diff, 0.0)[None]), 0.0)
    decay_q = jnp.exp(lg[:, None] * (pos + 1.0))[None, :, :, None]
    decay_k = jnp.exp(lg[:, None] * (C - 1.0 - pos))[None, :, :, None]
    decay_chunk = jnp.exp(lg * C)[None, :, None, None]

    def step(S, blk):
        qb, kb, vb = blk
        qf = qb.astype(jnp.float32)
        kf = kb.astype(jnp.float32)
        vf = vb.astype(jnp.float32)
        s = jnp.einsum('bhqd,bhkd->bhqk', qf, kf) * decay_intra
        o = jnp.einsum('bhqk,bhkv->bhqv', s, vf) + jnp.einsum('bhqd,bhdv->bhqv', qf * decay_q, S)
        S = S * decay_chunk + jnp.einsum('bhkd,bhkv->bhdv', kf * decay_k, vf)
        return S, o

    _, o = lax.scan(step, state0, (to_chunks(q), to_chunks(k), to_chunks(v)))
    return o.transpose(1, 0, 3, 2, 4).reshape(B, N, H, dv)

def retention_final_state(k, v, lg):
    L = k.shape[1]
    w = jnp.exp(lg[None, :] * (L - 1.0 - jnp.arange(L, dtype=jnp.float32))[:, None])
    return jnp.einsum('blhd,blhv->bhdv', k.astype(jnp.float32) * w[None, :, :, None], v.astype(jnp.float32))

def retention_output(o, g, gn_g, w_out):
    B, N = o.shape[0], o.shape[1]
    mu = jnp.mean(o, axis=-1, keepdims=True)
    var = jnp.mean(jnp.square(o - mu), axis=-1, keepdims=True)
    on = ((o - mu) * lax.rsqrt(var + EPS)).reshape(B, N, RET_V_WIDTH) * gn_g.astype(jnp.float32)
    return (jax.nn.silu(g) * on.astype(g.dtype)) @ w_out

def retention_mixer(h_ctx, h_lat, w_in, log_decay, gn_g, w_out, ctx_out):
    B, T, _ = h_lat.shape
    L = h_ctx.shape[1]
    H, dk, dv = RET_HEADS, RET_QK_DIM, RET_V_DIM
    splits = [RET_QK_WIDTH, 2 * RET_QK_WIDTH, 2 * RET_QK_WIDTH + RET_V_WIDTH]
    q, k, v, g = jnp.split(h_lat @ w_in, splits, axis=-1)
    cos, sin = axial_rope(T, dk)
    q = apply_rope(q.reshape(B, T, H, dk), cos, sin)
    k = apply_rope(k.reshape(B, T, H, dk) * dk ** -0.5, cos, sin)
    v = v.reshape(B, T, H, dv)
    if ctx_out:
        qc, kc, vc, gc = jnp.split(h_ctx @ w_in, splits, axis=-1)
        qc = qc.reshape(B, L, H, dk)
    else:
        kc, vc = jnp.split(h_ctx @ w_in[:, RET_QK_WIDTH:2 * RET_QK_WIDTH + RET_V_WIDTH], [RET_QK_WIDTH], axis=-1)
    kc = kc.reshape(B, L, H, dk) * dk ** -0.5
    vc = vc.reshape(B, L, H, dv)
    outs_lat = []
    outs_ctx = []
    for d in range(2):
        lg = log_decay[d].astype(jnp.float32)
        rev = (lambda a: a[:, ::-1]) if d == 1 else (lambda a: a)
        s_ctx = retention_final_state(rev(kc), rev(vc), lg)
        outs_lat.append(rev(retention_chunked(rev(q), rev(k), rev(v), lg, s_ctx)))
        if ctx_out:
            outs_ctx.append(rev(retention_chunked(rev(qc), rev(kc), rev(vc), lg, jnp.zeros_like(s_ctx))))
    y_lat = retention_output(outs_lat[0] + outs_lat[1], g, gn_g, w_out)
    y_ctx = None
    if ctx_out:
        y_ctx = retention_output(outs_ctx[0] + outs_ctx[1], gc, gn_g, w_out)
    return y_ctx, y_lat

def dwconv3(x, w, b):
    xp = jnp.pad(x, ((0, 0), (1, 1), (0, 0)))
    return xp[:, :-2] * w[0] + xp[:, 1:-1] * w[1] + xp[:, 2:] * w[2] + b

def conv_ffn(h, w_in, conv_w, conv_b, w_out):
    a = dwconv3(h @ w_in, conv_w, conv_b)
    gate, up = jnp.split(a, 2, axis=-1)
    return (jax.nn.silu(gate) * up) @ w_out

def first_inputs(seed: int = 0) -> dict:
    key = jax.random.key(seed)
    ks = jax.random.split(key, 20)
    nrm = lambda k, shape, s: jax.random.normal(k, shape, jnp.float32) * s
    base_decay = np.log1p(-2.0 ** (-5.0 - np.arange(RET_HEADS))).astype(np.float32)
    return {
        "x": nrm(ks[0], (BATCH, SEQ, D_MODEL), 1.0),
        "c": nrm(ks[1], (BATCH, D_MODEL), 1.0),
        "ctx": nrm(ks[2], (BATCH, CTX_LEN, D_MODEL), 1.0),
        "c_ctx": nrm(ks[3], (D_MODEL,), 1.0),
        "ada_w": nrm(ks[4], (DEPTH, D_MODEL, 6 * D_MODEL), 0.5 * D_MODEL ** -0.5),
        "ada_b": nrm(ks[5], (DEPTH, 6 * D_MODEL), 0.02),
        "norm_g": 1.0 + nrm(ks[6], (DEPTH, 4, D_MODEL), 0.1),
        "hyb_w_in": nrm(ks[7], (N_EVEN, D_MODEL, HYB_IN), D_MODEL ** -0.5),
        "na_rpb": nrm(ks[8], (N_EVEN, NA_HEADS, 2 * NA_KH - 1, 2 * NA_KW - 1), 0.1),
        "sgu_w": nrm(ks[9], (N_EVEN, SGU_GROUPS, SGU_CHUNK, SGU_CHUNK), SGU_CHUNK ** -0.5),
        "sgu_b": 1.0 + nrm(ks[10], (N_EVEN, SGU_GROUPS, SGU_CHUNK), 0.1),
        "hyb_w_out": nrm(ks[11], (N_EVEN, D_MODEL, D_MODEL), D_MODEL ** -0.5),
        "ret_w_in": nrm(ks[12], (N_ODD, D_MODEL, RET_IN), D_MODEL ** -0.5),
        "ret_log_decay": jnp.asarray(base_decay)[None, None, :] * (1.0 + nrm(ks[13], (N_ODD, 2, RET_HEADS), 0.05)),
        "ret_gn_g": 1.0 + nrm(ks[14], (N_ODD, RET_V_WIDTH), 0.1),
        "ret_w_out": nrm(ks[15], (N_ODD, RET_V_WIDTH, D_MODEL), RET_V_WIDTH ** -0.5),
        "ffn_w_in": nrm(ks[16], (DEPTH, D_MODEL, 2 * D_FF), D_MODEL ** -0.5),
        "ffn_conv_w": nrm(ks[17], (DEPTH, CONV_W, 2 * D_FF), CONV_W ** -0.5),
        "ffn_conv_b": nrm(ks[18], (DEPTH, 2 * D_FF), 0.02),
        "ffn_w_out": nrm(ks[19], (DEPTH, D_FF, D_MODEL), D_FF ** -0.5),
    }

def first_block(x, c, ctx, c_ctx, ada_w, ada_b, norm_g, hyb_w_in, na_rpb, sgu_w, sgu_b, hyb_w_out,
              ret_w_in, ret_log_decay, ret_gn_g, ret_w_out, ffn_w_in, ffn_conv_w, ffn_conv_b, ffn_w_out):
    xc = ctx
    silu_c = jax.nn.silu(c)
    silu_cc = jax.nn.silu(c_ctx)
    for i in range(DEPTH):
        ctx_out = i < DEPTH - 1
        j = i // 2
        mod_lat = (silu_c @ ada_w[i] + ada_b[i])[:, None, :]
        mod_ctx = (silu_cc @ ada_w[i] + ada_b[i])[None, None, :]
        sh1, sc1, g1, sh2, sc2, g2 = jnp.split(mod_lat, 6, axis=-1)
        csh1, csc1, cg1, csh2, csc2, cg2 = jnp.split(mod_ctx, 6, axis=-1)
        h_lat = modulate(rmsnorm(x, norm_g[i, 0]), sh1, sc1)
        h_ctx = modulate(rmsnorm(xc, norm_g[i, 0]), csh1, csc1)
        if i % 2 == 0:
            y_ctx, y_lat = hybrid_na_sgu(h_ctx, h_lat, hyb_w_in[j], na_rpb[j], sgu_w[j], sgu_b[j],
                                         hyb_w_out[j], ctx_out)
        else:
            y_ctx, y_lat = retention_mixer(h_ctx, h_lat, ret_w_in[j], ret_log_decay[j], ret_gn_g[j],
                                           ret_w_out[j], ctx_out)
        x = x + g1 * rmsnorm(y_lat, norm_g[i, 1])
        h = modulate(rmsnorm(x, norm_g[i, 2]), sh2, sc2)
        x = x + g2 * rmsnorm(conv_ffn(h, ffn_w_in[i], ffn_conv_w[i], ffn_conv_b[i], ffn_w_out[i]), norm_g[i, 3])
        if ctx_out:
            xc = xc + cg1 * rmsnorm(y_ctx, norm_g[i, 1])
            hc = modulate(rmsnorm(xc, norm_g[i, 2]), csh2, csc2)
            xc = xc + cg2 * rmsnorm(conv_ffn(hc, ffn_w_in[i], ffn_conv_w[i], ffn_conv_b[i], ffn_w_out[i]), norm_g[i, 3])
    return x


N_META = 16
A_HEADS = 4
A_WIDTH = D_MODEL
A_HEAD_DIM = A_WIDTH // A_HEADS
A_CHUNK = 64
B_WIDTH = D_MODEL
B_BLOCKS = 8
B_BLOCK_DIM = B_WIDTH // B_BLOCKS
B_CONV = 4
LRU_C = 8.0
C_HEADS = D_MODEL // 128
C_QK_DIM = D_MODEL // (2 * C_HEADS)
C_V_DIM = 2 * C_QK_DIM
ROT_DIM = C_QK_DIM // 4
ROPE_THETA = 500000.0
Q_BLOCK = 128
D_FF_2 = 4 * D_MODEL
N_AB = (DEPTH + 1) // 2
N_C = DEPTH // 2
AB_SPLITS = [A_WIDTH, A_WIDTH, A_WIDTH, A_WIDTH, A_HEADS, A_HEADS, B_WIDTH, B_WIDTH]
AB_IN = sum(AB_SPLITS)
C_SPLITS = [C_HEADS * 2 * C_QK_DIM, C_HEADS * 2 * C_QK_DIM, C_HEADS * C_V_DIM]
C_IN = sum(C_SPLITS)


def _rmsnorm(x, g):
    xf = x.astype(jnp.float32)
    y = xf * lax.rsqrt(jnp.mean(xf * xf, axis=-1, keepdims=True) + EPS)
    return (y * g.astype(jnp.float32)).astype(x.dtype)

def _split(a, sizes):
    return jnp.split(a, np.cumsum(sizes)[:-1].tolist(), axis=-1)

def _mlstm_chunk(state, inp):
    c_mem, n_mem, m_prev = state
    q, k, v, log_i, log_f = inp
    L = q.shape[2]
    b = jnp.cumsum(log_f, axis=-1)
    causal = jnp.tril(jnp.ones((L, L), dtype=bool))
    log_d = b[..., :, None] - b[..., None, :] + log_i[..., None, :]
    log_d = jnp.where(causal, log_d, -jnp.inf)
    log_prev = b + m_prev[..., None]
    m_t = jnp.maximum(log_prev, jnp.max(log_d, axis=-1))
    d = jnp.exp(log_d - m_t[..., None])
    w_prev = jnp.exp(log_prev - m_t)
    s = jnp.einsum('bhtd,bhsd->bhts', q, k) * d
    num = (w_prev[..., None] * jnp.einsum('bhvk,bhtk->bhtv', c_mem, q)
           + jnp.einsum('bhts,bhsv->bhtv', s, v))
    den = w_prev * jnp.einsum('bhk,bhtk->bht', n_mem, q) + jnp.sum(s, axis=-1)
    h = num / jnp.maximum(jnp.abs(den), jnp.exp(-m_t))[..., None]
    log_end = b[..., -1:] - b + log_i
    m_new = jnp.maximum(b[..., -1] + m_prev, jnp.max(log_end, axis=-1))
    w_s = jnp.exp(log_end - m_new[..., None])
    decay = jnp.exp(b[..., -1] + m_prev - m_new)
    c_new = decay[..., None, None] * c_mem + jnp.einsum('bhs,bhsv,bhsk->bhvk', w_s, v, k)
    n_new = decay[..., None] * n_mem + jnp.einsum('bhs,bhsk->bhk', w_s, k)
    return (c_new, n_new, m_new), h

def _mlstm(q, k, v, i_pre, f_pre):
    bsz, t_all, nh, dh = q.shape
    seq = t_all - N_META
    nc = seq // A_CHUNK
    q = q.transpose(0, 2, 1, 3)
    k = k.transpose(0, 2, 1, 3) * (dh ** -0.5)
    v = v.transpose(0, 2, 1, 3)
    log_i = i_pre.transpose(0, 2, 1)
    log_f = jax.nn.log_sigmoid(f_pre).transpose(0, 2, 1)
    state = (jnp.zeros((bsz, nh, dh, dh), jnp.float32),
             jnp.zeros((bsz, nh, dh), jnp.float32),
             jnp.zeros((bsz, nh), jnp.float32))
    state, h_meta = _mlstm_chunk(
        state, (q[:, :, :N_META], k[:, :, :N_META], v[:, :, :N_META],
                log_i[:, :, :N_META], log_f[:, :, :N_META]))

    def chunks(a):
        a = a[:, :, N_META:]
        return jnp.moveaxis(a.reshape(bsz, nh, nc, A_CHUNK, *a.shape[3:]), 2, 0)

    _, h_rest = lax.scan(_mlstm_chunk, state,
                         (chunks(q), chunks(k), chunks(v), chunks(log_i), chunks(log_f)))
    h_rest = jnp.moveaxis(h_rest, 0, 2).reshape(bsz, nh, seq, dh)
    h = jnp.concatenate([h_meta, h_rest], axis=2)
    return h.transpose(0, 2, 1, 3)

def _rg_lru_branch(xb, gate, conv_w, conv_b, w_r, b_r, w_i, b_i, lam):
    bsz, t_all, w = xb.shape
    xc = lax.conv_general_dilated(
        xb.astype(jnp.float32), conv_w.astype(jnp.float32)[:, None, :],
        window_strides=(1,), padding=[(B_CONV - 1, 0)],
        dimension_numbers=('NWC', 'WIO', 'NWC'), feature_group_count=w)
    xc = xc + conv_b.astype(jnp.float32)
    xg = xc.reshape(bsz, t_all, B_BLOCKS, B_BLOCK_DIM)
    r = jax.nn.sigmoid(jnp.einsum('btnd,nde->btne', xg, w_r.astype(jnp.float32)).reshape(bsz, t_all, w)
                       + b_r.astype(jnp.float32))
    i = jax.nn.sigmoid(jnp.einsum('btnd,nde->btne', xg, w_i.astype(jnp.float32)).reshape(bsz, t_all, w)
                       + b_i.astype(jnp.float32))
    log_a = -LRU_C * r * jax.nn.softplus(-lam.astype(jnp.float32))
    a = jnp.exp(log_a)
    u = jnp.sqrt(-jnp.expm1(2.0 * log_a)) * (i * xc)

    def combine(left, right):
        a1, b1 = left
        a2, b2 = right
        return a1 * a2, a2 * b1 + b2

    _, h = lax.associative_scan(combine, (a, u), axis=1)
    return h * jax.nn.gelu(gate.astype(jnp.float32))

def _ab_mixer(hn, w_in, if_bias, mlstm_norm, conv_w, conv_b, w_r, b_r, w_i, b_i, lam, w_out):
    bsz, t_all, _ = hn.shape
    proj = hn @ w_in
    q, k, v, o, gi, gf, xb, gate = _split(proj, AB_SPLITS)
    f32 = jnp.float32
    hs = (bsz, t_all, A_HEADS, A_HEAD_DIM)
    ifb = if_bias.astype(f32)
    h_a = _mlstm(q.astype(f32).reshape(hs), k.astype(f32).reshape(hs), v.astype(f32).reshape(hs),
                 gi.astype(f32) + ifb[:A_HEADS], gf.astype(f32) + ifb[A_HEADS:])
    h_a = jax.nn.sigmoid(o.astype(f32)).reshape(hs) * h_a
    h_a = h_a * lax.rsqrt(jnp.mean(h_a * h_a, axis=-1, keepdims=True) + EPS)
    h_a = (h_a * mlstm_norm.astype(f32).reshape(A_HEADS, A_HEAD_DIM)).reshape(bsz, t_all, A_WIDTH)
    h_b = _rg_lru_branch(xb, gate, conv_w, conv_b, w_r, b_r, w_i, b_i, lam)
    y = jnp.concatenate([h_a, h_b], axis=-1).astype(hn.dtype)
    return y @ w_out

def _partial_rope(x, cos, sin):
    half = ROT_DIM // 2
    x1, x2, rest = x[..., :half], x[..., half:ROT_DIM], x[..., ROT_DIM:]
    c = cos[:, None, None, :]
    s = sin[:, None, None, :]
    return jnp.concatenate([x1 * c - x2 * s, x2 * c + x1 * s, rest], axis=-1)

def _diff_attend(qb, q_pos, kh, vh, k_pos, lam):
    s = jnp.einsum('bhcqd,bhckd->bhcqk', qb, kh)
    mask = k_pos[None, :] <= q_pos[:, None]
    p = jax.nn.softmax(jnp.where(mask, s, -jnp.inf), axis=-1)
    pd = p[:, :, 0] - lam * p[:, :, 1]
    return jnp.einsum('bhqk,bhkv->bhqv', pd, vh)

def _diff_attn(hn, w_in, lam_vecs, subln, w_out, lambda_init):
    bsz, t_all, _ = hn.shape
    seq = t_all - N_META
    f32 = jnp.float32
    q, k, v = _split(hn @ w_in, C_SPLITS)
    q = q.astype(f32).reshape(bsz, t_all, C_HEADS, 2, C_QK_DIM)
    k = k.astype(f32).reshape(bsz, t_all, C_HEADS, 2, C_QK_DIM)
    v = v.astype(f32).reshape(bsz, t_all, C_HEADS, C_V_DIM)
    pos = jnp.arange(t_all, dtype=jnp.int32)
    inv_freq = jnp.power(jnp.float32(ROPE_THETA), -jnp.arange(0, ROT_DIM, 2, dtype=f32) / ROT_DIM)
    ang = pos.astype(f32)[:, None] * inv_freq[None, :]
    cos, sin = jnp.cos(ang), jnp.sin(ang)
    q = _partial_rope(q, cos, sin) * (C_QK_DIM ** -0.5)
    k = _partial_rope(k, cos, sin)
    lv = lam_vecs.astype(f32)
    lam = jnp.exp(jnp.sum(lv[0] * lv[1])) - jnp.exp(jnp.sum(lv[2] * lv[3])) + lambda_init
    qh = q.transpose(0, 2, 3, 1, 4)
    kh = k.transpose(0, 2, 3, 1, 4)
    vh = v.transpose(0, 2, 1, 3)
    o_meta = _diff_attend(qh[:, :, :, :N_META], pos[:N_META], kh[:, :, :, :N_META],
                          vh[:, :, :N_META], pos[:N_META], lam)
    nb = seq // Q_BLOCK
    q_blocks = jnp.moveaxis(qh[:, :, :, N_META:].reshape(bsz, C_HEADS, 2, nb, Q_BLOCK, C_QK_DIM), 3, 0)
    pos_blocks = pos[N_META:].reshape(nb, Q_BLOCK)
    o_rest = lax.map(lambda a: _diff_attend(a[0], a[1], kh, vh, pos, lam), (q_blocks, pos_blocks))
    o_rest = jnp.moveaxis(o_rest, 0, 2).reshape(bsz, C_HEADS, seq, C_V_DIM)
    o = jnp.concatenate([o_meta, o_rest], axis=2)
    o = o * lax.rsqrt(jnp.mean(o * o, axis=-1, keepdims=True) + EPS) * subln.astype(f32)
    o = o * (1.0 - lambda_init)
    o = o.transpose(0, 2, 1, 3).reshape(bsz, t_all, C_HEADS * C_V_DIM).astype(hn.dtype)
    return o @ w_out

def _sq_relu_mlp(hn, w1, w2):
    a = jax.nn.relu(hn @ w1)
    return (a * a) @ w2

def second_inputs(seed: int = 0) -> dict:
    key = jax.random.key(seed)
    ks = jax.random.split(key, 24)
    f32 = jnp.float32

    def nrm(k, shape, scale):
        return jax.random.normal(k, shape, f32) * scale

    x = nrm(ks[0], (BATCH, SEQ, D_MODEL), 1.0)
    meta_tokens = nrm(ks[1], (N_META, D_MODEL), 1.0)
    norm_mix = 1.0 + nrm(ks[2], (DEPTH, D_MODEL), 0.05)
    norm_mlp = 1.0 + nrm(ks[3], (DEPTH, D_MODEL), 0.05)
    norm_final = 1.0 + nrm(ks[4], (D_MODEL,), 0.05)
    ab_w_in = nrm(ks[5], (N_AB, D_MODEL, AB_IN), D_MODEL ** -0.5)
    i_b = -1.0 + nrm(ks[6], (N_AB, A_HEADS), 0.1)
    f_b = jnp.linspace(3.0, 6.0, A_HEADS, dtype=f32)[None, :] + nrm(ks[7], (N_AB, A_HEADS), 0.1)
    ab_if_bias = jnp.concatenate([i_b, f_b], axis=-1)
    mlstm_norm = 1.0 + nrm(ks[8], (N_AB, A_WIDTH), 0.05)
    lru_conv_w = nrm(ks[9], (N_AB, B_CONV, B_WIDTH), B_CONV ** -0.5)
    lru_conv_b = nrm(ks[10], (N_AB, B_WIDTH), 0.01)
    lru_w_r = nrm(ks[11], (N_AB, B_BLOCKS, B_BLOCK_DIM, B_BLOCK_DIM), B_BLOCK_DIM ** -0.5)
    lru_b_r = nrm(ks[12], (N_AB, B_WIDTH), 0.01)
    lru_w_i = nrm(ks[13], (N_AB, B_BLOCKS, B_BLOCK_DIM, B_BLOCK_DIM), B_BLOCK_DIM ** -0.5)
    lru_b_i = nrm(ks[14], (N_AB, B_WIDTH), 0.01)
    u = jax.random.uniform(ks[15], (N_AB, B_WIDTH), f32, 0.9, 0.999)
    p = u ** (1.0 / LRU_C)
    lru_lambda = jnp.log(p) - jnp.log1p(-p)
    ab_w_out = nrm(ks[16], (N_AB, A_WIDTH + B_WIDTH, D_MODEL), (A_WIDTH + B_WIDTH) ** -0.5)
    c_w_in = nrm(ks[17], (N_C, D_MODEL, C_IN), D_MODEL ** -0.5)
    c_lambda = nrm(ks[18], (N_C, 4, C_QK_DIM), 0.1)
    c_subln = 1.0 + nrm(ks[19], (N_C, C_V_DIM), 0.05)
    c_w_out = nrm(ks[20], (N_C, C_HEADS * C_V_DIM, D_MODEL), (C_HEADS * C_V_DIM) ** -0.5)
    mlp_w1 = nrm(ks[21], (DEPTH, D_MODEL, D_FF_2), D_MODEL ** -0.5)
    mlp_w2 = nrm(ks[22], (DEPTH, D_FF_2, D_MODEL), D_FF_2 ** -0.5)
    return {"x": x, "meta_tokens": meta_tokens, "norm_mix": norm_mix, "norm_mlp": norm_mlp,
            "norm_final": norm_final, "ab_w_in": ab_w_in, "ab_if_bias": ab_if_bias,
            "mlstm_norm": mlstm_norm, "lru_conv_w": lru_conv_w, "lru_conv_b": lru_conv_b,
            "lru_w_r": lru_w_r, "lru_b_r": lru_b_r, "lru_w_i": lru_w_i, "lru_b_i": lru_b_i,
            "lru_lambda": lru_lambda, "ab_w_out": ab_w_out, "c_w_in": c_w_in,
            "c_lambda": c_lambda, "c_subln": c_subln, "c_w_out": c_w_out,
            "mlp_w1": mlp_w1, "mlp_w2": mlp_w2}

def second_block(x, meta_tokens, norm_mix, norm_mlp, norm_final, ab_w_in, ab_if_bias,
              mlstm_norm, lru_conv_w, lru_conv_b, lru_w_r, lru_b_r, lru_w_i, lru_b_i,
              lru_lambda, ab_w_out, c_w_in, c_lambda, c_subln, c_w_out, mlp_w1, mlp_w2):
    bsz = x.shape[0]
    meta = jnp.broadcast_to(meta_tokens[None].astype(x.dtype), (bsz, N_META, x.shape[-1]))
    h = jnp.concatenate([meta, x], axis=1)
    for layer in range(DEPTH):
        j = layer // 2
        hn = _rmsnorm(h, norm_mix[layer])
        if layer % 2 == 0:
            h = h + _ab_mixer(hn, ab_w_in[j], ab_if_bias[j], mlstm_norm[j], lru_conv_w[j],
                              lru_conv_b[j], lru_w_r[j], lru_b_r[j], lru_w_i[j], lru_b_i[j],
                              lru_lambda[j], ab_w_out[j])
        else:
            lambda_init = 0.8 - 0.6 * math.exp(-0.3 * layer)
            h = h + _diff_attn(hn, c_w_in[j], c_lambda[j], c_subln[j], c_w_out[j], lambda_init)
        h = h + _sq_relu_mlp(_rmsnorm(h, norm_mlp[layer]), mlp_w1[layer], mlp_w2[layer])
    h = _rmsnorm(h, norm_final)
    return h[:, N_META:, :]


def setup_inputs(seed=0):
    out = dict(first_inputs(seed))
    for name, value in second_inputs(seed + 1).items():
        if name != "x":
            out[name + "_2"] = value
    return out


def reference(
    x, c, ctx, c_ctx, ada_w, ada_b, norm_g, hyb_w_in, na_rpb, sgu_w, sgu_b, hyb_w_out, ret_w_in,
    ret_log_decay, ret_gn_g, ret_w_out, ffn_w_in, ffn_conv_w, ffn_conv_b, ffn_w_out,
    meta_tokens_2, norm_mix_2, norm_mlp_2, norm_final_2, ab_w_in_2, ab_if_bias_2, mlstm_norm_2,
    lru_conv_w_2, lru_conv_b_2, lru_w_r_2, lru_b_r_2, lru_w_i_2, lru_b_i_2, lru_lambda_2,
    ab_w_out_2, c_w_in_2, c_lambda_2, c_subln_2, c_w_out_2, mlp_w1_2, mlp_w2_2,
):
    x = first_block(
        x, c, ctx, c_ctx, ada_w, ada_b, norm_g, hyb_w_in, na_rpb, sgu_w, sgu_b, hyb_w_out,
        ret_w_in, ret_log_decay, ret_gn_g, ret_w_out, ffn_w_in, ffn_conv_w, ffn_conv_b,
        ffn_w_out,
    )
    return second_block(
        x, meta_tokens_2, norm_mix_2, norm_mlp_2, norm_final_2, ab_w_in_2, ab_if_bias_2,
        mlstm_norm_2, lru_conv_w_2, lru_conv_b_2, lru_w_r_2, lru_b_r_2, lru_w_i_2, lru_b_i_2,
        lru_lambda_2, ab_w_out_2, c_w_in_2, c_lambda_2, c_subln_2, c_w_out_2, mlp_w1_2,
        mlp_w2_2,
    )


_drawn_inputs = setup_inputs


def setup_inputs(seed=0):
    import zlib

    import numpy as np

    out = dict(_drawn_inputs(seed))
    spreads = {}
    factors = {'na_rpb': 21.572,
     'ffn_conv_b': 3.295,
     'lru_conv_b_2': 3.748,
     'lru_b_r_2': 64.0,
     'lru_b_i_2': 63.764,
     'c_lambda_2': 8.0,
     'c_subln_2': 3.688}
    for name, (base, spread) in spreads.items():
        noise = np.random.default_rng([zlib.crc32(name.encode()), seed]).standard_normal(out[name].shape)
        drawn = base * np.exp(spread * noise) if base else spread * noise
        out[name] = __import__('jax').numpy.asarray(drawn.astype(out[name].dtype))
    for name, factor in factors.items():
        out[name] = (out[name] * factor).astype(out[name].dtype)
    return out
```

```python
from contextlib import ExitStack
import math

import numpy as np

import concourse.bass as bass
from concourse import mybir

F32 = mybir.dt.float32
F32R = mybir.dt.float32r
ALU = mybir.AluOpType
ACT = mybir.ActivationFunctionType
AX = mybir.AxisListType

P = 128
D = 1024
DC = D // P
SEQ = 256
CTX = 256
META = 16
T1 = CTX + SEQ
T2 = META + SEQ
LAT = CTX
X2 = CTX - META
EPS = 1e-6
SLOT = 2048
FFH = 11
MLH = 16
GRID_W = 64
NEG = -1e30

TILES2 = [(0, 128), (128, 128), (256, 16)]


def _columns():
    at, n = {}, 0
    for name, width in [
        ("c", 16), ("norm_g", 64), ("ada_b", 96), ("conv_w", 2 * 3 * 44), ("conv_b", 2 * 44), ("gn_g", 16),
        ("decay", 16), ("norm_mix", 16), ("norm_mlp", 16), ("norm_final", 8),
        ("mlstm_norm", 8), ("lru_conv_w", 32), ("lru_conv_b", 8), ("lru_b_r", 8), ("lru_b_i", 8),
        ("lru_lam", 8), ("subln", 1), ("lambda", 256), ("if_bias", 2), ("eps", 1), ("pad", 5),
    ]:
        at[name] = n
        n += width
    return at, n


VEC, NVEC = _columns()


class Proj:

    def __init__(self, name, n, K, C, T, kind="feat", freed_by="dve"):
        self.name, self.n, self.K, self.C, self.T, self.kind, self.freed_by = name, n, K, C, T, kind, freed_by
        self.width = K * (256 if kind == "tok" else P * C)
        self.tiles = 4 if kind == "tok" else C


PROJ = [
    Proj("ada0", 24, 8, 2, 2), Proj("ada1", 24, 8, 2, 2),
    Proj("hyb_g", 2, 8, 2, T1, freed_by="act"), Proj("hyb_u", 2, 8, 2, T1, freed_by="act"),
    Proj("hyb_v", 2, 8, 2, T1, kind="tok"), Proj("hyb_k", 2, 8, 2, T1), Proj("hyb_q", 2, 8, 2, T1),
    Proj("hyb_out", 4, 8, 2, T1),
    Proj("ffn0_in0", FFH, 8, 2, T1), Proj("ffn0_out0", 8, FFH, 1, T1),
    Proj("ffn0_in1", FFH, 8, 2, T1), Proj("ffn0_out1", 8, FFH, 1, T1),
    Proj("ret_k", 4, 8, 2, T1), Proj("ret_v", 8, 8, 2, T1, kind="tok"), Proj("ret_q", 4, 8, 2, SEQ),
    Proj("ret_g", 8, 8, 2, SEQ, freed_by="act"), Proj("ret_out", 8, 16, 1, SEQ),
    Proj("ffn1_in0", FFH, 8, 2, SEQ), Proj("ffn1_out0", 8, FFH, 1, SEQ),
    Proj("ffn1_in1", FFH, 8, 2, SEQ), Proj("ffn1_out1", 8, FFH, 1, SEQ),
    Proj("ab_if", 1, 8, 2, T2), Proj("ab_qk", 8, 8, 2, T2), Proj("ab_v", 4, 8, 2, T2),
    Proj("ab_o", 4, 8, 2, T2, freed_by="act"), Proj("ab_xb", 4, 8, 2, T2),
    Proj("ab_gate", 4, 8, 2, T2, freed_by="act"), Proj("ab_out", 8, 16, 1, T2),
    Proj("mlp0_in0", 8, 8, 2, T2, freed_by="act"), Proj("mlp0_out0", 8, MLH, 1, T2),
    Proj("mlp0_in1", 8, 8, 2, T2, freed_by="act"), Proj("mlp0_out1", 8, MLH, 1, T2),
    Proj("c_q", 4, 8, 2, T2), Proj("c_k", 4, 8, 2, T2), Proj("c_v", 4, 8, 2, T2), Proj("c_out", 4, 8, 2, T2),
    Proj("mlp1_in0", 8, 8, 2, T2, freed_by="act"), Proj("mlp1_out0", 8, MLH, 1, T2),
    Proj("mlp1_in1", 8, 8, 2, T2, freed_by="act"), Proj("mlp1_out1", 8, MLH, 1, T2),
]


STOP = None


def _number(projections):
    slot, tile, freed, before = 0, 0, {"act": 0, "dve": 0}, None
    for p in projections:
        p.slot0, p.tile0, p.freed0 = slot, tile, freed[p.freed_by]
        p.handover = (before, freed[before]) if before not in (None, p.freed_by) else None
        slot, tile = slot + p.n, tile + p.n * p.tiles
        freed[p.freed_by] += p.n
        before = p.freed_by
        p.last = False
        p.next_width = None
        p.peel = p.freed0 < 2 or p.name in ("ffn0_in0", "mlp0_in0")
    for p, q in zip(projections, projections[1:]):
        p.next_width = q.width
    return {p.name: p for p in projections}, slot


class Step:

    def __init__(self, p, i, b):
        self.p, self.i, self.b = p, i, b
        self.s = b if i is None else 2 * i + b

    def parity(self, ahead=0):
        return (self.p.slot0 + self.b + ahead) % 2

    def turn(self, ahead=0):
        n = (self.p.slot0 + self.b + ahead) // 2
        return n if self.i is None else self.i + n

    def tile(self, c):
        return self.p.tile0 + self.s * self.p.tiles + c + 1


def each_slot(eng, p, body, peel=False):
    first = min(2, p.n) if p.peel or peel else 0
    pairs = (p.n - 1 - first) // 2
    if pairs < 2:
        pairs = 0
    for s in range(first):
        body(Step(p, None, s))
    if pairs:
        with eng.Fori(0, pairs) as i:
            for b in range(2):
                body(Step(p, i, first + b))
    for s in range(first + 2 * pairs, p.n):
        body(Step(p, None, s))


def stack_kernel(nc, t, out, layers):
    proj, n_slots = _number(layers)
    ctx = ExitStack()
    with ctx:
        base = 16512

        def at(name, shape, offset, dt=F32):
            assert offset + 4 * int(np.prod(shape[1:])) <= 229344 - base, name
            return nc.alloc_sbuf_tensor_at(name, shape, dt, offset=base + offset)

        KB = 1024
        w_raw = at("w_raw", [P, 2, SLOT], 0)
        w_hi = at("w_hi", [P, 2, SLOT], 16 * KB, F32R)
        w_lo = at("w_lo", [P, 2, SLOT], 32 * KB, F32R)
        X = at("X", [P, DC, T1], 48 * KB)
        HB = 4352 * 4
        h0 = 64 * KB
        c0 = h0 + 2 * HB
        at_const = [c0]

        def const(name, shape):
            t = at(name, shape, at_const[0])
            at_const[0] += (4 * int(np.prod(shape[1:])) + 31) // 32 * 32
            return t

        vec = const("vec", [P, NVEC])
        ident = const("ident", [P, P])
        ones = const("ones", [P, P])
        flip = const("flip", [P, P])
        swap_ret = const("swap_ret", [P, P])
        swap_c = const("swap_c", [P, P])
        head_sel = const("head_sel", [P, 4, P])
        one_row = const("one_row", [P, T2])
        rope_ret = const("rope_ret", [P, 2, SEQ])
        rope_c = const("rope_c", [P, 2, T2])
        dist = const("dist", [P, SEQ])
        cvec = const("cvec", [P, DC, 2])
        mod = const("mod", [P, 2, 48, 2])
        gains = const("gains", [P, 2, 4, 2, DC])
        tiny = const("tiny", [P, 96])
        A = at_const[0]

        H_hi = {T1: at("Hhi512", [P, DC, T1], h0, F32R), SEQ: at("Hhi256", [P, 16, SEQ], h0, F32R),
                T2: at("Hhi272", [P, 16, T2], h0, F32R), 2: at("Hhi2", [P, DC, 2], h0, F32R)}
        H_lo = {T1: at("Hlo512", [P, DC, T1], h0 + HB, F32R), SEQ: at("Hlo256", [P, 16, SEQ], h0 + HB, F32R),
                T2: at("Hlo272", [P, 16, T2], h0 + HB, F32R), 2: at("Hlo2", [P, DC, 2], h0 + HB, F32R)}

        Y = at("Y", [P, DC, T1], A)
        nt0 = A + 62 * KB
        sq = at("sq", [P, 2, T1], nt0)
        sq_acc = at("sq_acc", [P, T1], nt0 + 4 * KB)
        root = at("root", [P, T1], nt0 + 6 * KB)
        rstd = at("rstd", [P, T1], nt0 + 8 * KB)
        nt = at("nt", [P, 2, T1], nt0 + 10 * KB)
        n32 = at("n32", [P, 2, T1], nt0 + 14 * KB)
        F_hi = {T1: at("Fhi512", [P, FFH, T1], A + 16 * KB, F32R), SEQ: at("Fhi256", [P, FFH, SEQ], A + 16 * KB, F32R),
                T2: at("Fhi272", [P, MLH, T2], A + 16 * KB, F32R)}
        F_lo = {T1: at("Flo512", [P, FFH, T1], A + 38 * KB, F32R), SEQ: at("Flo256", [P, FFH, SEQ], A + 38 * KB, F32R),
                T2: at("Flo272", [P, MLH, T2], A + 38 * KB, F32R)}
        cgu = at("cgu", [P, 2, 2, T1], A + 60 * KB)
        sg = at("sg", [P, 2, T1], A + 68 * KB)
        hid = at("hid", [P, 2, T1], A + 72 * KB)
        hid2 = at("hid2", [P, 2, 2, T2], A + 72 * KB)
        g_sb = at("g_sb", [P, 4, T1], A)
        u_sb = at("u_sb", [P, 4, T1], A + 8 * KB)
        v_sb = at("v_sb", [P, 4, 512], A + 16 * KB)
        k_sb = at("k_sb", [P, 4, T1], A + 24 * KB)
        q_sb = at("q_sb", [P, 4, T1], A + 32 * KB)
        rpb = at("rpb", [P, 8, 6, GRID_W], A + 40 * KB)
        rpb_up = at("rpb_up", [P, 8, 6, GRID_W], A + 78 * KB)
        sgu_w = at("sgu_w", [P, 8, P], A + 52 * KB)
        sgu_b = at("sgu_b", [P, 4, P], A + 56 * KB)
        gT = at("gT", [P, 4, 512], A + 62 * KB)
        sgu_t = at("sgu_t", [P, 2, T1], A + 70 * KB)
        sgu_r = at("sgu_r", [P, 2, T1], A + 74 * KB)
        s_sb = at("s_sb", [P, 3, T1], A + 62 * KB)
        pT = at("pT", [P, 2, 4, SEQ], A + 68 * KB)
        rk = at("rk", [P, 8, T1], A)
        ro = at("ro", [P, 8, 2, SEQ], A)
        rv = at("rv", [P, 4, 2048], A + 16 * KB)
        rq = at("rq", [P, 8, SEQ], A + 48 * KB)
        rg = at("rg", [P, 16, SEQ], A + 56 * KB)
        r_dist = at("r_dist", [P, 2, 2, SEQ], A + 72 * KB)
        r_dec = [at(f"r_dec{i}", [P, 4, SEQ], A + (76 + 4 * i) * KB) for i in range(2)]
        r_rope = at("r_rope", [P, 2, 2, SEQ], A + 80 * KB)
        r_e = at("r_e", [P, 2, SEQ], A + 84 * KB)
        r_rs = at("r_rs", [P, 2, SEQ], A + 86 * KB)
        r_mix = at("r_mix", [P, 2, SEQ], A + 88 * KB)
        r_sq = at("r_sq", [P, 2, SEQ], A + 90 * KB)
        qk = at("qk", [P, 16, T2], A)
        vF = at("vF", [P, 8, T2], A + 17 * KB)
        og = at("og", [P, 8, T2], A + 26 * KB)
        xb = at("xb", [P, 8, T2], A + 35 * KB)
        gate = at("gate", [P, 8, T2], A + 44 * KB)
        vT = at("vT", [P, 3, D], A + 53 * KB)
        l_t = at("l_t", [P, 8, T2], A + 53 * KB)
        IF = at("IF", [P, 12, T2], A + 65 * KB)
        c_mask = at("c_mask", [P, 3, T2], A + 80 * KB)
        lru_w = at("lru_w", [P, 2, 8, P], A + 84 * KB)
        m0, m1 = h0 + 8 * 4 * T2, h0 + HB + 8 * 4 * T2
        m_Dk = at("m_Dk", [P, 3, T2], m0)
        m_P = at("m_P", [P, 3, T2], m0 + 12 * T2)
        m_E = at("m_E", [P, T2], m0 + 24 * T2)
        m_ad = at("m_ad", [P, T2], m0 + 28 * T2)
        m_h = at("m_h", [P, 2, T2], m1)
        m_sqr = at("m_sqr", [P, 2, T2], m1 + 8 * T2)
        m_rt = at("m_rt", [P, 2, T2], m1 + 16 * T2)
        cq = at("cq", [P, 8, T2], A)
        ck = at("ck", [P, 8, T2], A + 9 * KB)
        cvF = at("cvF", [P, 8, T2], A + 18 * KB)
        cvT = at("cvT", [P, 3, D], A + 27 * KB)
        c_sb = at("c_sb", [P, 3, 2, T2], A + 39 * KB)
        cP = at("cP", [P, 2, 3, T2], A + 46 * KB)
        c_rope = at("c_rope", [P, 2, 2, T2], A + 53 * KB)
        co = at("co", [P, 2, T2], A + 58 * KB)
        csq = at("csq", [P, 2, T2], A + 61 * KB)
        crt = at("crt", [P, 2, T2], A + 64 * KB)

        wk = ctx.enter_context(nc.psum_tensor("wk", [P, 4, 512], F32))
        acc = ctx.enter_context(nc.psum_tensor("acc", [P, 4, 512], F32))

        sems = {}

        def sem(name):
            sems[name] = ctx.enter_context(nc.semaphore(name))
            return sems[name]

        w_loaded = [sem("w_loaded0"), sem("w_loaded1")]
        hi_done, lo_done = sem("w_hi_done"), sem("w_lo_done")
        acc_ready = sem("acc_ready")
        freed = {"act": sem("acc_freed_act"), "dve": sem("acc_freed_dve")}
        own = {"act": sem("act_chain"), "dve": sem("dve_chain"), "pool": sem("pool_chain")}

        def chain(eng, name):
            count = [0]

            def link(ins):
                count[0] += 1
                ins.then_inc(own[name], 1)
                eng.wait_ge(own[name], count[0])
            return link

        def acc_tile(p, r, c):
            if p.kind == "tok":
                return acc[:, 2 * r + c // 2, (c % 2) * 256:(c % 2) * 256 + 256]
            return acc[:, 2 * r + c, 0:p.T]

        def stream_weights(sp):
            for p in layers:
                src = t["w_" + p.name]

                def load(slot, r, value):
                    if value is not None:
                        sp.wait_ge(lo_done, value)
                    sp.dma_start(w_raw[:, r, 0:p.width], slot).then_inc(w_loaded[r], 16)

                pairs = p.n // 2 if p.slot0 >= 2 and p.n >= 4 else 0
                if pairs:
                    with sp.Fori(0, pairs) as i:
                        for b in range(2):
                            s = 2 * i + b
                            load(src[bass.ds(s, 1), :, :].rearrange("a p n -> p (a n)"), (p.slot0 + b) % 2,
                                 s + (p.slot0 - 1))
                for s in range(2 * pairs, p.n):
                    g = p.slot0 + s
                    load(src[s], g % 2, g - 1 if g >= 2 else None)

        def split_hi(act, st):
            p, r = st.p, st.parity(1)
            width = p.width if st.i is not None or st.b + 1 < p.n else p.next_width
            if width is None:
                return
            act.wait_ge(w_loaded[r], 16 * (st.turn(1) + 1))
            if st.i is not None or p.tile0 + st.s * p.tiles > 0:
                act.wait_ge(acc_ready, st.tile(-1))
            act.activation(w_hi[:, r, 0:width], w_raw[:, r, 0:width], ACT.Copy).then_inc(hi_done, 1)

        def split_lo(dve, st):
            p, r = st.p, st.parity(1)
            width = p.width if st.i is not None or st.b + 1 < p.n else p.next_width
            if width is None:
                return
            dve.wait_ge(hi_done, p.slot0 + st.s + 2)
            dve.tensor_tensor(w_lo[:, r, 0:width], w_raw[:, r, 0:width], w_hi[:, r, 0:width].bitcast(F32),
                              ALU.subtract).then_inc(lo_done, 1)

        def project(pe, name, x_hi, x_lo, need=None):
            p = proj[name]
            if p.handover:
                pe.wait_ge(freed[p.handover[0]], p.handover[1])

            def slot(st):
                r = st.parity()
                pe.wait_ge(lo_done, p.slot0 + st.s + 1)
                if st.i is not None or p.freed0 + st.s - 1 > 0:
                    pe.wait_ge(freed[p.freed_by], p.freed0 + st.s - 1)
                for c in range(p.tiles):
                    o = acc_tile(p, r, c)
                    for k in range(p.K):
                        if need and st.i is None and st.b == 0 and c == 0:
                            need(k)
                        if p.kind == "tok":
                            w = slice(k * 256, k * 256 + 256)
                            toks = slice(P * c, P * c + P)
                            pe.matmul(o, x_hi(k)[:, toks], w_hi[:, r, w], start=k == 0, stop=False)
                            pe.matmul(o, x_hi(k)[:, toks], w_lo[:, r, w], start=False, stop=False)
                            mm = pe.matmul(o, x_lo(k)[:, toks], w_hi[:, r, w], start=False, stop=k == p.K - 1)
                        else:
                            w = slice((k * p.C + c) * P, (k * p.C + c + 1) * P)
                            pe.matmul(o, w_hi[:, r, w], x_hi(k), start=k == 0, stop=False)
                            pe.matmul(o, w_hi[:, r, w], x_lo(k), start=False, stop=False)
                            mm = pe.matmul(o, w_lo[:, r, w], x_hi(k), start=False, stop=k == p.K - 1)
                    mm.then_inc(acc_ready, 1)

            each_slot(pe, p, slot, peel=need is not None)

        s_const, s_x, s_ada_in = sem("constants_loaded"), sem("x_loaded"), sem("c_split")
        CONSTS = [("vec", vec), ("ident", ident), ("ones", ones), ("flip", flip), ("swap_ret", swap_ret), ("swap_c", swap_c),
                  ("head_sel", head_sel), ("one_row", one_row), ("rope_ret", rope_ret), ("rope_c", rope_c),
                  ("dist", dist), ("sgu_w", sgu_w), ("sgu_b", sgu_b)]
        N_CONST = 16 * (len(CONSTS) + 16)

        def load_constants(act):
            for name, dst in CONSTS:
                act.dma_start(dst[:], t[name]).then_inc(s_const, 16)
            act.dma_start(X[:, :, :], t["x"]).then_inc(s_x, 16)
            rows = t["na_rpb"].tensor
            for s in range(2):
                for h in range(8):
                    src = bass.AP(rows, h * 465 + (5 - s) * 31 + 15 - 63, [[1, GRID_W], [31, 6], [1, GRID_W]])
                    act.dma_start(rpb_up[64 * s:64 * s + 64, h, :, :], src).then_inc(s_const, 16)

        NSUM = 0
        LAM = 40

        def V(name, i=0, n=1):
            return vec[:, VEC[name] + i:VEC[name] + i + n]

        def Vd(name, i):
            return vec[:, bass.ds(i + VEC[name], 1)]

        s_cvec, s_chi, s_clo, s_gain = sem("cvec_ready"), sem("c_hi"), sem("c_lo"), sem("gains_ready")

        def act_c(act):
            act.wait_ge(s_const, N_CONST)
            act.activation(cvec[:, :, :], V("c", 0, 16).rearrange("p (k s) -> p k s", s=2), ACT.Silu).then_inc(s_cvec, 1)
            act.wait_ge(s_cvec, 1)
            act.activation(H_hi[2][:, :, :], cvec[:, :, :], ACT.Copy).then_inc(s_chi, 1)

        def dve_c(dve):
            dve.wait_ge(s_const, N_CONST)
            dve.wait_ge(s_chi, 1)
            dve.tensor_tensor(H_lo[2][:, :, :], cvec[:, :, :], H_hi[2][:, :, :].bitcast(F32),
                              ALU.subtract).then_inc(s_clo, 1)

        def pe_ada(pe, layer):
            pe.wait_ge(s_clo, 1)
            project(pe, f"ada{layer}", lambda k: H_hi[2][:, k, :], lambda k: H_lo[2][:, k, :])

        def act_plain(act, name):
            each_slot(act, proj[name], lambda st: split_hi(act, st))

        def dve_plain(dve, name):
            each_slot(dve, proj[name], lambda st: split_lo(dve, st))

        def dve_ada(dve, layer, link):
            p = proj[f"ada{layer}"]

            def slot(st):
                split_lo(dve, st)
                for c in range(2):
                    dve.wait_ge(acc_ready, st.tile(c))
                    m = st.s * 2 + c
                    dst = mod[:, layer, m, :] if st.i is None else mod[:, layer, bass.ds(m, 1), :]
                    bias = V("ada_b", layer * 48 + m) if st.i is None else Vd("ada_b", m + layer * 48)
                    ins = dve.tensor_scalar(dst, acc_tile(p, st.parity(), c), bias, None, ALU.add)
                    if c == 1:
                        ins.then_inc(freed["dve"], 1)
            each_slot(dve, p, slot)
            dve.wait_ge(freed["dve"], p.freed0 + p.n)
            for s in range(2):
                for j, (part, norm, one) in enumerate([(1, 0, 1.0), (2, 1, 0.0), (4, 2, 1.0), (5, 3, 0.0)]):
                    ins = dve.scalar_tensor_tensor(gains[:, layer, j, s, :], mod[:, layer, 8 * part:8 * part + 8, s], one,
                                                   V("norm_g", layer * 32 + norm * 8, 8), ALU.add, ALU.mult)
            ins.then_inc(s_gain, 1)

        BOTH = [(1, 0, CTX), (0, CTX, T1)]
        ONLY = [(0, 0, SEQ)]

        def ada_gain(layer, j):
            return lambda s, c: gains[:, layer, j, s, c:c + 1]

        def ada_shift(layer, part):
            return lambda s, c: mod[:, layer, 8 * part + c, s:s + 1]

        NORMS = [(T1, 0, BOTH, ada_gain(0, 0), ada_shift(0, 0)), (T1, 0, BOTH, ada_gain(0, 2), ada_shift(0, 3)),
                 (T1, 0, BOTH, ada_gain(1, 0), ada_shift(1, 0)), (SEQ, LAT, ONLY, ada_gain(1, 2), ada_shift(1, 3))]
        for name, i in [("norm_mix", 0), ("norm_mlp", 0), ("norm_mix", 8), ("norm_mlp", 8), ("norm_final", 0)]:
            NORMS.append((T2, X2, [(0, 0, T2)], lambda s, c, name=name, i=i: V(name, i + c), None))
        FINAL = len(NORMS) - 1
        nsq_ready, nsq_used, root_ready = sem("norm_square_ready"), sem("norm_square_summed"), sem("norm_root_ready")
        rstd_ready, nt_ready = sem("norm_rstd_ready"), sem("norm_scaled_ready")
        n32_ready, hhi_ready, h_ready = sem("norm_out_ready"), sem("h_hi_ready"), sem("h_ready")
        s_out = [sem("out_stored0"), sem("out_stored1")]
        x_ready = sem("x_ready")
        s_meta = sem("meta_loaded")

        def x_ready_for(eng, j, c):
            if j == 0:
                eng.wait_ge(s_x, 16)
            elif j <= 4:
                eng.wait_ge(x_ready, 8 * (j - 1) + c + 1)
            else:
                p = proj[("ab_out", "mlp0_out1", "c_out", "mlp1_out1")[j - 5]]
                eng.wait_ge(freed["dve"], p.freed0 + c // p.C + 1)
            if j == 4:
                eng.wait_ge(s_meta, 4 * 16)

        def pe_norm(pe, j):
            n = NORMS[j][0]
            if j == 0:
                pe.wait_ge(s_const, N_CONST)
            for c in range(DC):
                pe.wait_ge(nsq_ready, DC * j + c + 1)
                pe.matmul(wk[:, 0, 0:n], ones[:, :], sq[:, c % 2, 0:n], start=c == 0, stop=c == DC - 1)\
                    .then_inc(nsq_used, 1)

        def act_norm(act, j):
            n, x0, groups, gain, shift = NORMS[j]
            for c in range(DC):
                x_ready_for(act, j, c)
                if c >= 2:
                    act.wait_ge(nsq_used, DC * j + c - 1)
                act.activation(sq[:, c % 2, 0:n], X[:, c, x0:x0 + n], ACT.Square).then_inc(nsq_ready, 1)
            act.wait_ge(nsq_used, DC * (j + 1))
            act.activation(root[:, 0:n], wk[:, 0, 0:n], ACT.Sqrt, bias=V("eps"), scale=1.0 / D).then_inc(root_ready, 1)
            if j == 0:
                act.wait_ge(s_gain, 1)
            if j == 2:
                act.wait_ge(s_gain, 2)
            for c in range(DC):
                act.wait_ge(nt_ready, DC * j + c + 1)
                if c >= 2 and j != FINAL:
                    act.wait_ge(h_ready, DC * j + c - 1)
                if c >= 2 and j == FINAL:
                    act.wait_ge(s_out[c % 2], 16 * (c // 2))
                for i, (s, a, b) in enumerate(groups):
                    kw = {} if shift is None else {"bias": shift(s, c)}
                    ins = act.activation(n32[:, c % 2, a:b], nt[:, c % 2, a:b], ACT.Identity, scale=gain(s, c), **kw)
                ins.then_inc(n32_ready, 1)
                if j == FINAL:
                    continue
                act.wait_ge(n32_ready, DC * j + c + 1)
                act.activation(H_hi[n][:, c, 0:n], n32[:, c % 2, 0:n], ACT.Copy).then_inc(hhi_ready, 1)

        def dve_norm(dve, j):
            n, x0, groups, gain, shift = NORMS[j]
            dve.wait_ge(root_ready, j + 1)
            dve.reciprocal(rstd[:, 0:n], root[:, 0:n]).then_inc(rstd_ready, 1)
            dve.wait_ge(rstd_ready, j + 1)

            def lo(c):
                dve.wait_ge(hhi_ready, DC * j + c + 1)
                dve.tensor_tensor(H_lo[n][:, c, 0:n], n32[:, c % 2, 0:n], H_hi[n][:, c, 0:n].bitcast(F32),
                                  ALU.subtract).then_inc(h_ready, 1)
            for c in range(DC):
                if c >= 2:
                    dve.wait_ge(n32_ready, DC * j + c - 1)
                dve.tensor_tensor(nt[:, c % 2, 0:n], X[:, c, x0:x0 + n], rstd[:, 0:n], ALU.mult).then_inc(nt_ready, 1)
                if c >= 1 and j != FINAL:
                    lo(c - 1)
            if j != FINAL:
                lo(DC - 1)

        def h_need(pe, j):
            return lambda k: pe.wait_ge(h_ready, DC * j + k + 1)

        RES = [(T1, 0, BOTH, (0, 1), "hyb_out"), (T1, 0, BOTH, (0, 3), "ffn0_out1"),
               (SEQ, LAT, ONLY, (1, 1), "ret_out"), (SEQ, LAT, ONLY, (1, 3), "ffn1_out1")]
        ysq_ready, ysq_used, ysum_ready = sem("y_square_ready"), sem("y_square_added"), sem("y_sum_ready")
        yroot_ready, yrstd_ready, yt_ready = sem("y_root_ready"), sem("y_rstd_ready"), sem("y_scaled_ready")

        def dve_y(dve, name, add=None):
            p = proj[name]
            n = p.T

            def slot(st):
                split_lo(dve, st)
                for c in range(p.C):
                    m = st.s * p.C + c
                    dst = Y[:, m, 0:n] if st.i is None else Y[:, bass.ds(m, 1), 0:n]
                    dve.wait_ge(acc_ready, st.tile(c))
                    if add:
                        dve.wait_ge(freed["dve"], proj[add].freed0 + st.s + 1)
                        ins = dve.tensor_tensor(dst, acc_tile(p, st.parity(), c), dst, ALU.add)
                    else:
                        ins = dve.tensor_copy(dst, acc_tile(p, st.parity(), c))
                    if c == p.C - 1:
                        ins.then_inc(freed["dve"], 1)
            each_slot(dve, p, slot)

        def act_y_squares(act, name, r):
            p = proj[name]
            n = p.T
            for s in range(p.n):
                st = Step(p, None, s)
                split_hi(act, st)
                act.wait_ge(freed["dve"], p.freed0 + s + 1)
                for c in range(p.C):
                    m = s * p.C + c
                    if m >= 2:
                        act.wait_ge(ysq_used, DC * r + m - 1)
                    act.activation(sq[:, m % 2, 0:n], Y[:, m, 0:n], ACT.Square).then_inc(ysq_ready, 1)

        def pool_y_sum(pool, r):
            n = RES[r][0]
            for m in range(DC):
                pool.wait_ge(ysq_ready, DC * r + m + 1)
                if m == 0:
                    pool.tensor_copy(sq_acc[:, 0:n], sq[:, 0, 0:n]).then_inc(ysq_used, 1)
                else:
                    pool.wait_ge(ysq_used, DC * r + m)
                    pool.tensor_tensor(sq_acc[:, 0:n], sq_acc[:, 0:n], sq[:, m % 2, 0:n], ALU.add).then_inc(ysq_used, 1)

        def pe_residual(pe, r):
            n = RES[r][0]
            pe.wait_ge(ysq_used, DC * (r + 1))
            pe.matmul(wk[:, 1, 0:n], ones[:, :], sq_acc[:, 0:n], start=True, stop=True).then_inc(ysum_ready, 1)

        def act_residual(act, r):
            n = RES[r][0]
            act.wait_ge(ysum_ready, r + 1)
            act.activation(root[:, 0:n], wk[:, 1, 0:n], ACT.Sqrt, bias=V("eps"), scale=1.0 / D).then_inc(yroot_ready, 1)

        def dve_residual(dve, r):
            n, x0, groups, (layer, j), _ = RES[r]
            dve.wait_ge(yroot_ready, r + 1)
            dve.reciprocal(rstd[:, 0:n], root[:, 0:n]).then_inc(yrstd_ready, 1)
            dve.wait_ge(yrstd_ready, r + 1)

            def update(c):
                dve.wait_ge(yt_ready, DC * r + c + 1)
                for s, a, b in groups:
                    ins = dve.scalar_tensor_tensor(X[:, c, x0 + a:x0 + b], nt[:, c % 2, a:b], gains[:, layer, j, s, c:c + 1],
                                                   X[:, c, x0 + a:x0 + b], ALU.mult, ALU.add)
                ins.then_inc(x_ready, 1)
            for c in range(DC):
                if c >= 2:
                    dve.wait_ge(x_ready, DC * r + c - 1)
                dve.tensor_tensor(nt[:, c % 2, 0:n], Y[:, c, 0:n], rstd[:, 0:n], ALU.mult).then_inc(yt_ready, 1)
                if c >= 1:
                    update(c - 1)
            update(DC - 1)

        conv_mid, conv_left, conv_gate = sem("conv_centre_done"), sem("conv_left_done"), sem("conv_gate_done")
        silu_done, hid_mul, hid_hi, hid_done = sem("silu_done"), sem("hidden_product"), sem("hidden_hi"), sem("hidden_done")

        def ffn_name(layer, half, what):
            return f"ffn{layer}_{what}{half}"

        def act_ffn_in(act, layer, half):
            p = proj[ffn_name(layer, half, "in")]
            n, f0 = p.T, (2 * layer + half) * FFH

            def slot(st):
                split_hi(act, st)
                f, r = st.s + f0, st.parity()
                for c in range(2):
                    act.wait_ge(acc_ready, st.tile(c))
                    if c == 0 and (st.i is not None or f >= 2):
                        act.wait_ge(hid_mul, 2 * f - 2)
                    m = st.s + (22 * c + FFH * half)
                    act.activation(cgu[:, r, c, 0:n], acc_tile(p, r, c), ACT.Identity,
                                   bias=Vd("conv_b", m + layer * 44), scale=Vd("conv_w", m + (layer * 3 + 1) * 44))\
                        .then_inc(conv_mid, 1)
                act.wait_ge(conv_gate, f + 1)
                act.activation(sg[:, r, 0:n], cgu[:, r, 0, 0:n], ACT.Silu).then_inc(silu_done, 1)
            each_slot(act, p, slot)

        def dve_ffn_in(dve, layer, half):
            p = proj[ffn_name(layer, half, "in")]
            n, f0 = p.T, (2 * layer + half) * FFH

            def seqs(ap, a, b):
                return ap.rearrange("p (q t) -> p q t", t=SEQ)[:, :, a:b]

            def slot(st):
                split_lo(dve, st)
                f, r = st.s + f0, st.parity()
                for c in range(2):
                    dve.wait_ge(conv_mid, 2 * f + c + 1)
                    o = cgu[:, r, c, 0:n]
                    w = Vd("conv_w", st.s + (22 * c + FFH * half + layer * 3 * 44))
                    dve.scalar_tensor_tensor(seqs(o, 1, SEQ), seqs(acc_tile(p, r, c), 0, SEQ - 1), w, seqs(o, 1, SEQ),
                                             ALU.mult, ALU.add).then_inc(conv_left, 1)
                for c in range(2):
                    dve.wait_ge(conv_left, 2 * f + c + 1)
                    o = cgu[:, r, c, 0:n]
                    w = Vd("conv_w", st.s + (22 * c + FFH * half + (layer * 3 + 2) * 44))
                    dve.scalar_tensor_tensor(seqs(o, 0, SEQ - 1), seqs(acc_tile(p, r, c), 1, SEQ), w, seqs(o, 0, SEQ - 1),
                                             ALU.mult, ALU.add).then_inc(conv_gate if c == 0 else freed["dve"], 1)
            each_slot(dve, p, slot)

        def pool_hidden(pool, p, f0, left, right, ready):
            n = p.T

            def slot(st):
                f, r = st.s + f0, st.parity()
                hi = F_hi[n][:, bass.ds(st.s, 1), :] if st.i is not None else F_hi[n][:, st.s, :]
                lo = F_lo[n][:, bass.ds(st.s, 1), :] if st.i is not None else F_lo[n][:, st.s, :]
                ready(st)
                pool.tensor_tensor(hid[:, r, 0:n], left(r), right(r), ALU.mult).then_inc(hid_mul, 1)
                pool.tensor_tensor(hi, left(r), right(r), ALU.mult).then_inc(hid_mul, 1)
                pool.wait_ge(hid_mul, 2 * f + 2)
                pool.tensor_tensor(lo, hid[:, r, 0:n], hi.bitcast(F32), ALU.subtract).then_inc(hid_done, 1)
            each_slot(pool, p, slot)

        def pool_ffn_in(pool, layer, half):
            p = proj[ffn_name(layer, half, "in")]
            f0 = (2 * layer + half) * FFH

            def ready(st):
                pool.wait_ge(freed["dve"], p.freed0 + st.s + 1)
                pool.wait_ge(silu_done, st.s + (f0 + 1))
            pool_hidden(pool, p, f0, lambda r: sg[:, r, 0:p.T], lambda r: cgu[:, r, 1, 0:p.T], ready)

        def pe_ffn(pe, layer, half, j):
            n = proj[ffn_name(layer, half, "in")].T
            f0 = (2 * layer + half) * FFH
            project(pe, ffn_name(layer, half, "in"), lambda k: H_hi[n][:, k, :], lambda k: H_lo[n][:, k, :],
                    need=h_need(pe, j) if half == 0 else None)
            project(pe, ffn_name(layer, half, "out"), lambda k: F_hi[n][:, k, :], lambda k: F_lo[n][:, k, :],
                    need=lambda k: pe.wait_ge(hid_done, f0 + k + 1))

        def act_gelu(act, name, dst, func=ACT.Gelu_apprx_tanh):
            p = proj[name]

            def slot(st):
                split_hi(act, st)
                for c in range(2):
                    m = st.s * 2 + c
                    act.wait_ge(acc_ready, st.tile(c))
                    o = dst[:, m, 0:p.T] if st.i is None else dst[:, bass.ds(m, 1), 0:p.T]
                    ins = act.activation(o, acc_tile(p, st.parity(), c), func)
                    if c == 1:
                        ins.then_inc(freed["act"], 1)
            each_slot(act, p, slot)

        def dve_copy(dve, name, dst, m0=0):
            p = proj[name]

            def slot(st):
                split_lo(dve, st)
                for c in range(2):
                    m = st.s * 2 + (c + m0)
                    dve.wait_ge(acc_ready, st.tile(c))
                    o = dst[:, m, 0:p.T] if st.i is None else dst[:, bass.ds(m, 1), 0:p.T]
                    ins = dve.tensor_copy(o, acc_tile(p, st.parity(), c))
                    if c == 1:
                        ins.then_inc(freed["dve"], 1)
            each_slot(dve, p, slot)

        def dve_copy_tokens(dve, name, dst):
            p = proj[name]

            def slot(st):
                split_lo(dve, st)
                for j in range(2):
                    dve.wait_ge(acc_ready, st.tile(2 * j + 1))
                    o = dst[:, 2 * j:2 * j + 2, st.s * 256:st.s * 256 + 256] if st.i is None \
                        else dst[:, 2 * j:2 * j + 2, bass.ds(st.s * 256, 256)]
                    ins = dve.tensor_copy(o, acc[:, 2 * st.parity() + j, :].rearrange("p (c n) -> p c n", c=2))
                ins.then_inc(freed["dve"], 1)
            each_slot(dve, p, slot)

        def all_freed(eng, name):
            p = proj[name]
            eng.wait_ge(freed[p.freed_by], p.freed0 + p.n)

        sgu_sum, sgu_cent, sgu_sq, sgu_sqsum = sem("sgu_sum"), sem("sgu_centred"), sem("sgu_square"), sem("sgu_square_sum")
        sgu_root, sgu_norm, sgu_tr, sgu_copied = sem("sgu_root"), sem("sgu_normed"), sem("sgu_transposed"), sem("sgu_copied")
        sgu_mixed, sgu_gated, sgu_hi, sgu_lo = sem("sgu_mixed"), sem("sgu_gated"), sem("sgu_hi"), sem("sgu_lo")

        def pe_sgu(pe):
            all_freed(pe, "hyb_g")
            for c in range(4):
                mm = pe.matmul(wk[:, 0, :], ones[:, :], g_sb[:, c, :], start=c == 0, stop=c == 3)
            mm.then_inc(sgu_sum, 1)
            for c in range(4):
                pe.wait_ge(sgu_sq, c + 1)
                pe.matmul(wk[:, 1, :], ones[:, :], sgu_t[:, c % 2, :], start=c == 0, stop=c == 3).then_inc(sgu_sqsum, 1)
            for tt in range(4):
                if tt == 0:
                    pe.wait_ge(sgu_norm, 4)
                if tt >= 2:
                    pe.wait_ge(sgu_copied, tt - 1)
                for c in range(4):
                    mm = pe.transpose(wk[:, 2 + tt % 2, c * P:(c + 1) * P], g_sb[:, c, tt * P:(tt + 1) * P], ident[:, :])
                mm.then_inc(sgu_tr, 1)
            pe.wait_ge(sgu_copied, 4)
            for c in range(4):
                if c == 0:
                    pe.wait_ge(sgu_norm, 4)
                if c >= 2:
                    pe.wait_ge(sgu_gated, 2 * (c - 2) + 1)
                for half in range(2):
                    g = 2 * c + half
                    for tt in range(4):
                        mm = pe.matmul(wk[64 * half:64 * half + 64, c % 2, tt * P:(tt + 1) * P],
                                       gT[:, tt, g * 64:(g + 1) * 64], sgu_w[:, g, :], start=True, stop=True)
                mm.then_inc(sgu_mixed, 1)

        def act_sgu(act):
            for c in range(4):
                act.wait_ge(sgu_cent, c + 1)
                if c >= 2:
                    act.wait_ge(sgu_sqsum, c - 1)
                act.activation(sgu_t[:, c % 2, :], g_sb[:, c, :], ACT.Square).then_inc(sgu_sq, 1)
            act.wait_ge(sgu_sqsum, 4)
            act.activation(sgu_r[:, 0, :], wk[:, 1, :], ACT.Sqrt, bias=V("eps"), scale=1.0 / 512).then_inc(sgu_root, 1)
            for tt in range(4):
                act.wait_ge(sgu_tr, tt + 1)
                act.activation(gT[:, tt, :], wk[:, 2 + tt % 2, :], ACT.Copy).then_inc(sgu_copied, 1)
            for c in range(4):
                act.wait_ge(sgu_gated, 2 * c + 2)
                act.activation(H_hi[T1][:, 4 + c, :], u_sb[:, c, :], ACT.Copy).then_inc(sgu_hi, 1)

        def dve_sgu(dve, link):
            dve.wait_ge(sgu_sum, 1)
            for c in range(4):
                dve.scalar_tensor_tensor(g_sb[:, c, :], wk[:, 0, :], -1.0 / 512, g_sb[:, c, :], ALU.mult, ALU.add)\
                    .then_inc(sgu_cent, 1)
            dve.wait_ge(sgu_root, 1)
            link(dve.reciprocal(sgu_r[:, 1, :], sgu_r[:, 0, :]))
            for c in range(4):
                dve.wait_ge(sgu_sqsum, c + 1)
                dve.wait_ge(sgu_cent, c + 1)
                dve.tensor_tensor(g_sb[:, c, :], g_sb[:, c, :], sgu_r[:, 1, :], ALU.mult).then_inc(sgu_norm, 1)
            all_freed(dve, "hyb_u")
            for c in range(4):
                dve.wait_ge(sgu_mixed, c + 1)
                bias = sgu_b[:, c, :].rearrange("p (a q) -> p a q", a=1).to_broadcast([P, 4, P])
                dve.tensor_tensor(sgu_t[:, c % 2, :].rearrange("p (n q) -> p n q", q=P),
                                  wk[:, c % 2, :].rearrange("p (n q) -> p n q", q=P), bias, ALU.add).then_inc(sgu_gated, 1)
                dve.wait_ge(sgu_gated, 2 * c + 1)
                dve.tensor_tensor(u_sb[:, c, :], u_sb[:, c, :], sgu_t[:, c % 2, :], ALU.mult).then_inc(sgu_gated, 1)
            for c in range(4):
                dve.wait_ge(sgu_hi, c + 1)
                dve.tensor_tensor(H_lo[T1][:, 4 + c, :], u_sb[:, c, :], H_hi[T1][:, 4 + c, :].bitcast(F32),
                                  ALU.subtract).then_inc(sgu_lo, 1)

        NU = 32
        at_s, at_scaled, at_max, at_exp = sem("attn_scores"), sem("attn_scaled"), sem("attn_max"), sem("attn_exp")
        at_rec, at_p, at_tr, at_pt = sem("attn_recip"), sem("attn_probs"), sem("attn_transposed"), sem("attn_probsT")
        at_o, at_hi, at_lo, s_rpb = sem("attn_out"), sem("attn_hi"), sem("attn_lo"), sem("rpb_masked")

        def keys_of(u):
            return CTX if u % 4 < 2 else T1

        s_flip, s_flipped = sem("rpb_flip_ready"), sem("rpb_flipped")

        def pe_rpb(pe):
            flat = rpb_up[:, :, :, :].rearrange("p h j k -> p (h j k)")
            for b in range(6):
                if b >= 4:
                    pe.wait_ge(s_flipped, b - 3)
                pe.matmul(wk[:, b % 4, :], flip[:, :], flat[:, b * 512:(b + 1) * 512], start=True, stop=True)\
                    .then_inc(s_flip, 1)

        def act_rpb(act):
            flat = rpb[:, :, :, :].rearrange("p h j k -> p (h j k)")
            for b in range(6):
                act.wait_ge(s_flip, b + 1)
                act.activation(flat[:, b * 512:(b + 1) * 512], wk[:, b % 4, :], ACT.Copy).then_inc(s_flipped, 1)

        def pool_rpb(pool, link):
            pool.wait_ge(s_flipped, 6)
            for s in range(2):
                part = rpb[64 * s:64 * s + 64, :, :, :].rearrange("p h j k -> p (h j) k")
                lower, upper = part[:, :, 0:48], part[:, :, 16:64]
                link(pool.affine_select(out=lower, in_=lower, compare_op=ALU.is_ge, fill=NEG, base=8,
                                        pattern=[[0, 48], [1, 48]], channel_multiplier=-1))
                ins = pool.affine_select(out=upper, in_=upper, compare_op=ALU.is_ge, fill=NEG, base=7 - 16,
                                         pattern=[[0, 48], [-1, 48]], channel_multiplier=1)
                if s == 0:
                    link(ins)
            ins.then_inc(s_rpb, 1)

        def pe_attn(pe):
            for name in ("hyb_k", "hyb_q", "hyb_v"):
                all_freed(pe, name)

            def scores(u):
                h, tt = u // 4, u % 4
                if u >= 2:
                    pe.wait_ge(at_scaled, u - 1)
                b = 64 * (h % 2)
                pe.matmul(acc[:, u % 2, 0:keys_of(u)], q_sb[b:b + 64, h // 2, tt * P:(tt + 1) * P],
                          k_sb[b:b + 64, h // 2, 0:keys_of(u)], start=True, stop=True).then_inc(at_s, 1)

            def turn(u):
                pe.wait_ge(at_p, u + 1)
                if u >= 2:
                    pe.wait_ge(at_pt, u - 1)
                for kt in range(keys_of(u) // P):
                    mm = pe.transpose(acc[:, 2 + u % 2, kt * P:(kt + 1) * P], s_sb[:, u % 3, kt * P:(kt + 1) * P], ident[:, :])
                mm.then_inc(at_tr, 1)

            def values(pair):
                h, n = pair // 2, keys_of(2 * pair) // P
                pe.wait_ge(at_pt, 2 * pair + 2)
                if pair >= 2:
                    pe.wait_ge(at_lo, pair - 1)
                b = 64 * (h % 2)
                for kt in range(n):
                    mm = pe.matmul(wk[b:b + 64, pair % 2, 0:256], v_sb[:, kt, h * 64:h * 64 + 64], pT[:, pair % 2, kt, :],
                                   start=kt == 0, stop=kt == n - 1)
                mm.then_inc(at_o, 1)

            pe.wait_ge(sgu_gated, 8)
            scores(0)
            scores(1)
            for u in range(NU):
                turn(u)
                if u + 2 < NU:
                    scores(u + 2)
                if u % 2 == 0 and u >= 2:
                    values(u // 2 - 1)
            values(NU // 2 - 1)

        def act_attn(act):
            def probs(u):
                act.wait_ge(at_max, u + 1)
                m = 4 * (u % 3)
                s = s_sb[:, u % 3, 0:keys_of(u)]
                if u >= 3:
                    act.wait_ge(at_p, u - 2)
                act.activation(s, s, ACT.Exp, bias=tiny[:, m:m + 1], accum_out=tiny[:, m + 1:m + 2]).then_inc(at_exp, 1)

            def copy(u):
                act.wait_ge(at_tr, u + 1)
                pair, n = u // 2, keys_of(u) // P
                if pair >= 2:
                    act.wait_ge(at_o, pair - 1)
                act.activation(pT[:, pair % 2, 0:n, (u % 2) * P:(u % 2) * P + P],
                               acc[:, 2 + u % 2, 0:n * P].rearrange("p (k q) -> p k q", q=P), ACT.Copy).then_inc(at_pt, 1)

            def hi(pair):
                act.wait_ge(at_o, pair + 1)
                h, x = pair // 2, (pair % 2) * CTX
                b = 64 * (h % 2)
                act.activation(H_hi[T1][b:b + 64, h // 2, x:x + 256], wk[b:b + 64, pair % 2, 0:256], ACT.Copy)\
                    .then_inc(at_hi, 1)

            for u in range(NU):
                probs(u)
                if u >= 1:
                    copy(u - 1)
                if u % 2 == 1 and u >= 3:
                    hi((u - 3) // 2)
            copy(NU - 1)
            hi(NU // 2 - 1)

        def dve_attn(dve):
            dve.wait_ge(s_rpb, 1)

            def scale(u):
                h, tt, s = u // 4, u % 4, s_sb[:, u % 3, :]
                dve.wait_ge(at_s, u + 1)
                if u >= 3:
                    dve.wait_ge(at_tr, u - 2)
                ins = dve.tensor_scalar(s[:, 0:CTX], acc[:, u % 2, 0:CTX], 0.125, None, ALU.mult)
                if tt >= 2:
                    j = 2 - 2 * (tt - 2)
                    for b in (0, 64):
                        ins = dve.scalar_tensor_tensor(
                            s[b:b + 64, CTX:T1], acc[b:b + 64, u % 2, CTX:T1], 0.125,
                            rpb[b:b + 64, h, j:j + 4, :].rearrange("p j k -> p (j k)"), ALU.mult, ALU.add)
                ins.then_inc(at_scaled, 1)
                dve.wait_ge(at_scaled, u + 1)
                m = 4 * (u % 3)
                dve.tensor_reduce(tiny[:, m:m + 1], s[:, 0:keys_of(u)], AX.X, ALU.max, negate=True).then_inc(at_max, 1)

            def norm(u):
                m = 4 * (u % 3)
                s = s_sb[:, u % 3, 0:keys_of(u)]
                dve.wait_ge(at_exp, u + 1)
                dve.reciprocal(tiny[:, m + 2:m + 3], tiny[:, m + 1:m + 2]).then_inc(at_rec, 1)
                dve.wait_ge(at_rec, u + 1)
                dve.tensor_scalar(s, s, tiny[:, m + 2:m + 3], None, ALU.mult).then_inc(at_p, 1)

            def lo(pair):
                dve.wait_ge(at_hi, pair + 1)
                h, x = pair // 2, (pair % 2) * CTX
                b = 64 * (h % 2)
                dve.tensor_tensor(H_lo[T1][b:b + 64, h // 2, x:x + 256], wk[b:b + 64, pair % 2, 0:256],
                                  H_hi[T1][b:b + 64, h // 2, x:x + 256].bitcast(F32), ALU.subtract).then_inc(at_lo, 1)

            for u in range(NU):
                scale(u)
                if u >= 1:
                    norm(u - 1)
                if u % 2 == 0 and u >= 4:
                    lo((u - 4) // 2)
            norm(NU - 1)
            lo(NU // 2 - 2)
            lo(NU // 2 - 1)

        RH = 8
        NDEC, B1, B2 = 48, 56, 72
        rot_ready, rot_mul, rot_done = sem("rope_swapped"), sem("rope_products"), sem("rope_done")
        r_arg, r_exp, r_D = sem("decay_arg"), sem("decay_exp"), sem("decay_ready")
        r_s, r_pt, r_o, r_oc = sem("ret_scores"), sem("ret_weighted"), sem("ret_out_ready"), sem("ret_out_copied")
        r_mean, r_cent, r_sqd, r_var = sem("ret_sum"), sem("ret_centred"), sem("ret_square"), sem("ret_square_sum")
        r_root, r_nrm, r_mixed, r_hi, r_lo = sem("ret_root"), sem("ret_normed"), sem("ret_mixed"), sem("ret_hi"), sem("ret_lo")
        s_decay, s_dist = sem("decay_columns"), sem("distances_ready")

        def r_weights(h):
            b = 4 * (h % 2)
            return X[:, b:b + 4, 0:SEQ]

        def rope_items():
            return [rk[:, h, LAT:T1] for h in range(RH)] + [rq[:, h, :] for h in range(RH)]

        def pe_rope(pe, items, n, swap, base, ready):
            ready()
            for i, x in enumerate(items):
                if i >= 4:
                    pe.wait_ge(rot_mul, base + i - 3)
                pe.matmul(wk[:, i % 4, 0:n], swap[:, :], x, start=True, stop=True).then_inc(rot_ready, 1)

        def dve_rope(dve, items, n, table, tmp, base):
            def add(i):
                dve.wait_ge(rot_mul, base + i + 1)
                dve.tensor_tensor(items[i], tmp[:, i % 2, 0, 0:n], tmp[:, i % 2, 1, 0:n], ALU.add).then_inc(rot_done, 1)
            for i, x in enumerate(items):
                if i >= 2:
                    dve.wait_ge(rot_done, base + i - 1)
                dve.tensor_tensor(tmp[:, i % 2, 0, 0:n], x, table[:, 0, :], ALU.mult)
                dve.wait_ge(rot_ready, base + i + 1)
                dve.tensor_tensor(tmp[:, i % 2, 1, 0:n], wk[:, i % 4, 0:n], table[:, 1, :], ALU.mult).then_inc(rot_mul, 1)
                if i >= 1:
                    add(i - 1)
            add(len(items) - 1)

        def pe_ret(pe):
            pe_rope(pe, rope_items(), SEQ, swap_ret, 0, lambda: (all_freed(pe, "ret_k"), all_freed(pe, "ret_q")))

            def scores(h):
                if h == 0:
                    pe.wait_ge(rot_done, 2 * RH)
                    all_freed(pe, "ret_v")
                    all_freed(pe, "ret_g")
                if h >= 2:
                    pe.wait_ge(r_pt, h - 1)
                for kt in range(4):
                    mm = pe.matmul(acc[:, 2 * (h % 2) + kt // 2, (kt % 2) * 256:(kt % 2) * 256 + 256],
                                   rk[:, h, kt * P:(kt + 1) * P], rq[:, h, :], start=True, stop=True)
                mm.then_inc(r_s, 1)

            def values(h):
                pe.wait_ge(r_pt, h + 1)
                if h >= 2:
                    pe.wait_ge(r_oc, h - 1)
                for c in range(2):
                    for kt in range(4):
                        mm = pe.matmul(wk[:, h % 2, c * 256:(c + 1) * 256], rv[:, kt, h * 256 + c * P:h * 256 + (c + 1) * P],
                                       r_weights(h)[:, kt, :], start=kt == 0, stop=kt == 3)
                mm.then_inc(r_o, 1)

            def mean(h):
                pe.wait_ge(r_oc, h + 1)
                if h >= 1:
                    pe.wait_ge(r_cent, 2 * h)
                for c in range(2):
                    mm = pe.matmul(wk[:, 2, 0:256], ones[:, :], ro[:, h, c, :], start=c == 0, stop=c == 1)
                mm.then_inc(r_mean, 1)

            def variance(h):
                pe.wait_ge(r_sqd, h + 1)
                if h >= 1:
                    pe.wait_ge(r_root, h)
                for c in range(2):
                    mm = pe.matmul(wk[:, 3, 0:256], ones[:, :], r_sq[:, c, :], start=c == 0, stop=c == 1)
                mm.then_inc(r_var, 1)

            scores(0)
            for h in range(RH):
                if h + 1 < RH:
                    scores(h + 1)
                values(h)
                if h >= 1:
                    variance(h - 1)
                mean(h)
            variance(RH - 1)

        def act_ret(act):
            def decay(h):
                if h == 0:
                    act.wait_ge(s_decay, 5)
                if h >= 2:
                    act.wait_ge(r_pt, h - 1)
                if h >= 1:
                    act.wait_ge(r_D, 3 * h)
                d = r_dec[h % 2]
                for kt in range(2):
                    act.activation(d[:, kt, :], dist[:, :], ACT.Exp, scale=V("decay", h), bias=tiny[:, B1 + 8 * kt + h:B1 + 8 * kt + h + 1])
                    act.activation(r_e[:, kt, :], dist[:, :], ACT.Exp, scale=tiny[:, NDEC + h:NDEC + h + 1],
                                   bias=tiny[:, B2 + 8 * kt + h:B2 + 8 * kt + h + 1])
                act.wait_ge(r_arg, 2 * h + 2)
                act.activation(d[:, 2:4, :], d[:, 2:4, :], ACT.Exp).then_inc(r_exp, 1)

            def copy(h):
                act.wait_ge(r_o, h + 1)
                act.activation(ro[:, h, :, :], wk[:, h % 2, :].rearrange("p (c n) -> p c n", c=2), ACT.Copy).then_inc(r_oc, 1)

            def root_of(h):
                act.wait_ge(r_var, h + 1)
                if h >= 1:
                    act.wait_ge(r_nrm, 3 * h - 2)
                act.activation(r_rs[:, 0, :], wk[:, 3, 0:256], ACT.Sqrt, bias=V("eps"), scale=1.0 / 256).then_inc(r_root, 1)

            def square(h):
                act.wait_ge(r_cent, 2 * h + 2)
                if h >= 1:
                    act.wait_ge(r_var, h)
                act.activation(r_sq[:, :, :], ro[:, h, :, :], ACT.Square).then_inc(r_sqd, 1)

            def hi(h):
                act.wait_ge(r_mixed, 2 * h + 2)
                act.activation(H_hi[SEQ][:, 2 * h:2 * h + 2, :], r_mix[:, :, :], ACT.Copy).then_inc(r_hi, 1)

            decay(0)
            for h in range(RH):
                if h + 1 < RH:
                    decay(h + 1)
                copy(h)
                if h >= 1:
                    root_of(h - 1)
                square(h)
                if h >= 1:
                    hi(h - 1)
            root_of(RH - 1)
            hi(RH - 1)

        def pool_ret(pool):
            for h in range(RH):
                d = r_dec[h % 2]
                pool.wait_ge(r_exp, h + 1)
                pool.tensor_tensor(d[:, 0:2, :], d[:, 0:2, :], r_e[:, :, :], ALU.add).then_inc(r_D, 1)
                for kt in range(2):
                    x = d[:, 2 + kt, kt * P:(kt + 1) * P]
                    pool.tensor_tensor(x, x, ident[:, :], ALU.add).then_inc(r_D, 1)

        def dve_ret(dve):
            dve_rope(dve, rope_items(), SEQ, rope_ret, r_rope, 0)
            lg2 = V("decay", 8, 8)
            dve.tensor_scalar(tiny[:, NDEC:NDEC + 8], lg2, -1.0, None, ALU.mult).then_inc(s_decay, 1)
            for kt in range(2):
                b = 8 * kt
                dve.tensor_scalar(tiny[:, B1 + b:B1 + b + 8], V("decay", 0, 8), float(CTX - P * kt), None, ALU.mult)\
                    .then_inc(s_decay, 1)
                dve.tensor_scalar(tiny[:, B2 + b:B2 + b + 8], lg2, float(CTX + P * kt), None, ALU.mult).then_inc(s_decay, 1)
                dve.tensor_scalar(r_dist[:, 0, kt, :], dist[:, :], float(-P * kt), 0.0, ALU.add, ALU.max).then_inc(s_dist, 1)
                dve.tensor_scalar(r_dist[:, 1, kt, :], dist[:, :], float(-P * kt), 0.0, ALU.add, ALU.min).then_inc(s_dist, 1)
            dve.wait_ge(s_decay, 5)
            dve.wait_ge(s_dist, 4)

            def arg(h):
                d = r_dec[h % 2][:, 2:4, :]
                if h >= 2:
                    dve.wait_ge(r_pt, h - 1)
                dve.tensor_scalar(d, r_dist[:, 0, :, :], V("decay", h), None, ALU.mult).then_inc(r_arg, 1)
                dve.wait_ge(r_arg, 2 * h + 1)
                dve.scalar_tensor_tensor(d, r_dist[:, 1, :, :], tiny[:, NDEC + h:NDEC + h + 1], d, ALU.mult, ALU.add)\
                    .then_inc(r_arg, 1)

            def weights(h):
                dve.wait_ge(r_s, h + 1)
                dve.wait_ge(r_D, 3 * h + 3)
                if h >= 2:
                    dve.wait_ge(r_o, h - 1)
                b = 2 * (h % 2)
                dve.scalar_tensor_tensor(r_weights(h), acc[:, b:b + 2, :].rearrange("p b (k n) -> p (b k) n", k=2), P ** -0.5,
                                         r_dec[h % 2][:, :, :], ALU.mult, ALU.mult).then_inc(r_pt, 1)

            def centre(h):
                dve.wait_ge(r_mean, h + 1)
                for c in range(2):
                    dve.scalar_tensor_tensor(ro[:, h, c, :], wk[:, 2, 0:256], -1.0 / 256, ro[:, h, c, :], ALU.mult, ALU.add)\
                        .then_inc(r_cent, 1)

            def normed(h):
                dve.wait_ge(r_root, h + 1)
                dve.reciprocal(r_rs[:, 1, :], r_rs[:, 0, :]).then_inc(r_nrm, 1)
                dve.wait_ge(r_nrm, 3 * h + 1)
                for c in range(2):
                    dve.tensor_tensor(ro[:, h, c, :], ro[:, h, c, :], r_rs[:, 1, :], ALU.mult).then_inc(r_nrm, 1)
                if h == 0:
                    all_freed(dve, "ret_g")
                for c in range(2):
                    dve.wait_ge(r_nrm, 3 * h + 2 + c)
                    if h >= 1:
                        dve.wait_ge(r_lo, h)
                    dve.scalar_tensor_tensor(r_mix[:, c, :], ro[:, h, c, :], V("gn_g", 2 * h + c), rg[:, 2 * h + c, :],
                                             ALU.mult, ALU.mult).then_inc(r_mixed, 1)

            def lo(h):
                dve.wait_ge(r_hi, h + 1)
                dve.tensor_tensor(H_lo[SEQ][:, 2 * h:2 * h + 2, :], r_mix[:, :, :],
                                  H_hi[SEQ][:, 2 * h:2 * h + 2, :].bitcast(F32), ALU.subtract).then_inc(r_lo, 1)

            arg(0)
            for h in range(RH):
                if h + 1 < RH:
                    arg(h + 1)
                weights(h)
                if h >= 1:
                    normed(h - 1)
                centre(h)
                if h >= 1:
                    lo(h - 1)
            normed(RH - 1)
            lo(RH - 1)

        mh_mul, mh_done = sem("mlp_products"), sem("mlp_hidden_done")

        def act_mlp_in(act, layer, half):
            p = proj[f"mlp{layer}_in{half}"]
            g0 = (2 * layer + half) * p.n

            def slot(st):
                split_hi(act, st)
                r = st.parity()
                for c in range(2):
                    act.wait_ge(acc_ready, st.tile(c))
                    if c == 0 and (st.i is not None or g0 + st.s >= 2):
                        act.wait_ge(mh_mul, 4 * st.s + 4 * (g0 - 1))
                    ins = act.activation(cgu[:, r, c, 0:T2], acc_tile(p, r, c), ACT.Relu)
                    if c == 1:
                        ins.then_inc(freed["act"], 1)
            each_slot(act, p, slot)

        def pool_mlp_in(pool, layer, half):
            p = proj[f"mlp{layer}_in{half}"]
            g0 = (2 * layer + half) * p.n

            def slot(st):
                r = st.parity()

                def part(F, c):
                    m = st.s * 2 + c
                    return F[T2][:, m, :] if st.i is None else F[T2][:, bass.ds(m, 1), :]
                pool.wait_ge(freed["act"], p.freed0 + st.s + 1)
                for c in range(2):
                    x = cgu[:, r, c, 0:T2]
                    pool.tensor_tensor(hid2[:, r, c, :], x, x, ALU.mult).then_inc(mh_mul, 1)
                    pool.tensor_tensor(part(F_hi, c), x, x, ALU.mult).then_inc(mh_mul, 1)
                pool.wait_ge(mh_mul, 4 * st.s + (4 * g0 + 4))
                for c in range(2):
                    pool.tensor_tensor(part(F_lo, c), hid2[:, r, c, :], part(F_hi, c).bitcast(F32), ALU.subtract)\
                        .then_inc(mh_done, 1)
            each_slot(pool, p, slot)

        def dve_add(dve, name, after=None):
            p = proj[name]

            def slot(st):
                split_lo(dve, st)
                for c in range(p.C):
                    m = st.s * p.C + c
                    x = X[:, m, X2:T1] if st.i is None else X[:, bass.ds(m, 1), X2:T1]
                    dve.wait_ge(acc_ready, st.tile(c))
                    if after and c == 0:
                        dve.wait_ge(freed["dve"], proj[after].freed0 + st.s + 1)
                    ins = dve.tensor_tensor(x, acc_tile(p, st.parity(), c), x, ALU.add)
                    if c == p.C - 1:
                        ins.then_inc(freed["dve"], 1)
            each_slot(dve, p, slot)

        def act_mlp(act, layer):
            for half in range(2):
                act_mlp_in(act, layer, half)
                act_plain(act, f"mlp{layer}_out{half}")

        def dve_mlp(dve, layer):
            dve_plain(dve, f"mlp{layer}_in0")
            dve_add(dve, f"mlp{layer}_out0")
            dve_plain(dve, f"mlp{layer}_in1")
            dve_add(dve, f"mlp{layer}_out1", after=f"mlp{layer}_out0")

        def pe_mlp(pe, layer, j):
            for half in range(2):
                g0 = (2 * layer + half) * MLH
                project(pe, f"mlp{layer}_in{half}", lambda k: H_hi[T2][:, k, :], lambda k: H_lo[T2][:, k, :],
                        need=h_need(pe, j) if half == 0 else None)
                project(pe, f"mlp{layer}_out{half}", lambda k: F_hi[T2][:, k, :], lambda k: F_lo[T2][:, k, :],
                        need=lambda k: pe.wait_ge(mh_done, g0 + k + 1))

        def load_second(pool):
            pool.wait_ge(h_ready, 4 * DC)
            pool.dma_start(X[:, :, X2:LAT], t["meta"]).then_inc(s_meta, 16)
            pool.dma_start(lru_w[:, 0, :, :], t["lru_wr"]).then_inc(s_meta, 16)
            pool.dma_start(lru_w[:, 1, :, :], t["lru_wi"]).then_inc(s_meta, 16)
            pool.dma_start(c_mask[:, :, :], t["c_mask"]).then_inc(s_meta, 16)

        (G_I, G_F, G_ABS, G_Z, G_Y, G_Y2, G_Q, G_LF, G_CUM, G_A, G_G, G_M) = range(12)
        LRU_ABS, LRU_Z, LRU_Y, LRU_Y2, LRU_Q, LRU_POS, LRU_NEG, LRU_T = range(0, 64, 8)
        AT = 64
        s_if, s_gabs, s_gz, s_gate = sem("if_ready"), sem("gate_abs"), sem("gate_exp"), sem("gates_ready")
        s_aT, s_aTc, s_vt, s_vtc = sem("a_transposed"), sem("a_copied"), sem("v_transposed"), sem("v_copied")

        def half_log1p(dve, link, z, y, y2, q):
            link(dve.tensor_scalar(y, z, 2.0, None, ALU.add))
            link(dve.reciprocal(y, y))
            link(dve.tensor_tensor(y, y, z, ALU.mult))
            link(dve.tensor_tensor(y2, y, y, ALU.mult))
            link(dve.tensor_scalar(q, y2, 1.0 / 19, None, ALU.mult))
            for k in range(17, 2, -2):
                link(dve.scalar_tensor_tensor(q, q, 1.0 / k, y2, ALU.add, ALU.mult))
            link(dve.scalar_tensor_tensor(q, q, 1.0, y, ALU.add, ALU.mult))

        def act_gates(act):
            lam = V("lru_lam", 0, 8)
            act.wait_ge(s_if, 1)
            act.activation(IF[0:4, G_ABS, :], IF[0:4, G_F, :], ACT.Abs).then_inc(s_gabs, 1)
            act.activation(tiny[:, LRU_ABS:LRU_ABS + 8], lam, ACT.Abs).then_inc(s_gabs, 1)
            act.wait_ge(s_gabs, 2)
            act.activation(IF[0:4, G_Z, :], IF[0:4, G_ABS, :], ACT.Exp, scale=-1.0).then_inc(s_gz, 1)
            act.activation(tiny[:, LRU_Z:LRU_Z + 8], tiny[:, LRU_ABS:LRU_ABS + 8], ACT.Exp, scale=-1.0).then_inc(s_gz, 1)

        def dve_gates(dve, link):
            p = proj["ab_if"]
            st = Step(p, None, 0)
            split_lo(dve, st)
            for c in range(2):
                dve.wait_ge(acc_ready, st.tile(c))
                link(dve.tensor_scalar(IF[0:4, c, :], acc_tile(p, st.parity(), c)[0:4], vec[0:4, VEC["if_bias"] + c:VEC["if_bias"] + c + 1],
                                       None, ALU.add))
            dve.tensor_copy(IF[0:4, G_LF, :], IF[0:4, G_F, :]).then_inc(freed["dve"], 1)
            link(dve.tensor_copy(IF[0:4, G_M, :], IF[0:4, G_I, :]))
            dve.tensor_copy(tiny[0:4, AT + 12:AT + 13], IF[0:4, G_F, 0:1]).then_inc(s_if, 1)

        def dve_gates2(dve, link):
            def row(i):
                return IF[0:4, i, :]
            dve.wait_ge(s_gz, 2)
            half_log1p(dve, link, row(G_Z), row(G_Y), row(G_Y2), row(G_Q))
            link(dve.tensor_scalar(row(G_LF), row(G_F), 0.0, None, ALU.min))
            link(dve.scalar_tensor_tensor(row(G_LF), row(G_Q), -2.0, row(G_LF), ALU.mult, ALU.add))
            link(dve.tensor_tensor_scan(row(G_CUM), one_row[0:4, :], row(G_LF), 0.0, ALU.mult, ALU.add))
            link(dve.tensor_tensor(row(G_A), row(G_I), row(G_CUM), ALU.subtract))
            link(dve.tensor_tensor_scan(row(G_G), one_row[0:4, :], row(G_A), 0.0, ALU.mult, ALU.max))
            dve.tensor_tensor(row(G_M), row(G_G), row(G_CUM), ALU.add).then_inc(s_gate, 1)
            def col(i):
                return tiny[:, i:i + 8]
            half_log1p(dve, link, col(LRU_Z), col(LRU_Y), col(LRU_Y2), col(LRU_Q))
            link(dve.tensor_scalar(col(LRU_T), V("lru_lam", 0, 8), -1.0, 0.0, ALU.mult, ALU.max))
            link(dve.scalar_tensor_tensor(col(LRU_T), col(LRU_Q), 2.0, col(LRU_T), ALU.mult, ALU.add))
            dve.tensor_scalar(col(LRU_POS), col(LRU_T), 8.0, None, ALU.mult)
            dve.tensor_scalar(col(LRU_NEG), col(LRU_T), -8.0, None, ALU.mult).then_inc(s_gate, 1)
            dve.wait_ge(s_aT, 1)
            dve.tensor_copy(tiny[:, AT:AT + 8], wk[:, 0, 0:8]).then_inc(s_aTc, 1)
            dve.tensor_copy(tiny[0:16, AT + 8:AT + 12], wk[0:16, 0, 8:12]).then_inc(s_aTc, 1)

        def pe_turn_values(pe, vF, g0):
            for i in range(6):
                (t0, n), half = TILES2[i // 2], i % 2
                if i >= 4:
                    pe.wait_ge(s_vtc, g0 + i - 3)
                for c in range(4):
                    mm = pe.transpose(acc[0:n, i % 4, c * P:(c + 1) * P], vF[:, 4 * half + c, t0:t0 + n], ident[:, :])
                mm.then_inc(s_vt, 1)
            pe.wait_ge(s_vtc, g0 + 6)

        def act_turn_values(act, vT, g0):
            for i in range(6):
                (t0, n), half = TILES2[i // 2], i % 2
                act.wait_ge(s_vt, g0 + i + 1)
                act.activation(vT[0:n, i // 2, half * 512:half * 512 + 512], acc[0:n, i % 4, :], ACT.Copy).then_inc(s_vtc, 1)

        MH = 4
        m_b, m_s, m_D, m_mask = sem("mlstm_broadcast"), sem("mlstm_scores"), sem("mlstm_decay"), sem("mlstm_masked")
        m_pt, m_num, m_e, m_r = sem("mlstm_weighted"), sem("mlstm_sums"), sem("mlstm_bounds"), sem("mlstm_divisor")
        m_hh, m_sq, m_var, m_root = sem("mlstm_h"), sem("mlstm_square"), sem("mlstm_square_sum"), sem("mlstm_root")
        m_out, m_hi, m_lo = sem("mlstm_out"), sem("mlstm_hi"), sem("mlstm_lo")

        def pe_mlstm(pe):
            pe.wait_ge(s_gate, 2)
            for st, (t0, n) in enumerate(TILES2):
                mm = pe.transpose(wk[0:n, 0, 4 * st:4 * st + 4], IF[0:4, G_A, t0:t0 + n], ident[0:4, 0:4])
            mm.then_inc(s_aT, 1)
            for name in ("ab_qk", "ab_v", "ab_o", "ab_xb", "ab_gate"):
                all_freed(pe, name)
            pe_turn_values(pe, vF, 0)
            pe.wait_ge(s_aTc, 2)
            for h in range(MH):
                if h >= 1:
                    pe.wait_ge(m_e, 2 * h)
                    pe.wait_ge(m_D, 3 * h)
                pe.matmul(wk[:, 0, 0:T2], head_sel[0:4, h, :], IF[0:4, G_G, :], start=True, stop=True)
                pe.matmul(wk[:, 1, 0:T2], head_sel[0:4, h, :], IF[0:4, G_M, :], start=True, stop=True).then_inc(m_b, 1)
                for st, (t0, n) in enumerate(TILES2):
                    if h >= 1:
                        pe.wait_ge(m_pt, 3 * (h - 1) + st + 1)
                    for c in range(2):
                        mm = pe.matmul(acc[0:n, st, t0:T2], qk[:, 8 + 2 * h + c, t0:t0 + n], qk[:, 2 * h + c, t0:T2],
                                       start=c == 0, stop=c == 1)
                    mm.then_inc(m_s, 1)
                if h >= 1:
                    pe.wait_ge(m_root, h)
                    pe.wait_ge(m_hh, 4 * h)
                for st, (t0, n) in enumerate(TILES2):
                    pe.wait_ge(m_pt, 3 * h + st + 1)
                    pe.matmul(acc[:, 3, t0:T2], ones[0:n, :], m_P[0:n, st, t0:T2], start=st == 0, stop=st == 2)
                for c in range(2):
                    for st, (t0, n) in enumerate(TILES2):
                        mm = pe.matmul(wk[:, 2 + c, t0:T2], vT[0:n, st, h * 256 + c * P:h * 256 + (c + 1) * P],
                                       m_P[0:n, st, t0:T2], start=st == 0, stop=st == 2)
                mm.then_inc(m_num, 1)
                pe.wait_ge(m_sq, h + 1)
                pe.wait_ge(m_e, 2 * h + 2)
                for c in range(2):
                    mm = pe.matmul(acc[:, 3, 0:T2], ones[:, :], m_sqr[:, c, :], start=c == 0, stop=c == 1)
                mm.then_inc(m_var, 1)

        def act_mlstm(act):
            act_turn_values(act, vT, 0)
            act.wait_ge(s_aTc, 2)
            for h in range(MH):
                act.wait_ge(m_b, h + 1)
                for st, (t0, n) in enumerate(TILES2):
                    if h >= 1:
                        act.wait_ge(m_pt, 3 * (h - 1) + st + 1)
                    act.activation(m_Dk[0:n, st, t0:T2], wk[0:n, 0, t0:T2], ACT.Exp, scale=-1.0,
                                   bias=tiny[0:n, AT + 4 * st + h:AT + 4 * st + h + 1]).then_inc(m_D, 1)
                if h >= 1:
                    act.wait_ge(m_r, 2 * h)
                act.activation(m_E[:, :], wk[:, 1, 0:T2], ACT.Exp, scale=-1.0).then_inc(m_e, 1)
                act.wait_ge(m_num, h + 1)
                act.activation(m_ad[:, :], acc[:, 3, 0:T2], ACT.Abs).then_inc(m_e, 1)
                act.wait_ge(m_hh, 4 * h + 4)
                act.activation(m_sqr[:, :, :], m_h[:, :, :], ACT.Square).then_inc(m_sq, 1)
                act.wait_ge(m_var, h + 1)
                act.activation(m_rt[:, 0, :], acc[:, 3, 0:T2], ACT.Sqrt, bias=V("eps"), scale=1.0 / 256).then_inc(m_root, 1)
                act.wait_ge(m_out, 2 * h + 2)
                act.activation(H_hi[T2][:, 2 * h:2 * h + 2, :], m_h[:, :, :], ACT.Copy).then_inc(m_hi, 1)

        def pool_mlstm(pool):
            for h in range(MH):
                for st, (t0, n) in enumerate(TILES2):
                    pool.wait_ge(m_D, 3 * h + st + 1)
                    x = m_Dk[0:n, st, t0:t0 + n]
                    pool.affine_select(out=x, in_=x, compare_op=ALU.is_ge, fill=0.0, base=0, pattern=[[1, n]],
                                       channel_multiplier=-1).then_inc(m_mask, 1)

        def dve_mlstm(dve, link):
            for h in range(MH):
                for st, (t0, n) in enumerate(TILES2):
                    dve.wait_ge(m_s, 3 * h + st + 1)
                    dve.wait_ge(m_mask, 3 * h + st + 1)
                    if h >= 1:
                        dve.wait_ge(m_num, h)
                    dve.scalar_tensor_tensor(m_P[0:n, st, t0:T2], acc[0:n, st, t0:T2], 1.0 / 16, m_Dk[0:n, st, t0:T2],
                                             ALU.mult, ALU.mult).then_inc(m_pt, 1)
                dve.wait_ge(m_e, 2 * h + 2)
                dve.tensor_tensor(m_ad[:, :], m_ad[:, :], m_E[:, :], ALU.max).then_inc(m_r, 1)
                dve.wait_ge(m_r, 2 * h + 1)
                if h == 0:
                    all_freed(dve, "ab_o")
                dve.reciprocal(m_ad[:, :], m_ad[:, :]).then_inc(m_r, 1)
                dve.wait_ge(m_r, 2 * h + 2)
                for c in range(2):
                    dve.tensor_tensor(m_h[:, c, :], wk[:, 2 + c, 0:T2], m_ad[:, :], ALU.mult).then_inc(m_hh, 1)
                for c in range(2):
                    dve.wait_ge(m_hh, 4 * h + c + 1)
                    dve.tensor_tensor(m_h[:, c, :], m_h[:, c, :], og[:, 2 * h + c, :], ALU.mult).then_inc(m_hh, 1)
                dve.wait_ge(m_root, h + 1)
                link(dve.reciprocal(m_rt[:, 1, :], m_rt[:, 0, :]))
                dve.wait_ge(m_hh, 4 * h + 4)
                for c in range(2):
                    dve.scalar_tensor_tensor(m_h[:, c, :], m_h[:, c, :], V("mlstm_norm", 2 * h + c), m_rt[:, 1, :],
                                             ALU.mult, ALU.mult).then_inc(m_out, 1)
                dve.wait_ge(m_hi, h + 1)
                dve.tensor_tensor(H_lo[T2][:, 2 * h:2 * h + 2, :], m_h[:, :, :], H_hi[T2][:, 2 * h:2 * h + 2, :].bitcast(F32),
                                  ALU.subtract).then_inc(m_lo, 1)
                if h + 1 < MH:
                    dve.wait_ge(m_lo, h + 1)

        l_conv, l_gate, l_act, l_tanh, l_dec = sem("lru_conv"), sem("lru_gate_sums"), sem("lru_gates"), sem("lru_tanh"), sem("lru_decay")
        l_arg, l_root, l_h, l_hi, l_lo = sem("lru_root_arg"), sem("lru_root"), sem("lru_out"), sem("lru_hi"), sem("lru_lo")
        R, I, XC, TT = qk[:, 0:8, :], qk[:, 8:16, :], vF, l_t

        def pe_lru(pe):
            for i in range(16):
                c, which = i // 2, i % 2
                pe.wait_ge(l_conv, 25 + c)
                if i == 0:
                    pe.wait_ge(m_root, MH)
                if i >= 4:
                    pe.wait_ge(l_act, i - 3)
                pe.matmul(acc[:, i % 4, 0:T2], lru_w[:, which, c, :], XC[:, c, :], start=True, stop=True).then_inc(l_gate, 1)

        def act_lru(act):
            for i in range(16):
                c, which = i // 2, i % 2
                act.wait_ge(l_gate, i + 1)
                act.activation((R, I)[which][:, c, :], acc[:, i % 4, 0:T2], ACT.Sigmoid,
                               bias=V("lru_b_i" if which else "lru_b_r", c)).then_inc(l_act, 1)
            for c in range(8):
                if c == 0:
                    act.wait_ge(l_act, 16)
                act.activation(TT[:, c, :], R[:, c, :], ACT.Tanh, scale=tiny[:, LRU_POS + c:LRU_POS + c + 1]).then_inc(l_tanh, 1)
            for c in range(8):
                act.activation(R[:, c, :], R[:, c, :], ACT.Exp, scale=tiny[:, LRU_NEG + c:LRU_NEG + c + 1]).then_inc(l_dec, 1)
            act.wait_ge(l_arg, 1)
            act.activation(TT[:, :, :], TT[:, :, :], ACT.Sqrt, scale=2.0).then_inc(l_root, 1)
            act.wait_ge(l_h, 9)
            act.activation(H_hi[T2][:, 8:16, :], XC[:, :, :], ACT.Copy).then_inc(l_hi, 1)

        def dve_lru(dve, link):
            all_freed(dve, "ab_xb")
            dve.wait_ge(m_num, MH)
            for c in range(8):
                dve.tensor_scalar(XC[:, c, :], xb[:, c, :], V("lru_conv_w", 24 + c), V("lru_conv_b", c), ALU.mult, ALU.add)\
                    .then_inc(l_conv, 1)
            for j, tap in enumerate((2, 1, 0)):
                d = j + 1
                for c in range(8):
                    dve.wait_ge(l_conv, 8 * j + c + 1)
                    dve.scalar_tensor_tensor(XC[:, c, d:T2], xb[:, c, 0:T2 - d], V("lru_conv_w", 8 * tap + c), XC[:, c, d:T2],
                                             ALU.mult, ALU.add).then_inc(l_conv, 1)
            dve.wait_ge(l_tanh, 8)
            dve.wait_ge(l_conv, 32)
            link(dve.tensor_scalar(xb[:, :, :], TT[:, :, :], 1.0, None, ALU.add))
            link(dve.reciprocal(xb[:, :, :], xb[:, :, :]))
            dve.tensor_tensor(TT[:, :, :], TT[:, :, :], xb[:, :, :], ALU.mult).then_inc(l_arg, 1)
            link(dve.tensor_tensor(I[:, :, :], I[:, :, :], XC[:, :, :], ALU.mult))
            dve.wait_ge(l_root, 1)
            link(dve.tensor_tensor(I[:, :, :], I[:, :, :], TT[:, :, :], ALU.mult))
            dve.wait_ge(l_dec, 8)
            for c in range(8):
                dve.tensor_tensor_scan(XC[:, c, :], R[:, c, :], I[:, c, :], 0.0, ALU.mult, ALU.add).then_inc(l_h, 1)
            all_freed(dve, "ab_gate")
            dve.wait_ge(l_h, 8)
            dve.tensor_tensor(XC[:, :, :], XC[:, :, :], gate[:, :, :], ALU.mult).then_inc(l_h, 1)
            dve.wait_ge(l_hi, 1)
            dve.tensor_tensor(H_lo[T2][:, 8:16, :], XC[:, :, :], H_hi[T2][:, 8:16, :].bitcast(F32), ALU.subtract).then_inc(l_lo, 1)

        CH = 8
        LAMBDA_INIT = 0.8 - 0.6 * math.exp(-0.3 * 1)
        CU = 3 * CH
        C_SUM, C_NLAM, C_GAIN, C_MAX = 64, 68, 69, 0
        c_s, c_scaled, c_max, c_exp = sem("diff_scores"), sem("diff_scaled"), sem("diff_max"), sem("diff_exp")
        c_rec, c_p, c_tr, c_pt, c_o = sem("diff_recip"), sem("diff_probs"), sem("diff_transposed"), sem("diff_probsT"), sem("diff_out")
        c_sq, c_var, c_root, c_fin = sem("diff_square"), sem("diff_square_sum"), sem("diff_root"), sem("diff_normed")
        c_hi, c_lo, c_lam = sem("diff_hi"), sem("diff_lo"), sem("diff_lambda")

        def unit(w):
            h, qt = w // 3, w % 3
            t0, n = TILES2[qt]
            return h, qt, t0, n, t0 + n

        def c_items():
            return [cq[:, h, :] for h in range(CH)] + [ck[:, h, :] for h in range(CH)]

        def pe_diff(pe):
            pe_rope(pe, c_items(), T2, swap_c, 16, lambda: (all_freed(pe, "c_q"), all_freed(pe, "c_k")))
            all_freed(pe, "c_v")
            pe_turn_values(pe, cvF, 6)
            pe.wait_ge(rot_done, 32)

            def scores(w):
                h, qt, t0, n, keys = unit(w)
                if w >= 2:
                    pe.wait_ge(c_scaled, w - 1)
                for m in range(2):
                    b = 64 * m
                    mm = pe.matmul(acc[0:n, 2 * (w % 2) + m, 0:keys], cq[b:b + 64, h, t0:t0 + n], ck[b:b + 64, h, 0:keys],
                                   start=True, stop=True)
                mm.then_inc(c_s, 1)

            def turn(w):
                h, qt, t0, n, keys = unit(w)
                pe.wait_ge(c_p, w + 1)
                if w >= 2:
                    pe.wait_ge(c_pt, w - 1)
                for kt in range(qt + 1):
                    k0, kn = TILES2[kt]
                    mm = pe.transpose(wk[0:kn, w % 2, kt * P:kt * P + n], c_sb[0:n, w % 3, 0, k0:k0 + kn], ident[0:n, 0:n])
                mm.then_inc(c_tr, 1)

            def values(h):
                pe.wait_ge(c_pt, 3 * h + 3)
                if h >= 2:
                    pe.wait_ge(c_root, h - 1)
                for kt, (k0, kn) in enumerate(TILES2):
                    mm = pe.matmul(wk[:, 2 + h % 2, k0:T2], cvT[0:kn, kt, h * P:(h + 1) * P], cP[0:kn, h % 2, kt, k0:T2],
                                   start=kt == 0, stop=kt == 2)
                mm.then_inc(c_o, 1)

            def total(h):
                pe.wait_ge(c_sq, 2 * h + 2)
                pe.matmul(wk[:, 2 + h % 2, 0:T2], ones[:, :], csq[:, h % 2, :], start=True, stop=True).then_inc(c_var, 1)

            scores(0)
            scores(1)
            for w in range(CU + 2):
                if w < CU:
                    turn(w)
                if w + 2 < CU:
                    scores(w + 2)
                if w % 3 == 0 and w >= 3:
                    values(w // 3 - 1)
                if w % 3 == 1 and w >= 4:
                    total((w - 4) // 3)

        def act_diff(act):
            act.wait_ge(c_lam, 2)
            act.activation(tiny[:, C_SUM:C_SUM + 2], tiny[:, C_SUM:C_SUM + 2], ACT.Exp).then_inc(c_lam, 1)
            act_turn_values(act, cvT, 6)

            def probs(w):
                h, qt, t0, n, keys = unit(w)
                act.wait_ge(c_max, w + 1)
                if w >= 3:
                    act.wait_ge(c_p, w - 2)
                o = C_MAX + 8 * (w % 3)
                for m in range(2):
                    s = c_sb[0:n, w % 3, m, 0:keys]
                    ins = act.activation(s, s, ACT.Exp, bias=tiny[0:n, o + m:o + m + 1], accum_out=tiny[0:n, o + 2 + m:o + 3 + m])
                ins.then_inc(c_exp, 1)

            def copy(w):
                h, qt, t0, n, keys = unit(w)
                act.wait_ge(c_tr, w + 1)
                if h >= 2:
                    act.wait_ge(c_o, h - 1)
                m = min(qt + 1, 2)
                ins = act.activation(cP[:, h % 2, 0:m, t0:t0 + n],
                                     wk[:, w % 2, 0:2 * P].rearrange("p (k q) -> p k q", q=P)[:, 0:m, 0:n], ACT.Copy)
                if qt == 2:
                    ins = act.activation(cP[0:16, h % 2, 2, t0:t0 + n], wk[0:16, w % 2, 2 * P:2 * P + n], ACT.Copy)
                ins.then_inc(c_pt, 1)

            def square(h):
                act.wait_ge(c_o, h + 1)
                if h >= 2:
                    act.wait_ge(c_lo, h - 1)
                act.activation(co[:, h % 2, :], wk[:, 2 + h % 2, 0:T2], ACT.Copy).then_inc(c_sq, 1)
                act.activation(csq[:, h % 2, :], wk[:, 2 + h % 2, 0:T2], ACT.Square).then_inc(c_sq, 1)

            def root_of(h):
                act.wait_ge(c_var, h + 1)
                if h >= 1:
                    act.wait_ge(c_fin, 2 * h)
                act.activation(crt[:, 0, :], wk[:, 2 + h % 2, 0:T2], ACT.Sqrt, bias=V("eps"), scale=1.0 / P).then_inc(c_root, 1)

            def hi(h):
                act.wait_ge(c_fin, 2 * h + 2)
                act.activation(H_hi[T2][:, h, :], co[:, h % 2, :], ACT.Copy).then_inc(c_hi, 1)

            for w in range(CU + 4):
                if w < CU:
                    probs(w)
                if 1 <= w <= CU:
                    copy(w - 1)
                if w % 3 == 1 and w >= 4:
                    square((w - 4) // 3)
                if w % 3 == 2 and w >= 5:
                    root_of((w - 5) // 3)
                if w % 3 == 0 and w >= 6:
                    hi((w - 6) // 3)

        def dve_diff(dve, link):
            lam = V("lambda", 0, 256).rearrange("p (a b d) -> p a b d", a=2, b=2)
            link(dve.tensor_tensor(csq[:, 0, 0:128].rearrange("p (a d) -> p a d", a=2), lam[:, :, 0, :], lam[:, :, 1, :], ALU.mult))
            for i in range(2):
                dve.tensor_reduce(tiny[:, C_SUM + i:C_SUM + i + 1], csq[:, 0, 64 * i:64 * i + 64], AX.X, ALU.add).then_inc(c_lam, 1)
            dve.wait_ge(c_lam, 3)
            link(dve.tensor_tensor(tiny[:, C_NLAM:C_NLAM + 1], tiny[:, C_SUM + 1:C_SUM + 2], tiny[:, C_SUM:C_SUM + 1], ALU.subtract))
            link(dve.tensor_scalar(tiny[:, C_NLAM:C_NLAM + 1], tiny[:, C_NLAM:C_NLAM + 1], -LAMBDA_INIT, None, ALU.add))
            link(dve.tensor_scalar(tiny[:, C_GAIN:C_GAIN + 1], V("subln"), 1.0 - LAMBDA_INIT, None, ALU.mult))
            dve_rope(dve, c_items(), T2, rope_c, c_rope, 16)

            def scale(w):
                h, qt, t0, n, keys = unit(w)
                dve.wait_ge(c_s, w + 1)
                if w >= 3:
                    dve.wait_ge(c_tr, w - 2)
                s = c_sb[0:n, w % 3, :, 0:keys]
                mask = c_mask[0:n, qt:qt + 1, 0:keys].to_broadcast([n, 2, keys])
                b = 2 * (w % 2)
                dve.scalar_tensor_tensor(s, acc[0:n, b:b + 2, 0:keys], 0.125, mask, ALU.mult, ALU.add).then_inc(c_scaled, 1)
                dve.wait_ge(c_scaled, w + 1)
                o = C_MAX + 8 * (w % 3)
                dve.tensor_reduce(tiny[0:n, o:o + 2], s, AX.X, ALU.max, negate=True).then_inc(c_max, 1)

            def norm(w):
                h, qt, t0, n, keys = unit(w)
                o = C_MAX + 8 * (w % 3)
                dve.wait_ge(c_exp, w + 1)
                dve.reciprocal(tiny[0:n, o + 4:o + 6], tiny[0:n, o + 2:o + 4]).then_inc(c_rec, 1)
                dve.wait_ge(c_rec, 2 * w + 1)
                s = c_sb[0:n, w % 3, :, 0:keys]
                dve.tensor_scalar(s[:, 1, :], s[:, 1, :], tiny[0:n, o + 5:o + 6], tiny[0:n, C_NLAM:C_NLAM + 1], ALU.mult, ALU.mult)\
                    .then_inc(c_rec, 1)
                dve.wait_ge(c_rec, 2 * w + 2)
                dve.scalar_tensor_tensor(s[:, 0, :], s[:, 0, :], tiny[0:n, o + 4:o + 5], s[:, 1, :], ALU.mult, ALU.add)\
                    .then_inc(c_p, 1)

            def finish(h):
                dve.wait_ge(c_root, h + 1)
                dve.reciprocal(crt[:, 1, :], crt[:, 0, :]).then_inc(c_fin, 1)
                dve.wait_ge(c_fin, 2 * h + 1)
                dve.scalar_tensor_tensor(co[:, h % 2, :], co[:, h % 2, :], tiny[:, C_GAIN:C_GAIN + 1], crt[:, 1, :],
                                         ALU.mult, ALU.mult).then_inc(c_fin, 1)

            def lo(h):
                dve.wait_ge(c_hi, h + 1)
                dve.tensor_tensor(H_lo[T2][:, h, :], co[:, h % 2, :], H_hi[T2][:, h, :].bitcast(F32), ALU.subtract).then_inc(c_lo, 1)

            for w in range(CU + 5):
                if w < CU:
                    scale(w)
                if 1 <= w <= CU:
                    norm(w - 1)
                if w % 3 == 0 and w >= 6:
                    finish((w - 6) // 3)
                if w % 3 == 1 and w >= 7:
                    lo((w - 7) // 3)

        def act_ffn(act, layer, r):
            act_ffn_in(act, layer, 0)
            act_plain(act, ffn_name(layer, 0, "out"))
            act_ffn_in(act, layer, 1)
            act_y_squares(act, ffn_name(layer, 1, "out"), r)
            act_residual(act, r)

        def dve_ffn(dve, layer, r):
            dve_ffn_in(dve, layer, 0)
            dve_y(dve, ffn_name(layer, 0, "out"))
            dve_ffn_in(dve, layer, 1)
            dve_y(dve, ffn_name(layer, 1, "out"), add=ffn_name(layer, 0, "out"))
            dve_residual(dve, r)

        def pool_ffn(pool, layer, r):
            pool_ffn_in(pool, layer, 0)
            pool_ffn_in(pool, layer, 1)
            pool_y_sum(pool, r)

        def pe_ffn_halves(pe, layer, j):
            pe_ffn(pe, layer, 0, j)
            pe_ffn(pe, layer, 1, j)
            pe_residual(pe, j)


        def store_out(sp):
            if t["stop"] is not None:
                last = layers[-1]
                sp.wait_ge(*((x_ready, 8 * t["stop"]) if t["stop"] < 5 else (freed["dve"], last.freed0 + last.n)))
                sp.dma_start(out, X[:, :, :] if t["stop"] < 3 else X[:, :, LAT:T1] if t["stop"] < 5 else X[:, :, X2:T1]).then_inc(s_out[0], 16)
                sp.wait_ge(s_out[0], 16)
                return
            for c in range(DC):
                sp.wait_ge(n32_ready, DC * FINAL + c + 1)
                sp.dma_start(out[:, c, :], n32[:, c % 2, META:T2]).then_inc(s_out[c % 2], 16)
            for s in s_out:
                sp.wait_ge(s, 16 * DC // 2)

        block = ctx.enter_context(nc.Block())

        @block.sync
        def _(sp):
            stream_weights(sp)
            store_out(sp)

        @block.scalar
        def _(act):
            load_constants(act)
            act_c(act)
            act.wait_ge(w_loaded[0], 16)
            act.activation(w_hi[:, 0, 0:layers[0].width], w_raw[:, 0, 0:layers[0].width], ACT.Copy).then_inc(hi_done, 1)
            act_plain(act, "ada0")
            act_rpb(act)
            act_plain(act, "ada1")
            act_norm(act, 0)
            act_gelu(act, "hyb_g", g_sb)
            act_gelu(act, "hyb_u", u_sb)
            for name in ("hyb_v", "hyb_k", "hyb_q"):
                act_plain(act, name)
            act_sgu(act)
            act_attn(act)
            act_y_squares(act, "hyb_out", 0)
            act_residual(act, 0)
            act_norm(act, 1)
            act_ffn(act, 0, 1)
            act_norm(act, 2)
            for name in ("ret_k", "ret_v", "ret_q"):
                act_plain(act, name)
            act_gelu(act, "ret_g", rg, ACT.Silu)
            act_ret(act)
            act_y_squares(act, "ret_out", 2)
            act_residual(act, 2)
            act_norm(act, 3)
            act_ffn(act, 1, 3)
            act_norm(act, 4)
            act_plain(act, "ab_if")
            act_gates(act)
            act_plain(act, "ab_qk")
            act_plain(act, "ab_v")
            act_gelu(act, "ab_o", og, ACT.Sigmoid)
            act_plain(act, "ab_xb")
            act_gelu(act, "ab_gate", gate)
            act_mlstm(act)
            act_lru(act)
            act_plain(act, "ab_out")
            act_norm(act, 5)
            act_mlp(act, 0)
            act_norm(act, 6)
            for name in ("c_q", "c_k", "c_v"):
                act_plain(act, name)
            act_diff(act)
            act_plain(act, "c_out")
            act_norm(act, 7)
            act_mlp(act, 1)
            act_norm(act, 8)

        @block.vector
        def _(dve):
            link = chain(dve, "dve")
            dve_c(dve)
            dve.wait_ge(hi_done, 1)
            dve.tensor_tensor(w_lo[:, 0, 0:layers[0].width], w_raw[:, 0, 0:layers[0].width],
                              w_hi[:, 0, 0:layers[0].width].bitcast(F32), ALU.subtract).then_inc(lo_done, 1)
            dve_ada(dve, 0, link)
            dve_ada(dve, 1, link)
            dve_norm(dve, 0)
            dve_plain(dve, "hyb_g")
            dve_plain(dve, "hyb_u")
            dve_copy_tokens(dve, "hyb_v", v_sb)
            dve_copy(dve, "hyb_k", k_sb)
            dve_copy(dve, "hyb_q", q_sb)
            dve_sgu(dve, link)
            dve_attn(dve)
            dve_y(dve, "hyb_out")
            dve_residual(dve, 0)
            dve_norm(dve, 1)
            dve_ffn(dve, 0, 1)
            dve_norm(dve, 2)
            dve_copy(dve, "ret_k", rk)
            dve_copy_tokens(dve, "ret_v", rv)
            dve_copy(dve, "ret_q", rq)
            dve_plain(dve, "ret_g")
            dve_ret(dve)
            dve_y(dve, "ret_out")
            dve_residual(dve, 2)
            dve_norm(dve, 3)
            dve_ffn(dve, 1, 3)
            dve_norm(dve, 4)
            dve_gates(dve, link)
            dve_copy(dve, "ab_qk", qk)
            dve_copy(dve, "ab_v", vF)
            dve_plain(dve, "ab_o")
            dve_copy(dve, "ab_xb", xb)
            dve_plain(dve, "ab_gate")
            dve_gates2(dve, link)
            dve_mlstm(dve, link)
            dve_lru(dve, link)
            dve_add(dve, "ab_out")
            dve_norm(dve, 5)
            dve_mlp(dve, 0)
            dve_norm(dve, 6)
            dve_copy(dve, "c_q", cq)
            dve_copy(dve, "c_k", ck)
            dve_copy(dve, "c_v", cvF)
            dve_diff(dve, link)
            dve_add(dve, "c_out")
            dve_norm(dve, 7)
            dve_mlp(dve, 1)
            dve_norm(dve, 8)

        @block.gpsimd
        def _(pool):
            link = chain(pool, "pool")
            pool_rpb(pool, link)
            pool_y_sum(pool, 0)
            pool_ffn(pool, 0, 1)
            pool_ret(pool)
            pool_y_sum(pool, 2)
            pool_ffn(pool, 1, 3)
            load_second(pool)
            pool_mlstm(pool)
            pool_mlp_in(pool, 0, 0)
            pool_mlp_in(pool, 0, 1)
            pool_mlp_in(pool, 1, 0)
            pool_mlp_in(pool, 1, 1)

        @block.tensor
        def _(pe):
            pe_ada(pe, 0)
            pe_rpb(pe)
            pe_ada(pe, 1)
            pe.wait_ge(s_flipped, 6)
            pe_norm(pe, 0)
            hyb = (lambda k: H_hi[T1][:, k, :], lambda k: H_lo[T1][:, k, :])
            project(pe, "hyb_g", *hyb, need=h_need(pe, 0))
            for name in ("hyb_u", "hyb_v", "hyb_k", "hyb_q"):
                project(pe, name, *hyb)
            pe_sgu(pe)
            pe_attn(pe)
            project(pe, "hyb_out", *hyb, need=lambda k: pe.wait_ge(at_lo, NU // 2) if k < 4 else pe.wait_ge(sgu_lo, k - 3))
            pe_residual(pe, 0)
            pe_norm(pe, 1)
            pe_ffn_halves(pe, 0, 1)
            pe_norm(pe, 2)
            ret = (lambda k: H_hi[T1][:, k, LAT:T1], lambda k: H_lo[T1][:, k, LAT:T1])
            project(pe, "ret_k", *hyb, need=h_need(pe, 2))
            project(pe, "ret_v", *hyb)
            project(pe, "ret_q", *ret)
            project(pe, "ret_g", *ret)
            pe_ret(pe)
            project(pe, "ret_out", lambda k: H_hi[SEQ][:, k, :], lambda k: H_lo[SEQ][:, k, :],
                    need=lambda k: pe.wait_ge(r_lo, k // 2 + 1))
            pe_residual(pe, 2)
            pe_norm(pe, 3)
            pe_ffn_halves(pe, 1, 3)
            pe_norm(pe, 4)
            second = (lambda k: H_hi[T2][:, k, :], lambda k: H_lo[T2][:, k, :])
            project(pe, "ab_if", *second, need=h_need(pe, 4))
            for name in ("ab_qk", "ab_v", "ab_o", "ab_xb", "ab_gate"):
                project(pe, name, *second)
            pe_mlstm(pe)
            pe_lru(pe)
            pe.wait_ge(l_act, 16)
            project(pe, "ab_out", *second,
                    need=lambda k: pe.wait_ge(m_lo, k // 2 + 1) if k < 8 else pe.wait_ge(l_lo, 1))
            pe_norm(pe, 5)
            pe_mlp(pe, 0, 5)
            pe_norm(pe, 6)
            project(pe, "c_q", *second, need=h_need(pe, 6))
            project(pe, "c_k", *second)
            project(pe, "c_v", *second)
            pe_diff(pe)
            project(pe, "c_out", *second, need=lambda k: pe.wait_ge(c_lo, k + 1))
            pe_norm(pe, 7)
            pe_mlp(pe, 1, 7)
            pe_norm(pe, 8)


def _slots(w, cols=256):
    rows, m = w.shape
    return np.ascontiguousarray(w.reshape(rows // P, P, m // cols, cols).transpose(2, 1, 0, 3)
                                .reshape(m // cols, P, rows // P * cols))


def _chunks(v):
    return np.ascontiguousarray(v.reshape(-1, P).T)


def _packed(a):
    cols = np.zeros((P, NVEC), np.float32)

    def put(name, block):
        cols[:block.shape[0], VEC[name]:VEC[name] + block.shape[1]] = block
    both = np.stack([a["c"][0], a["c_ctx"]])
    put("c", both.reshape(2, DC, P).transpose(2, 1, 0).reshape(P, 2 * DC))
    for name, v in [("norm_g", a["norm_g"]), ("ada_b", a["ada_b"]), ("conv_w", a["ffn_conv_w"]), ("conv_b", a["ffn_conv_b"]),
                    ("gn_g", a["ret_gn_g"]), ("norm_mix", a["norm_mix_2"]), ("norm_mlp", a["norm_mlp_2"]),
                    ("norm_final", a["norm_final_2"]), ("mlstm_norm", a["mlstm_norm_2"]), ("lru_conv_w", a["lru_conv_w_2"]),
                    ("lru_conv_b", a["lru_conv_b_2"]), ("lru_b_r", a["lru_b_r_2"]), ("lru_b_i", a["lru_b_i_2"]),
                    ("lru_lam", a["lru_lambda_2"]), ("subln", a["c_subln_2"])]:
        put(name, _chunks(v))
    put("decay", np.broadcast_to(a["ret_log_decay"].reshape(1, 16), (P, 16)))
    put("lambda", np.broadcast_to(a["c_lambda_2"].reshape(1, 256), (P, 256)))
    put("if_bias", a["ab_if_bias_2"].reshape(2, 4).T)
    put("eps", np.full((P, 1), EPS, np.float32))
    return cols


def _swap(pairs):
    m = np.zeros((P, P), np.float32)
    for i, j in pairs:
        m[j, i] = -1.0
        m[i, j] = 1.0
    return m


def _constants():
    c = {"ident": np.eye(P, dtype=np.float32), "ones": np.ones((P, P), np.float32), "one_row": np.ones((P, T2), np.float32)}
    flip = np.zeros((P, P), np.float32)
    flip[np.arange(P), np.concatenate([np.arange(64)[::-1], 64 + np.arange(64)[::-1]])] = 1.0
    c["flip"] = flip
    c["swap_ret"] = _swap([(i, i + 64) for i in range(64)])
    c["swap_c"] = _swap([(b + i, b + i + 8) for b in (0, 64) for i in range(8)])
    sel = np.zeros((P, 4, P), np.float32)
    for h in range(4):
        sel[h, h, :] = 1.0
    c["head_sel"] = sel
    tok = np.arange(SEQ)
    inv = (np.float32(10000.0) ** (-np.arange(32, dtype=np.float32) / np.float32(32))).astype(np.float32)
    ang = np.concatenate([(tok // GRID_W).astype(np.float32)[:, None] * inv, (tok % GRID_W).astype(np.float32)[:, None] * inv], -1)
    ang = np.concatenate([ang, ang], -1).T
    c["rope_ret"] = np.stack([np.cos(ang), np.sin(ang)], 1).astype(np.float32)
    inv2 = (np.float32(500000.0) ** (-np.arange(0, 16, 2, dtype=np.float32) / np.float32(16))).astype(np.float32)
    ang2 = np.arange(T2, dtype=np.float32)[None, :] * inv2[:, None]
    cs, sn = np.ones((P, T2), np.float32), np.zeros((P, T2), np.float32)
    for b in (0, 8, 64, 72):
        cs[b:b + 8], sn[b:b + 8] = np.cos(ang2), np.sin(ang2)
    c["rope_c"] = np.stack([cs, sn], 1)
    c["dist"] = (np.arange(SEQ)[None, :] - np.arange(P)[:, None]).astype(np.float32)
    mask = np.zeros((P, 3, T2), np.float32)
    for i, (t0, n) in enumerate(TILES2):
        mask[:, i, :] = np.where(np.arange(T2)[None, :] <= t0 + np.arange(P)[:, None], 0.0, NEG)
    c["c_mask"] = mask
    return c


def _weights(a):
    w = {}
    for i in range(2):
        w[f"ada{i}"] = _slots(a["ada_w"][i])
        win, wout = a["ffn_w_in"][i], a["ffn_w_out"][i]
        pair = win.reshape(D, 2, 22, P).transpose(0, 2, 1, 3).reshape(D, 2 * 22 * P)
        for half in range(2):
            w[f"ffn{i}_in{half}"] = _slots(pair[:, half * 2816:(half + 1) * 2816])
            w[f"ffn{i}_out{half}"] = _slots(wout[half * 1408:(half + 1) * 1408], P)
            w[f"mlp{i}_in{half}"] = _slots(a["mlp_w1_2"][i][:, half * 2048:(half + 1) * 2048])
            w[f"mlp{i}_out{half}"] = _slots(a["mlp_w2_2"][i][half * 2048:(half + 1) * 2048], P)
    hyb = a["hyb_w_in"][0]
    for j, name in enumerate("qkvug"):
        w["hyb_" + name] = _slots(hyb[:, j * 512:(j + 1) * 512])
    w["hyb_out"] = _slots(a["hyb_w_out"][0])
    ret = a["ret_w_in"][0]
    for name, x, y in [("q", 0, 1024), ("k", 1024, 2048), ("v", 2048, 4096), ("g", 4096, 6144)]:
        w["ret_" + name] = _slots(ret[:, x:y])
    w["ret_out"] = _slots(a["ret_w_out"][0], P)
    ab = a["ab_w_in_2"][0]
    gates = np.zeros((D, 256), np.float32)
    gates[:, 0:4], gates[:, 128:132] = ab[:, 4096:4100], ab[:, 4100:4104]
    w["ab_if"] = _slots(gates)
    for name, x, y in [("qk", 0, 2048), ("v", 2048, 3072), ("o", 3072, 4096), ("xb", 4104, 5128), ("gate", 5128, 6152)]:
        w["ab_" + name] = _slots(ab[:, x:y])
    w["ab_out"] = _slots(a["ab_w_out_2"][0], P)
    for j, name in enumerate("qkv"):
        w["c_" + name] = _slots(a["c_w_in_2"][0][:, j * D:(j + 1) * D])
    w["c_out"] = _slots(a["c_w_out_2"][0])
    return w


def kernel(**inputs):
    import concourse.bacc as _bacc
    from concourse.bass_utils import run_bass_kernel_spmd as _run

    a = {k: np.asarray(v) for k, v in inputs.items()}
    arrays = {"w_" + k: v for k, v in _weights(a).items() if k in {p.name for p in PROJ}}
    arrays.update(_constants())
    arrays["vec"] = _packed(a)
    arrays["x"] = np.concatenate([a["ctx"][0], a["x"][0]]).T.reshape(DC, P, T1).transpose(1, 0, 2)
    arrays["meta"] = a["meta_tokens_2"].T.reshape(DC, P, META).transpose(1, 0, 2)
    arrays["na_rpb"] = a["na_rpb"].reshape(-1)
    arrays["sgu_w"] = a["sgu_w"][0].transpose(2, 0, 1)
    arrays["sgu_b"] = np.repeat(a["sgu_b"][0].reshape(4, 2, P), 64, axis=1).transpose(1, 0, 2)
    for name, w in (("lru_wr", a["lru_w_r_2"]), ("lru_wi", a["lru_w_i_2"])):
        arrays[name] = w[0].transpose(1, 0, 2)
    arrays = {k: np.ascontiguousarray(v) for k, v in arrays.items()}
    nc = _bacc.Bacc("TRN2", target_bir_lowering=False, num_devices=1)
    t = {k: nc.dram_tensor("in_" + k, v.shape, F32, kind="ExternalInput").ap() for k, v in arrays.items()}
    t["stop"] = STOP
    shape = (P, DC, SEQ if STOP in (None, 3, 4) else T1 if STOP < 3 else T2)
    out = nc.dram_tensor("out_0", shape, F32, kind="ExternalOutput").ap()
    stack_kernel(nc, t, out, PROJ)
    r = _run(nc, [{"in_" + k: v for k, v in arrays.items()}], core_ids=[0])
    got = r.results[0]["out_0"]
    return np.ascontiguousarray(got.transpose(2, 1, 0)).reshape(1, shape[2], D)
```

```python
from contextlib import ExitStack
import math

import numpy as np

import concourse.bass as bass
from concourse import mybir

F32 = mybir.dt.float32
F32R = mybir.dt.float32r
ALU = mybir.AluOpType
ACT = mybir.ActivationFunctionType
AX = mybir.AxisListType

P = 128
D = 1024
DC = D // P
SEQ = 256
CTX = 256
META = 16
T1 = CTX + SEQ
T2 = META + SEQ
LAT = CTX
X2 = CTX - META
EPS = 1e-6
SLOT = 2048
FFH = 11
MLH = 16
GRID_W = 64
NEG = -1e30

TILES2 = [(0, 128), (128, 128), (256, 16)]


def _columns():
    at, n = {}, 0
    for name, width in [
        ("c", 16), ("norm_g", 64), ("ada_b", 96), ("conv_w", 2 * 3 * 44), ("conv_b", 2 * 44), ("gn_g", 16),
        ("decay", 16), ("norm_mix", 16), ("norm_mlp", 16), ("norm_final", 8),
        ("mlstm_norm", 8), ("lru_conv_w", 32), ("lru_conv_b", 8), ("lru_b_r", 8), ("lru_b_i", 8),
        ("lru_lam", 8), ("subln", 1), ("lambda", 256), ("if_bias", 2), ("eps", 1), ("pad", 5),
    ]:
        at[name] = n
        n += width
    return at, n


VEC, NVEC = _columns()


class Proj:

    def __init__(self, name, n, K, C, T, kind="feat", freed_by="dve"):
        self.name, self.n, self.K, self.C, self.T, self.kind, self.freed_by = name, n, K, C, T, kind, freed_by
        self.width = K * (256 if kind == "tok" else P * C)
        self.half = (K + 1) // 2
        self.cut = self.half * self.width // K
        self.tiles = 4 if kind == "tok" else C


PROJ = [
    Proj("hyb_g", 2, 8, 2, T1, freed_by="act"), Proj("hyb_u", 2, 8, 2, T1, freed_by="act"),
    Proj("hyb_v", 2, 8, 2, T1, kind="tok"), Proj("hyb_k", 2, 8, 2, T1), Proj("hyb_q", 2, 8, 2, T1),
    Proj("hyb_out", 4, 8, 2, T1),
    Proj("ffn0_in0", FFH, 8, 2, T1), Proj("ffn0_out0", 8, FFH, 1, T1),
    Proj("ffn0_in1", FFH, 8, 2, T1), Proj("ffn0_out1", 8, FFH, 1, T1),
    Proj("ret_k", 4, 8, 2, T1), Proj("ret_v", 8, 8, 2, T1, kind="tok"), Proj("ret_q", 4, 8, 2, SEQ),
    Proj("ret_g", 8, 8, 2, SEQ, freed_by="act"), Proj("ret_out", 8, 16, 1, SEQ),
    Proj("ffn1_in0", FFH, 8, 2, SEQ), Proj("ffn1_out0", 8, FFH, 1, SEQ),
    Proj("ffn1_in1", FFH, 8, 2, SEQ), Proj("ffn1_out1", 8, FFH, 1, SEQ),
    Proj("ab_if", 1, 8, 2, T2), Proj("ab_qk", 8, 8, 2, T2), Proj("ab_v", 4, 8, 2, T2),
    Proj("ab_o", 4, 8, 2, T2, freed_by="act"), Proj("ab_xb", 4, 8, 2, T2),
    Proj("ab_gate", 4, 8, 2, T2, freed_by="act"), Proj("ab_out0", 4, 8, 2, T2), Proj("ab_out1", 4, 8, 2, T2),
    Proj("mlp0_in0", 8, 8, 2, T2, freed_by="act"), Proj("mlp0_out0", 8, MLH, 1, T2),
    Proj("mlp0_in1", 8, 8, 2, T2, freed_by="act"), Proj("mlp0_out1", 8, MLH, 1, T2),
    Proj("c_q", 4, 8, 2, T2), Proj("c_k", 4, 8, 2, T2), Proj("c_v", 4, 8, 2, T2), Proj("c_out", 4, 8, 2, T2),
    Proj("mlp1_in0", 8, 8, 2, T2, freed_by="act"), Proj("mlp1_out0", 8, MLH, 1, T2),
    Proj("mlp1_in1", 8, 8, 2, T2, freed_by="act"), Proj("mlp1_out1", 8, MLH, 1, T2),
]


def _number(projections):
    slot, tile, freed, before = 0, 0, {"act": 0, "dve": 0}, None
    for p in projections:
        p.slot0, p.tile0, p.freed0 = slot, tile, freed[p.freed_by]
        p.handover = (before, freed[before]) if before not in (None, p.freed_by) else None
        slot, tile = slot + p.n, tile + p.n * p.tiles
        freed[p.freed_by] += p.n
        before = p.freed_by
        p.last = False
        p.next = None
        p.peel = p.freed0 < 2 or p.name in ("ffn0_in0", "mlp0_in0")
    for p, q in zip(projections, projections[1:]):
        p.next = q
    return {p.name: p for p in projections}


class Step:

    def __init__(self, p, i, b):
        self.p, self.i, self.b = p, i, b
        self.s = b if i is None else 2 * i + b

    def parity(self, ahead=0):
        return (self.p.slot0 + self.b + ahead) % 2

    def turn(self, ahead=0):
        n = (self.p.slot0 + self.b + ahead) // 2
        return n if self.i is None else self.i + n

    def tile(self, c):
        return self.p.tile0 + self.s * self.p.tiles + c + 1


def each_slot(eng, p, body, peel=False, after=None):
    if after:
        for s in range(p.n):
            body(Step(p, None, s))
            after(s)
        return
    first = min(2, p.n) if p.peel or peel else 0
    pairs = (p.n - 1 - first) // 2
    if pairs < 2:
        pairs = 0
    for s in range(first):
        body(Step(p, None, s))
    if pairs:
        with eng.Fori(0, pairs) as i:
            for b in range(2):
                body(Step(p, i, first + b))
    for s in range(first + 2 * pairs, p.n):
        body(Step(p, None, s))


def stack_kernel(nc, t, out, layers):
    proj = _number(layers)
    ctx = ExitStack()
    with ctx:
        base = 16512

        def at(name, shape, offset, dt=F32):
            assert offset + 4 * int(np.prod(shape[1:])) <= 229344 - base, name
            return nc.alloc_sbuf_tensor_at(name, shape, dt, offset=base + offset)

        KB = 1024
        w_raw = at("w_raw", [P, 2, SLOT], 0)
        w_hi = at("w_hi", [P, 2, SLOT], 16 * KB, F32R)
        w_lo = at("w_lo", [P, 2, SLOT], 32 * KB, F32R)
        X = at("X", [P, DC, T1], 48 * KB)
        HB = 4352 * 4
        h0 = 64 * KB
        c0 = h0 + 2 * HB
        at_const = [c0]

        def const(name, shape):
            t = at(name, shape, at_const[0])
            at_const[0] += (4 * int(np.prod(shape[1:])) + 31) // 32 * 32
            return t

        vec = const("vec", [P, NVEC])
        ident = const("ident", [P, P])
        ones = const("ones", [P, P])
        flip = const("flip", [P, P])
        swap_ret = const("swap_ret", [P, P])
        swap_c = const("swap_c", [P, P])
        head_sel = const("head_sel", [P, 4, P])
        one_row = const("one_row", [P, T2])
        rope_ret = const("rope_ret", [P, 2, SEQ])
        rope_c = const("rope_c", [P, 2, T2])
        dist = const("dist", [P, SEQ])
        cvec = const("cvec", [P, DC, 2])
        mod = const("mod", [P, 2, 48, 2])
        gains = const("gains", [P, 2, 4, 2, DC])
        tiny = const("tiny", [P, 96])
        A = at_const[0]

        H_hi = {T1: at("Hhi512", [P, DC, T1], h0, F32R), SEQ: at("Hhi256", [P, 16, SEQ], h0, F32R),
                T2: at("Hhi272", [P, 16, T2], h0, F32R)}
        H_lo = {T1: at("Hlo512", [P, DC, T1], h0 + HB, F32R), SEQ: at("Hlo256", [P, 16, SEQ], h0 + HB, F32R),
                T2: at("Hlo272", [P, 16, T2], h0 + HB, F32R)}

        Y = at("Y", [P, DC, T1], A)
        nt0 = A + 60 * KB - 256
        sq_acc = at("sq_acc", [P, T1], nt0 + 12 * KB)
        sq = at("sq", [P, 2, T1], nt0 + 2 * KB)
        root = at("root", [P, T1], nt0 + 6 * KB)
        rstd = at("rstd", [P, T1], nt0 + 8 * KB)
        nt = at("nt", [P, 2, T1], nt0 + 10 * KB)
        n32 = at("n32", [P, 2, T1], nt0 + 14 * KB)
        ada_first = [at("ada_first0", [P, 4, SLOT], A), at("ada_first1", [P, 4, SLOT], h0)]
        ada_ring = at("ada_ring", [P, 2, SLOT], nt0 + 18 * KB)
        ada_sums = [at("ada_sums0", [P, 4, 2, 256], A + 32 * KB), at("ada_sums1", [P, 2, 2, 256], A + 58 * KB)]
        F_hi = {T1: at("Fhi512", [P, FFH, T1], A + 16 * KB, F32R), SEQ: at("Fhi256", [P, FFH, SEQ], A + 16 * KB, F32R),
                T2: at("Fhi272", [P, MLH, T2], A + 16 * KB, F32R)}
        F_lo = {T1: at("Flo512", [P, FFH, T1], A + 38 * KB, F32R), SEQ: at("Flo256", [P, FFH, SEQ], A + 38 * KB, F32R),
                T2: at("Flo272", [P, MLH, T2], A + 38 * KB, F32R)}
        cgu = at("cgu", [P, 2, 2, T1], A + 60 * KB)
        sg = at("sg", [P, 2, T1], A + 68 * KB)
        hid = at("hid", [P, 2, T1], A + 72 * KB)
        hid2 = at("hid2", [P, 2, 2, T2], A + 72 * KB)
        g_sb = at("g_sb", [P, 4, T1], A)
        u_sb = at("u_sb", [P, 4, T1], A + 8 * KB)
        v_sb = at("v_sb", [P, 4, 512], A + 16 * KB)
        k_sb = at("k_sb", [P, 4, T1], A + 24 * KB)
        q_sb = at("q_sb", [P, 4, T1], A + 32 * KB)
        rpb = at("rpb", [P, 8, 6, GRID_W], A + 40 * KB)
        rpb_up = at("rpb_up", [P, 8, 6, GRID_W], A + 78 * KB)
        sgu_w = at("sgu_w", [P, 8, P], A + 52 * KB)
        sgu_b = at("sgu_b", [P, 4, P], A + 56 * KB)
        gT = at("gT", [P, 4, 512], A + 62 * KB)
        sgu_t = at("sgu_t", [P, 2, T1], A + 70 * KB)
        sgu_r = at("sgu_r", [P, 2, T1], A + 58 * KB)
        s_sb = at("s_sb", [P, 3, T1], A + 62 * KB)
        pT = at("pT", [P, 2, 4, SEQ], A + 68 * KB)
        rk = at("rk", [P, 8, T1], A)
        ro = at("ro", [P, 8, 2, SEQ], A)
        rv = at("rv", [P, 4, 2048], A + 16 * KB)
        rq = at("rq", [P, 8, SEQ], A + 48 * KB)
        rg = at("rg", [P, 16, SEQ], A + 56 * KB)
        r_dist = at("r_dist", [P, 2, 2, SEQ], A + 72 * KB)
        r_dec = [at(f"r_dec{i}", [P, 4, SEQ], A + (76 + 4 * i) * KB) for i in range(2)]
        r_rope = at("r_rope", [P, 2, 2, SEQ], A + 80 * KB)
        r_e = at("r_e", [P, 2, SEQ], A + 84 * KB)
        r_rs = at("r_rs", [P, 2, SEQ], A + 86 * KB)
        r_mix = at("r_mix", [P, 2, SEQ], A + 88 * KB)
        r_sq = at("r_sq", [P, 2, SEQ], A + 90 * KB)
        qk = at("qk", [P, 16, T2], A)
        vF = at("vF", [P, 8, T2], A + 17 * KB)
        og = at("og", [P, 8, T2], A + 26 * KB)
        xb = at("xb", [P, 8, T2], A + 35 * KB)
        gate = at("gate", [P, 8, T2], A + 44 * KB)
        vT = at("vT", [P, 3, D], A + 53 * KB)
        l_t = at("l_t", [P, 8, T2], A + 53 * KB)
        IF = at("IF", [P, 12, T2], A + 65 * KB)
        c_mask = at("c_mask", [P, 3, T2], A + 80 * KB)
        lru_w = at("lru_w", [P, 2, 8, P], A + 84 * KB)
        m0, m1 = h0 + 8 * 4 * T2, h0 + HB + 8 * 4 * T2
        m_Dk = at("m_Dk", [P, 3, T2], m0)
        m_P = at("m_P", [P, 3, T2], m0 + 12 * T2)
        m_E = at("m_E", [P, T2], m0 + 24 * T2)
        m_ad = at("m_ad", [P, T2], m0 + 28 * T2)
        m_h = at("m_h", [P, 2, T2], m1)
        m_sqr = at("m_sqr", [P, 2, T2], m1 + 8 * T2)
        m_rt = at("m_rt", [P, 2, T2], m1 + 16 * T2)
        cq = at("cq", [P, 8, T2], A)
        ck = at("ck", [P, 8, T2], A + 9 * KB)
        cvF = at("cvF", [P, 8, T2], A + 18 * KB)
        cvT = at("cvT", [P, 3, D], A + 27 * KB)
        c_sb = at("c_sb", [P, 3, 2, T2], A + 39 * KB)
        cP = at("cP", [P, 2, 3, T2], A + 46 * KB)
        c_rope = at("c_rope", [P, 2, 2, T2], A + 53 * KB)
        co = at("co", [P, 2, T2], A + 58 * KB)
        csq = at("csq", [P, 2, T2], A + 61 * KB)
        crt = at("crt", [P, 2, T2], A + 64 * KB)

        wk = ctx.enter_context(nc.psum_tensor("wk", [P, 4, 512], F32))
        acc = ctx.enter_context(nc.psum_tensor("acc", [P, 4, 512], F32))

        sems = {}

        def sem(name):
            sems[name] = ctx.enter_context(nc.semaphore(name))
            return sems[name]

        w_loaded = [sem("w_loaded0"), sem("w_loaded1")]
        hi_done, lo_done = sem("w_hi_done"), sem("w_lo_done")
        acc_ready = sem("acc_ready")
        freed = {"act": sem("acc_freed_act"), "dve": sem("acc_freed_dve")}
        own = {"act": sem("act_chain"), "dve": sem("dve_chain"), "pool": sem("pool_chain")}

        def chain(eng, name):
            count = [0]

            def link(ins):
                count[0] += 1
                ins.then_inc(own[name], 1)
                eng.wait_ge(own[name], count[0])
            return link

        def acc_tile(p, r, c):
            if p.kind == "tok":
                return acc[:, 2 * r + c // 2, (c % 2) * 256:(c % 2) * 256 + 256]
            return acc[:, 2 * r + c, 0:p.T]

        def stream_weights(sp):
            for p in layers:
                src = t["w_" + p.name]

                def load(slot, r, value):
                    if value is not None:
                        sp.wait_ge(lo_done, 2 * value)
                    sp.dma_start(w_raw[:, r, 0:p.width], slot).then_inc(w_loaded[r], 16)

                pairs = p.n // 2 if p.slot0 >= 2 and p.n >= 4 else 0
                if pairs:
                    with sp.Fori(0, pairs) as i:
                        for b in range(2):
                            s = 2 * i + b
                            load(src[bass.ds(s, 1), :, :].rearrange("a p n -> p (a n)"), (p.slot0 + b) % 2,
                                 s + (p.slot0 - 1))
                for s in range(2 * pairs, p.n):
                    g = p.slot0 + s
                    load(src[s], g % 2, g - 1 if g >= 2 else None)

        def split_hi(act, st):
            p, r = st.p, st.parity(1)
            q = p if st.i is not None or st.b + 1 < p.n else p.next
            if q is None:
                return
            act.wait_ge(w_loaded[r], 16 * (st.turn(1) + 1))
            if st.i is not None or p.tile0 + st.s * p.tiles > 0:
                act.wait_ge(acc_ready, st.tile(-1))
            for a, b in ((0, q.cut), (q.cut, q.width)):
                act.activation(w_hi[:, r, a:b], w_raw[:, r, a:b], ACT.Copy).then_inc(hi_done, 1)

        def split_lo(dve, st):
            p, r = st.p, st.parity(1)
            q = p if st.i is not None or st.b + 1 < p.n else p.next
            if q is None:
                return
            for i, (a, b) in enumerate(((0, q.cut), (q.cut, q.width))):
                dve.wait_ge(hi_done, 2 * st.s + (2 * p.slot0 + 3 + i))
                dve.tensor_tensor(w_lo[:, r, a:b], w_raw[:, r, a:b], w_hi[:, r, a:b].bitcast(F32),
                                  ALU.subtract).then_inc(lo_done, 1)

        def split_first(eng):
            q = layers[0]
            for i, (a, b) in enumerate(((0, q.cut), (q.cut, q.width))):
                if eng is nc.scalar:
                    eng.wait_ge(w_loaded[0], 16)
                    eng.activation(w_hi[:, 0, a:b], w_raw[:, 0, a:b], ACT.Copy).then_inc(hi_done, 1)
                else:
                    eng.wait_ge(hi_done, i + 1)
                    eng.tensor_tensor(w_lo[:, 0, a:b], w_raw[:, 0, a:b], w_hi[:, 0, a:b].bitcast(F32),
                                      ALU.subtract).then_inc(lo_done, 1)

        def project(pe, name, x_hi, x_lo, need=None, after=None):
            p = proj[name]
            if p.handover:
                pe.wait_ge(freed[p.handover[0]], p.handover[1])

            def slot(st):
                r = st.parity()
                if st.i is not None or p.freed0 + st.s - 1 > 0:
                    pe.wait_ge(freed[p.freed_by], p.freed0 + st.s - 1)
                order = [(c, k) for c in range(p.tiles) for k in range(p.K)]
                first = need is not None and st.i is None and st.b == 0
                if first:
                    order.sort(key=lambda ck: ck[1])
                for c, k in order:
                    o = acc_tile(p, r, c)
                    if c == 0:
                        if k in (0, p.half):
                            pe.wait_ge(lo_done, 2 * st.s + (2 * p.slot0 + (1 if k == 0 else 2)))
                        if first:
                            need(k)
                    if p.kind == "tok":
                        w = slice(k * 256, k * 256 + 256)
                        toks = slice(P * c, P * c + P)
                        pe.matmul(o, x_hi(k)[:, toks], w_hi[:, r, w], start=k == 0, stop=False)
                        pe.matmul(o, x_hi(k)[:, toks], w_lo[:, r, w], start=False, stop=False)
                        mm = pe.matmul(o, x_lo(k)[:, toks], w_hi[:, r, w], start=False, stop=k == p.K - 1)
                    else:
                        w = slice((k * p.C + c) * P, (k * p.C + c + 1) * P)
                        pe.matmul(o, w_hi[:, r, w], x_hi(k), start=k == 0, stop=False)
                        pe.matmul(o, w_hi[:, r, w], x_lo(k), start=False, stop=False)
                        mm = pe.matmul(o, w_lo[:, r, w], x_hi(k), start=False, stop=k == p.K - 1)
                    if k == p.K - 1:
                        mm.then_inc(acc_ready, 1)

            each_slot(pe, p, slot, peel=need is not None, after=after)

        s_vec, s_const, s_const2, s_bias, s_x = (sem(n) for n in ("vec_loaded", "constants_loaded", "late_constants_loaded",
                                                                 "rpb_loaded", "x_loaded"))
        CONSTS = [("ones", ones), ("flip", flip)]
        CONSTS2 = [("ident", ident), ("one_row", one_row), ("sgu_w", sgu_w), ("sgu_b", sgu_b), ("dist", dist),
                   ("rope_ret", rope_ret), ("head_sel", head_sel), ("swap_ret", swap_ret), ("swap_c", swap_c),
                   ("rope_c", rope_c)]
        N_CONST, N_CONST2, N_BIAS = 16 * len(CONSTS), 16 * len(CONSTS2), 16 * 16

        def load_constants(act):
            act.dma_start(vec[:], t["vec"]).then_inc(s_vec, 16)
            act.dma_start(X[:, :, :], t["x"]).then_inc(s_x, 16)
            for name, dst in CONSTS:
                act.dma_start(dst[:], t[name]).then_inc(s_const, 16)

        def load_biases(pool):
            rows = t["na_rpb"].tensor
            for s in range(2):
                for h in range(8):
                    src = bass.AP(rows, h * 465 + (5 - s) * 31 + 15 - 63, [[1, GRID_W], [31, 6], [1, GRID_W]])
                    pool.dma_start(rpb_up[64 * s:64 * s + 64, h, :, :], src).then_inc(s_bias, 16)

        def load_late_constants(pool):
            for name, dst in CONSTS2:
                pool.dma_start(dst[:], t[name]).then_inc(s_const2, 16)

        NSUM = 0
        LAM = 40

        def V(name, i=0, n=1):
            return vec[:, VEC[name] + i:VEC[name] + i + n]

        def Vd(name, i):
            return vec[:, bass.ds(i + VEC[name], 1)]

        ADA_FIRST, ADA_SLOTS = 8, 24
        s_cvec, s_gain, s_mod = sem("cvec_ready"), sem("gains_ready"), sem("mod_taken")
        ada_loaded, ada_ring_loaded = [sem("ada_first_loaded0"), sem("ada_first_loaded1")], \
            [sem("ada_ring_loaded0"), sem("ada_ring_loaded1")]
        ada_done, ada_used = sem("ada_first_done"), sem("ada_ring_used")

        def load_ada_first(sp):
            for s in range(ADA_FIRST):
                sp.dma_start(ada_first[s // 4][:, s % 4, :], t["w_ada"][s]).then_inc(ada_loaded[s // 4], 16)

        def load_ada_ring(pool):
            pool.wait_ge(s_flip, 6)
            for r in range(2):
                pool.dma_start(ada_ring[:, r, :], t["w_ada"][ADA_FIRST + r]).then_inc(ada_ring_loaded[r], 16)

        def load_ada_pairs(pool, first, last):
            with pool.Fori(0, (last - first) // 2) as i:
                for r in range(2):
                    pool.wait_ge(ada_used, 2 * i + (first - 1 + r))
                    pool.dma_start(ada_ring[:, r, :], t["w_ada"][bass.ds(2 * i + (ADA_FIRST + first + r), 1), :, :]
                                   .rearrange("a p n -> p (a n)")).then_inc(ada_ring_loaded[r], 16)

        def act_c(act):
            act.wait_ge(s_vec, 16)
            act.activation(cvec[:, :, :], V("c", 0, 16).rearrange("p (k s) -> p k s", s=2), ACT.Silu).then_inc(s_cvec, 1)

        def ada_products(pe, w, bank, m):
            for k in range(DC):
                mm = pe.matmul(wk[:, bank, 2 * m:2 * m + 2], w[:, (2 * k + m % 2) * P:(2 * k + m % 2 + 1) * P],
                               cvec[:, k, :], start=k == 0, stop=k == DC - 1)
            return mm

        ADA_DVE = 8
        ada_mac = sem("ada_chunk_added")

        def ada_sum(j):
            return ada_sums[0][:, j, :, :] if j < 4 else ada_sums[1][:, j % 2, :, :]

        def dve_ada(dve, j):
            if j == 0:
                dve.wait_ge(s_cvec, 1)
                dve.wait_ge(ada_loaded[1], 4 * 16)
            if j >= 4:
                g = j - 4
                dve.wait_ge(ada_ring_loaded[g % 2], 16 * (g // 2 + 1))
                if g >= 2:
                    dve.wait_ge(ada_used, g - 1)
            w = ada_first[1][:, j, :] if j < 4 else ada_ring[:, j % 2, :]
            for k in range(DC):
                for s in range(2):
                    o, x, c = ada_sum(j)[:, s, :], w[:, k * 256:(k + 1) * 256], cvec[:, k, s:s + 1]
                    if k == 0:
                        dve.tensor_scalar(o, x, c, None, ALU.mult).then_inc(ada_mac, 1)
                    else:
                        dve.wait_ge(ada_mac, 16 * j + 2 * k + s - 1)
                        dve.scalar_tensor_tensor(o, x, c, o, ALU.mult, ALU.add).then_inc(ada_mac, 1)

        def pe_ada_sum(pe, j):
            m = 8 + 2 * j if j < 4 else 16 + 2 * (j - 4)
            if j == 4:
                pe.wait_ge(s_mod, 1)
            pe.wait_ge(ada_mac, 16 * (j + 1))
            for c in range(2):
                for s in range(2):
                    mm = pe.matmul(wk[:, 3, 2 * (m + c) + s:2 * (m + c) + s + 1], ada_sum(j)[:, s, c * P:(c + 1) * P],
                                   ones[:, 0:1], start=True, stop=True)
            if j >= 4:
                mm.then_inc(ada_used, 1)
            if j == 3:
                mm.then_inc(ada_done, 1)

        def pe_ada_first(pe):
            pe.wait_ge(s_cvec, 1)
            pe.wait_ge(ada_loaded[0], 4 * 16)
            for s in range(4):
                for c in range(2):
                    ada_products(pe, ada_first[0][:, s, :], 3, 2 * s + c)
            for j in range(4):
                pe_ada_sum(pe, j)

        def pe_ada_ring(pe, first, last):
            for e in range(first, last):
                g = e // 2
                if e % 2 == 0:
                    pe.wait_ge(ada_ring_loaded[g % 2], 16 * (g // 2 + 1))
                m = e + 2 * ADA_FIRST
                mm = ada_products(pe, ada_ring[:, g % 2, :], 3 if m < 48 else 2, m % 48)
                if e % 2 == 1:
                    mm.then_inc(ada_used, 1)

        def act_plain(act, name, meanwhile={}):
            def slot(st):
                split_hi(act, st)
                if meanwhile:
                    meanwhile[st.s]()
            each_slot(act, proj[name], slot)

        def dve_plain(dve, name, after=None):
            each_slot(dve, proj[name], lambda st: split_lo(dve, st), after=after)

        def dve_mod(dve, link, layer, m0, m1, parts):
            n = m1 - m0
            bias = V("ada_b", layer * 48 + m0, n).rearrange("p (m s) -> p m s", s=1).to_broadcast([P, n, 2])
            dve.tensor_tensor(mod[:, layer, m0:m1, :], wk[:, 3 - layer, 2 * m0:2 * m1].rearrange("p (m s) -> p m s", s=2), bias,
                              ALU.add).then_inc(s_mod, 1)
            dve.wait_ge(s_mod, {(0, 0): 1, (0, 16): 2, (1, 0): 3}[layer, m0])
            for s in range(2):
                for j in parts:
                    part, one = [(1, 1.0), (2, 0.0), (4, 1.0), (5, 0.0)][j]
                    ins = dve.scalar_tensor_tensor(gains[:, layer, j, s, :], mod[:, layer, 8 * part:8 * part + 8, s], one,
                                                   V("norm_g", layer * 32 + j * 8, 8), ALU.add, ALU.mult)
            ins.then_inc(s_gain, 1)

        def dve_mod_first(dve, link):
            dve.wait_ge(ada_done, 1)
            dve_mod(dve, link, 0, 0, 16, [0])

        def dve_mod_rest(dve, link, layer):
            dve.wait_ge(ada_used, (ADA_SLOTS - ADA_FIRST) + layer * ADA_SLOTS)
            dve_mod(dve, link, layer, 16 * (1 - layer), 48, [1, 2, 3] if layer == 0 else [0, 1, 2, 3])

        BOTH = [(1, 0, CTX), (0, CTX, T1)]
        ONLY = [(0, 0, SEQ)]

        def ada_gain(layer, j):
            return lambda s, c: gains[:, layer, j, s, c:c + 1]

        def ada_shift(layer, part):
            return lambda s, c: mod[:, layer, 8 * part + c, s:s + 1]

        NORMS = [(T1, 0, BOTH, ada_gain(0, 0), ada_shift(0, 0)), (T1, 0, BOTH, ada_gain(0, 2), ada_shift(0, 3)),
                 (T1, 0, BOTH, ada_gain(1, 0), ada_shift(1, 0)), (SEQ, LAT, ONLY, ada_gain(1, 2), ada_shift(1, 3))]
        for name, i in [("norm_mix", 0), ("norm_mlp", 0), ("norm_mix", 8), ("norm_mlp", 8), ("norm_final", 0)]:
            NORMS.append((T2, X2, [(0, 0, T2)], lambda s, c, name=name, i=i: V(name, i + c), None))
        FINAL = len(NORMS) - 1
        nsq_ready, nsq_used, root_ready = sem("norm_square_ready"), sem("norm_square_summed"), sem("norm_root_ready")
        rstd_ready, nt_ready = sem("norm_rstd_ready"), sem("norm_scaled_ready")
        n32_ready, hhi_ready, h_ready = sem("norm_out_ready"), sem("h_hi_ready"), sem("h_ready")
        s_out = [sem("out_stored0"), sem("out_stored1")]
        x_ready = sem("x_ready")
        s_meta = sem("meta_loaded")

        def x_ready_for(eng, j, c):
            if j == 0:
                eng.wait_ge(s_x, 16)
            elif j <= 4:
                eng.wait_ge(x_ready, 8 * (j - 1) + c + 1)
            else:
                p = proj[("ab_out1", "mlp0_out1", "c_out", "mlp1_out1")[j - 5]]
                eng.wait_ge(freed["dve"], p.freed0 + c // p.C + 1)
            if j == 4:
                eng.wait_ge(s_meta, 4 * 16)

        def pe_norm(pe, j):
            n = NORMS[j][0]
            if j == 0:
                pe.wait_ge(s_const, N_CONST)
            for c in range(DC):
                pe.wait_ge(nsq_ready, DC * j + c + 1)
                pe.matmul(wk[:, 0, 0:n], ones[:, :], sq[:, c % 2, 0:n], start=c == 0, stop=c == DC - 1)\
                    .then_inc(nsq_used, 1)

        def act_norm(act, j, meanwhile=None):
            n, x0, groups, gain, shift = NORMS[j]
            if j == 0:
                act.wait_ge(s_vec, 16)
            for c in range(DC):
                x_ready_for(act, j, c)
                if c >= 2:
                    act.wait_ge(nsq_used, DC * j + c - 1)
                act.activation(sq[:, c % 2, 0:n], X[:, c, x0:x0 + n], ACT.Square).then_inc(nsq_ready, 1)
            act.wait_ge(nsq_used, DC * (j + 1))
            act.activation(root[:, 0:n], wk[:, 0, 0:n], ACT.Sqrt, bias=V("eps"), scale=1.0 / D).then_inc(root_ready, 1)
            if meanwhile:
                meanwhile()
            if j < 3:
                act.wait_ge(s_gain, j + 1)
            for c in range(DC):
                act.wait_ge(nt_ready, DC * j + c + 1)
                if c >= 2 and j != FINAL:
                    act.wait_ge(h_ready, DC * j + c - 1)
                if c >= 2 and j == FINAL:
                    act.wait_ge(s_out[c % 2], 16 * (c // 2))
                for i, (s, a, b) in enumerate(groups):
                    kw = {} if shift is None else {"bias": shift(s, c)}
                    ins = act.activation(n32[:, c % 2, a:b], nt[:, c % 2, a:b], ACT.Identity, scale=gain(s, c), **kw)
                ins.then_inc(n32_ready, 1)
                if j == FINAL:
                    continue
                act.wait_ge(n32_ready, DC * j + c + 1)
                act.activation(H_hi[n][:, c, 0:n], n32[:, c % 2, 0:n], ACT.Copy).then_inc(hhi_ready, 1)

        def dve_norm(dve, j, meanwhile=None):
            n, x0, groups, gain, shift = NORMS[j]
            dve.wait_ge(root_ready, j + 1)
            dve.reciprocal(rstd[:, 0:n], root[:, 0:n]).then_inc(rstd_ready, 1)
            if meanwhile:
                meanwhile()
            dve.wait_ge(rstd_ready, j + 1)

            def lo(c):
                dve.wait_ge(hhi_ready, DC * j + c + 1)
                dve.tensor_tensor(H_lo[n][:, c, 0:n], n32[:, c % 2, 0:n], H_hi[n][:, c, 0:n].bitcast(F32),
                                  ALU.subtract).then_inc(h_ready, 1)
            for c in range(DC):
                if c >= 2:
                    dve.wait_ge(n32_ready, DC * j + c - 1)
                dve.tensor_tensor(nt[:, c % 2, 0:n], X[:, c, x0:x0 + n], rstd[:, 0:n], ALU.mult).then_inc(nt_ready, 1)
                if c >= 1 and j != FINAL:
                    lo(c - 1)
            if j != FINAL:
                lo(DC - 1)

        def h_need(pe, j):
            return lambda k: pe.wait_ge(h_ready, DC * j + k + 1)

        RES = [(T1, 0, BOTH, (0, 1), "hyb_out"), (T1, 0, BOTH, (0, 3), "ffn0_out1"),
               (SEQ, LAT, ONLY, (1, 1), "ret_out"), (SEQ, LAT, ONLY, (1, 3), "ffn1_out1")]
        ysq_ready, ysq_used, ysum_ready = sem("y_square_ready"), sem("y_square_added"), sem("y_sum_ready")
        yroot_ready, yrstd_ready, yt_ready = sem("y_root_ready"), sem("y_rstd_ready"), sem("y_scaled_ready")

        def dve_y(dve, name, add=None):
            p = proj[name]
            n = p.T

            def slot(st):
                split_lo(dve, st)
                for c in range(p.C):
                    m = st.s * p.C + c
                    dst = Y[:, m, 0:n] if st.i is None else Y[:, bass.ds(m, 1), 0:n]
                    dve.wait_ge(acc_ready, st.tile(c))
                    if add:
                        dve.wait_ge(freed["dve"], proj[add].freed0 + st.s + 1)
                        ins = dve.tensor_tensor(dst, acc_tile(p, st.parity(), c), dst, ALU.add)
                    else:
                        ins = dve.tensor_copy(dst, acc_tile(p, st.parity(), c))
                    if c == p.C - 1:
                        ins.then_inc(freed["dve"], 1)
            each_slot(dve, p, slot)

        def act_y_squares(act, name, r):
            p = proj[name]
            n = p.T
            for s in range(p.n):
                st = Step(p, None, s)
                split_hi(act, st)
                act.wait_ge(freed["dve"], p.freed0 + s + 1)
                for c in range(p.C):
                    m = s * p.C + c
                    if m >= 2:
                        act.wait_ge(ysq_used, DC * r + m - 1)
                    act.activation(sq[:, m % 2, 0:n], Y[:, m, 0:n], ACT.Square).then_inc(ysq_ready, 1)

        def pool_y_sum(pool, r):
            n = RES[r][0]
            for m in range(DC):
                pool.wait_ge(ysq_ready, DC * r + m + 1)
                if m == 0:
                    pool.tensor_copy(sq_acc[:, 0:n], sq[:, 0, 0:n]).then_inc(ysq_used, 1)
                else:
                    pool.wait_ge(ysq_used, DC * r + m)
                    pool.tensor_tensor(sq_acc[:, 0:n], sq_acc[:, 0:n], sq[:, m % 2, 0:n], ALU.add).then_inc(ysq_used, 1)

        def pe_residual(pe, r):
            n = RES[r][0]
            pe.wait_ge(ysq_used, DC * (r + 1))
            pe.matmul(wk[:, 1, 0:n], ones[:, :], sq_acc[:, 0:n], start=True, stop=True).then_inc(ysum_ready, 1)

        def act_residual(act, r):
            n = RES[r][0]
            act.wait_ge(ysum_ready, r + 1)
            act.activation(root[:, 0:n], wk[:, 1, 0:n], ACT.Sqrt, bias=V("eps"), scale=1.0 / D).then_inc(yroot_ready, 1)

        def dve_residual(dve, r):
            n, x0, groups, (layer, j), _ = RES[r]
            dve.wait_ge(s_gain, 2 + layer)
            dve.wait_ge(yroot_ready, r + 1)
            dve.reciprocal(rstd[:, 0:n], root[:, 0:n]).then_inc(yrstd_ready, 1)
            dve.wait_ge(yrstd_ready, r + 1)

            def update(c):
                dve.wait_ge(yt_ready, DC * r + c + 1)
                for s, a, b in groups:
                    ins = dve.scalar_tensor_tensor(X[:, c, x0 + a:x0 + b], nt[:, c % 2, a:b], gains[:, layer, j, s, c:c + 1],
                                                   X[:, c, x0 + a:x0 + b], ALU.mult, ALU.add)
                ins.then_inc(x_ready, 1)
            for c in range(DC):
                if c >= 2:
                    dve.wait_ge(x_ready, DC * r + c - 1)
                dve.tensor_tensor(nt[:, c % 2, 0:n], Y[:, c, 0:n], rstd[:, 0:n], ALU.mult).then_inc(yt_ready, 1)
                if c >= 1:
                    update(c - 1)
            update(DC - 1)

        conv_mid, conv_left, conv_gate = sem("conv_centre_done"), sem("conv_left_done"), sem("conv_gate_done")
        silu_done, hid_mul, hid_hi, hid_done = sem("silu_done"), sem("hidden_product"), sem("hidden_hi"), sem("hidden_done")

        def ffn_name(layer, half, what):
            return f"ffn{layer}_{what}{half}"

        def act_ffn_in(act, layer, half):
            p = proj[ffn_name(layer, half, "in")]
            n, f0 = p.T, (2 * layer + half) * FFH

            def slot(st):
                split_hi(act, st)
                f, r = st.s + f0, st.parity()
                for c in range(2):
                    act.wait_ge(acc_ready, st.tile(c))
                    if c == 0 and (st.i is not None or f >= 2):
                        act.wait_ge(hid_mul, 2 * f - 2)
                    m = st.s + (22 * c + FFH * half)
                    act.activation(cgu[:, r, c, 0:n], acc_tile(p, r, c), ACT.Identity,
                                   bias=Vd("conv_b", m + layer * 44), scale=Vd("conv_w", m + (layer * 3 + 1) * 44))\
                        .then_inc(conv_mid, 1)
                act.wait_ge(conv_gate, f + 1)
                act.activation(sg[:, r, 0:n], cgu[:, r, 0, 0:n], ACT.Silu).then_inc(silu_done, 1)
            each_slot(act, p, slot)

        def dve_ffn_in(dve, layer, half):
            p = proj[ffn_name(layer, half, "in")]
            n, f0 = p.T, (2 * layer + half) * FFH

            def seqs(ap, a, b):
                return ap.rearrange("p (q t) -> p q t", t=SEQ)[:, :, a:b]

            def slot(st):
                split_lo(dve, st)
                f, r = st.s + f0, st.parity()
                for c in range(2):
                    dve.wait_ge(conv_mid, 2 * f + c + 1)
                    o = cgu[:, r, c, 0:n]
                    w = Vd("conv_w", st.s + (22 * c + FFH * half + layer * 3 * 44))
                    dve.scalar_tensor_tensor(seqs(o, 1, SEQ), seqs(acc_tile(p, r, c), 0, SEQ - 1), w, seqs(o, 1, SEQ),
                                             ALU.mult, ALU.add).then_inc(conv_left, 1)
                for c in range(2):
                    dve.wait_ge(conv_left, 2 * f + c + 1)
                    o = cgu[:, r, c, 0:n]
                    w = Vd("conv_w", st.s + (22 * c + FFH * half + (layer * 3 + 2) * 44))
                    dve.scalar_tensor_tensor(seqs(o, 0, SEQ - 1), seqs(acc_tile(p, r, c), 1, SEQ), w, seqs(o, 0, SEQ - 1),
                                             ALU.mult, ALU.add).then_inc(conv_gate if c == 0 else freed["dve"], 1)
            each_slot(dve, p, slot)

        def pool_hidden(pool, p, f0, left, right, ready):
            n = p.T

            def slot(st):
                f, r = st.s + f0, st.parity()
                hi = F_hi[n][:, bass.ds(st.s, 1), :] if st.i is not None else F_hi[n][:, st.s, :]
                lo = F_lo[n][:, bass.ds(st.s, 1), :] if st.i is not None else F_lo[n][:, st.s, :]
                ready(st)
                pool.tensor_tensor(hid[:, r, 0:n], left(r), right(r), ALU.mult).then_inc(hid_mul, 1)
                pool.tensor_tensor(hi, left(r), right(r), ALU.mult).then_inc(hid_mul, 1)
                pool.wait_ge(hid_mul, 2 * f + 2)
                pool.tensor_tensor(lo, hid[:, r, 0:n], hi.bitcast(F32), ALU.subtract).then_inc(hid_done, 1)
            each_slot(pool, p, slot)

        def pool_ffn_in(pool, layer, half):
            p = proj[ffn_name(layer, half, "in")]
            f0 = (2 * layer + half) * FFH

            def ready(st):
                pool.wait_ge(freed["dve"], p.freed0 + st.s + 1)
                pool.wait_ge(silu_done, st.s + (f0 + 1))
            pool_hidden(pool, p, f0, lambda r: sg[:, r, 0:p.T], lambda r: cgu[:, r, 1, 0:p.T], ready)

        def pe_ffn(pe, layer, half, j):
            n = proj[ffn_name(layer, half, "in")].T
            f0 = (2 * layer + half) * FFH
            project(pe, ffn_name(layer, half, "in"), lambda k: H_hi[n][:, k, :], lambda k: H_lo[n][:, k, :],
                    need=h_need(pe, j) if half == 0 else None)
            project(pe, ffn_name(layer, half, "out"), lambda k: F_hi[n][:, k, :], lambda k: F_lo[n][:, k, :],
                    need=lambda k: pe.wait_ge(hid_done, f0 + k + 1))

        def act_gelu(act, name, dst, func=ACT.Gelu_apprx_tanh, after=None):
            p = proj[name]

            def slot(st):
                split_hi(act, st)
                for c in range(2):
                    m = st.s * 2 + c
                    act.wait_ge(acc_ready, st.tile(c))
                    o = dst[:, m, 0:p.T] if st.i is None else dst[:, bass.ds(m, 1), 0:p.T]
                    ins = act.activation(o, acc_tile(p, st.parity(), c), func)
                    if c == 1:
                        ins.then_inc(freed["act"], 1)
            each_slot(act, p, slot, after=after)

        def dve_copy(dve, name, dst, m0=0, after=None):
            p = proj[name]

            def slot(st):
                split_lo(dve, st)
                for c in range(2):
                    m = st.s * 2 + (c + m0)
                    dve.wait_ge(acc_ready, st.tile(c))
                    o = dst[:, m, 0:p.T] if st.i is None else dst[:, bass.ds(m, 1), 0:p.T]
                    ins = dve.tensor_copy(o, acc_tile(p, st.parity(), c))
                    if c == 1:
                        ins.then_inc(freed["dve"], 1)
            each_slot(dve, p, slot, after=after)

        def dve_copy_tokens(dve, name, dst, after=None):
            p = proj[name]

            def slot(st):
                split_lo(dve, st)
                for j in range(2):
                    dve.wait_ge(acc_ready, st.tile(2 * j + 1))
                    o = dst[:, 2 * j:2 * j + 2, st.s * 256:st.s * 256 + 256] if st.i is None \
                        else dst[:, 2 * j:2 * j + 2, bass.ds(st.s * 256, 256)]
                    ins = dve.tensor_copy(o, acc[:, 2 * st.parity() + j, :].rearrange("p (c n) -> p c n", c=2))
                ins.then_inc(freed["dve"], 1)
            each_slot(dve, p, slot, after=after)

        def all_freed(eng, name):
            p = proj[name]
            eng.wait_ge(freed[p.freed_by], p.freed0 + p.n)

        sgu_sum, sgu_cent, sgu_sq, sgu_sqsum = sem("sgu_sum"), sem("sgu_centred"), sem("sgu_square"), sem("sgu_square_sum")
        sgu_root, sgu_norm, sgu_tr, sgu_copied = sem("sgu_root"), sem("sgu_normed"), sem("sgu_transposed"), sem("sgu_copied")
        sgu_mixed, sgu_gated, sgu_hi, sgu_lo = sem("sgu_mixed"), sem("sgu_gated"), sem("sgu_hi"), sem("sgu_lo")

        def turned(tt):
            return wk[:, 2, :] if tt % 2 == 0 else acc[:, 0, :]

        def pe_sgu(pe):
            for name in ("hyb_k", "hyb_q", "hyb_v"):
                all_freed(pe, name)
            pe.wait_ge(s_const2, N_CONST2)
            all_freed(pe, "hyb_g")
            for c in range(4):
                mm = pe.matmul(wk[:, 0, :], ones[:, :], g_sb[:, c, :], start=c == 0, stop=c == 3)
            mm.then_inc(sgu_sum, 1)
            pe_ada_ring(pe, 16, 20)
            for c in range(4):
                pe.wait_ge(sgu_sq, c + 1)
                pe.matmul(wk[:, 1, :], ones[:, :], sgu_t[:, c % 2, :], start=c == 0, stop=c == 3).then_inc(sgu_sqsum, 1)
            for tt in range(4):
                if tt == 0:
                    pe_ada_ring(pe, 20, 24)
                    pe.wait_ge(sgu_norm, 4)
                if tt >= 2:
                    pe.wait_ge(sgu_copied, tt - 1)
                for c in range(4):
                    mm = pe.transpose(turned(tt)[:, c * P:(c + 1) * P], g_sb[:, c, tt * P:(tt + 1) * P], ident[:, :])
                mm.then_inc(sgu_tr, 1)
            pe.wait_ge(sgu_copied, 4)
            for c in range(4):
                if c == 0:
                    pe.wait_ge(sgu_norm, 4)
                if c >= 2:
                    pe.wait_ge(sgu_gated, 2 * (c - 2) + 1)
                for half in range(2):
                    g = 2 * c + half
                    for tt in range(4):
                        mm = pe.matmul(wk[64 * half:64 * half + 64, c % 2, tt * P:(tt + 1) * P],
                                       gT[:, tt, g * 64:(g + 1) * 64], sgu_w[:, g, :], start=True, stop=True)
                mm.then_inc(sgu_mixed, 1)

        def act_sgu(act):
            for c in range(4):
                act.wait_ge(sgu_cent, c + 1)
                if c >= 2:
                    act.wait_ge(sgu_sqsum, c - 1)
                act.activation(sgu_t[:, c % 2, :], g_sb[:, c, :], ACT.Square).then_inc(sgu_sq, 1)
            act.wait_ge(sgu_sqsum, 4)
            act.activation(sgu_r[:, 0, :], wk[:, 1, :], ACT.Sqrt, bias=V("eps"), scale=1.0 / 512).then_inc(sgu_root, 1)
            for tt in range(4):
                act.wait_ge(sgu_tr, tt + 1)
                act.activation(gT[:, tt, :], turned(tt), ACT.Copy).then_inc(sgu_copied, 1)
            for c in range(4):
                act.wait_ge(sgu_gated, 2 * c + 2)
                act.activation(H_hi[T1][:, 4 + c, :], u_sb[:, c, :], ACT.Copy).then_inc(sgu_hi, 1)

        def dve_sgu(dve, link):
            dve.wait_ge(sgu_sum, 1)
            for c in range(4):
                dve.scalar_tensor_tensor(g_sb[:, c, :], wk[:, 0, :], -1.0 / 512, g_sb[:, c, :], ALU.mult, ALU.add)\
                    .then_inc(sgu_cent, 1)
            dve.wait_ge(sgu_root, 1)
            link(dve.reciprocal(sgu_r[:, 1, :], sgu_r[:, 0, :]))
            for c in range(4):
                dve.wait_ge(sgu_sqsum, c + 1)
                dve.wait_ge(sgu_cent, c + 1)
                dve.tensor_tensor(g_sb[:, c, :], g_sb[:, c, :], sgu_r[:, 1, :], ALU.mult).then_inc(sgu_norm, 1)
            all_freed(dve, "hyb_u")
            dve.wait_ge(s_const2, N_CONST2)
            for c in range(4):
                dve.wait_ge(sgu_mixed, c + 1)
                bias = sgu_b[:, c, :].rearrange("p (a q) -> p a q", a=1).to_broadcast([P, 4, P])
                dve.tensor_tensor(sgu_t[:, c % 2, :].rearrange("p (n q) -> p n q", q=P),
                                  wk[:, c % 2, :].rearrange("p (n q) -> p n q", q=P), bias, ALU.add).then_inc(sgu_gated, 1)
                dve.wait_ge(sgu_gated, 2 * c + 1)
                dve.tensor_tensor(u_sb[:, c, :], u_sb[:, c, :], sgu_t[:, c % 2, :], ALU.mult).then_inc(sgu_gated, 1)
            for c in range(4):
                dve.wait_ge(sgu_hi, c + 1)
                dve.tensor_tensor(H_lo[T1][:, 4 + c, :], u_sb[:, c, :], H_hi[T1][:, 4 + c, :].bitcast(F32),
                                  ALU.subtract).then_inc(sgu_lo, 1)

        NU = 32
        at_s, at_scaled, at_max, at_exp = sem("attn_scores"), sem("attn_scaled"), sem("attn_max"), sem("attn_exp")
        at_rec, at_p, at_tr, at_pt = sem("attn_recip"), sem("attn_probs"), sem("attn_transposed"), sem("attn_probsT")
        at_o, at_hi, at_lo, s_rpb = sem("attn_out"), sem("attn_hi"), sem("attn_lo"), sem("rpb_masked")

        def keys_of(u):
            return CTX if u % 4 < 2 else T1

        s_flip, s_flipped = sem("rpb_flip_ready"), sem("rpb_flipped")

        def pe_rpb(pe, first, last):
            flat = rpb_up[:, :, :, :].rearrange("p h j k -> p (h j k)")
            pe.wait_ge(s_bias, N_BIAS)
            pe.wait_ge(root_ready, 1)
            for b in range(first, last):
                if b >= 3:
                    pe.wait_ge(s_flipped, b - 2)
                pe.matmul(wk[:, b % 3, :], flip[:, :], flat[:, b * 512:(b + 1) * 512], start=True, stop=True)\
                    .then_inc(s_flip, 1)

        def act_rpb(act, first, last):
            flat = rpb[:, :, :, :].rearrange("p h j k -> p (h j k)")
            for b in range(first, last):
                act.wait_ge(s_flip, b + 1)
                act.activation(flat[:, b * 512:(b + 1) * 512], wk[:, b % 3, :], ACT.Copy).then_inc(s_flipped, 1)

        def pool_rpb(pool, link):
            pool.wait_ge(s_flipped, 6)
            for s in range(2):
                part = rpb[64 * s:64 * s + 64, :, :, :].rearrange("p h j k -> p (h j) k")
                lower, upper = part[:, :, 0:48], part[:, :, 16:64]
                link(pool.affine_select(out=lower, in_=lower, compare_op=ALU.is_ge, fill=NEG, base=8,
                                        pattern=[[0, 48], [1, 48]], channel_multiplier=-1))
                ins = pool.affine_select(out=upper, in_=upper, compare_op=ALU.is_ge, fill=NEG, base=7 - 16,
                                         pattern=[[0, 48], [-1, 48]], channel_multiplier=1)
                if s == 0:
                    link(ins)
            ins.then_inc(s_rpb, 1)

        def pe_attn(pe):

            def scores(u):
                h, tt = u // 4, u % 4
                if u >= 2:
                    pe.wait_ge(at_scaled, u - 1)
                b = 64 * (h % 2)
                pe.matmul(acc[:, u % 2, 0:keys_of(u)], q_sb[b:b + 64, h // 2, tt * P:(tt + 1) * P],
                          k_sb[b:b + 64, h // 2, 0:keys_of(u)], start=True, stop=True).then_inc(at_s, 1)

            def turn(u):
                pe.wait_ge(at_p, u + 1)
                if u >= 2:
                    pe.wait_ge(at_pt, u - 1)
                for kt in range(keys_of(u) // P):
                    mm = pe.transpose(acc[:, 2 + u % 2, kt * P:(kt + 1) * P], s_sb[:, u % 3, kt * P:(kt + 1) * P], ident[:, :])
                mm.then_inc(at_tr, 1)

            def values(pair):
                h, n = pair // 2, keys_of(2 * pair) // P
                pe.wait_ge(at_pt, 2 * pair + 2)
                if pair >= 2:
                    pe.wait_ge(at_lo, pair - 1)
                b = 64 * (h % 2)
                for kt in range(n):
                    mm = pe.matmul(wk[b:b + 64, pair % 2, 0:256], v_sb[:, kt, h * 64:h * 64 + 64], pT[:, pair % 2, kt, :],
                                   start=kt == 0, stop=kt == n - 1)
                mm.then_inc(at_o, 1)

            pe.wait_ge(sgu_gated, 8)
            scores(0)
            scores(1)
            for u in range(NU):
                if u + 2 < NU:
                    scores(u + 2)
                turn(u)
                if u % 2 == 0 and u >= 4:
                    values(u // 2 - 2)
                e0, e1 = 24 + 5 * u // 4, 24 + 5 * (u + 1) // 4
                pe_ada_ring(pe, e0, e1)
            values(NU // 2 - 2)
            values(NU // 2 - 1)

        def act_attn(act):
            def probs(u):
                act.wait_ge(at_max, u + 1)
                m = 4 * (u % 3)
                s = s_sb[:, u % 3, 0:keys_of(u)]
                if u >= 3:
                    act.wait_ge(at_p, u - 2)
                act.activation(s, s, ACT.Exp, bias=tiny[:, m:m + 1], accum_out=tiny[:, m + 1:m + 2]).then_inc(at_exp, 1)

            def copy(u):
                act.wait_ge(at_tr, u + 1)
                pair, n = u // 2, keys_of(u) // P
                if pair >= 2:
                    act.wait_ge(at_o, pair - 1)
                act.activation(pT[:, pair % 2, 0:n, (u % 2) * P:(u % 2) * P + P],
                               acc[:, 2 + u % 2, 0:n * P].rearrange("p (k q) -> p k q", q=P), ACT.Copy).then_inc(at_pt, 1)

            def hi(pair):
                act.wait_ge(at_o, pair + 1)
                h, x = pair // 2, (pair % 2) * CTX
                b = 64 * (h % 2)
                act.activation(H_hi[T1][b:b + 64, h // 2, x:x + 256], wk[b:b + 64, pair % 2, 0:256], ACT.Copy)\
                    .then_inc(at_hi, 1)

            for u in range(NU):
                probs(u)
                if u >= 2:
                    copy(u - 2)
                if u % 2 == 1 and u >= 5:
                    hi((u - 5) // 2)
            copy(NU - 2)
            copy(NU - 1)
            hi(NU // 2 - 2)
            hi(NU // 2 - 1)

        def dve_attn(dve, link):
            dve.wait_ge(s_rpb, 1)

            def scale(u):
                h, tt, s = u // 4, u % 4, s_sb[:, u % 3, :]
                dve.wait_ge(at_s, u + 1)
                if u >= 3:
                    dve.wait_ge(at_tr, u - 2)
                ins = dve.tensor_scalar(s[:, 0:CTX], acc[:, u % 2, 0:CTX], 0.125, None, ALU.mult)
                if tt >= 2:
                    j = 2 - 2 * (tt - 2)
                    for b in (0, 64):
                        ins = dve.scalar_tensor_tensor(
                            s[b:b + 64, CTX:T1], acc[b:b + 64, u % 2, CTX:T1], 0.125,
                            rpb[b:b + 64, h, j:j + 4, :].rearrange("p j k -> p (j k)"), ALU.mult, ALU.add)
                ins.then_inc(at_scaled, 1)
                dve.wait_ge(at_scaled, u + 1)
                m = 4 * (u % 3)
                dve.tensor_reduce(tiny[:, m:m + 1], s[:, 0:keys_of(u)], AX.X, ALU.max, negate=True).then_inc(at_max, 1)

            def norm(u):
                m = 4 * (u % 3)
                s = s_sb[:, u % 3, 0:keys_of(u)]
                dve.wait_ge(at_exp, u + 1)
                dve.reciprocal(tiny[:, m + 2:m + 3], tiny[:, m + 1:m + 2]).then_inc(at_rec, 1)
                dve.wait_ge(at_rec, u + 1)
                dve.tensor_scalar(s, s, tiny[:, m + 2:m + 3], None, ALU.mult).then_inc(at_p, 1)

            def lo(pair):
                dve.wait_ge(at_hi, pair + 1)
                h, x = pair // 2, (pair % 2) * CTX
                b = 64 * (h % 2)
                dve.tensor_tensor(H_lo[T1][b:b + 64, h // 2, x:x + 256], wk[b:b + 64, pair % 2, 0:256],
                                  H_hi[T1][b:b + 64, h // 2, x:x + 256].bitcast(F32), ALU.subtract).then_inc(at_lo, 1)

            for u in range(NU):
                scale(u)
                if u >= 1:
                    norm(u - 1)
                if u % 2 == 0 and u >= 6:
                    lo((u - 6) // 2)
                if u == 8:
                    dve_mod_rest(dve, link, 0)
            norm(NU - 1)
            lo(NU // 2 - 3)
            lo(NU // 2 - 2)
            lo(NU // 2 - 1)

        RH = 8
        NDEC, B1, B2 = 48, 56, 72
        rot_ready, rot_mul, rot_done = sem("rope_swapped"), sem("rope_products"), sem("rope_done")
        r_arg, r_exp, r_D = sem("decay_arg"), sem("decay_exp"), sem("decay_ready")
        r_s, r_pt, r_o, r_oc = sem("ret_scores"), sem("ret_weighted"), sem("ret_out_ready"), sem("ret_out_copied")
        r_mean, r_cent, r_sqd, r_var = sem("ret_sum"), sem("ret_centred"), sem("ret_square"), sem("ret_square_sum")
        r_root, r_nrm, r_mixed, r_hi, r_lo = sem("ret_root"), sem("ret_normed"), sem("ret_mixed"), sem("ret_hi"), sem("ret_lo")
        s_decay, s_dist = sem("decay_columns"), sem("distances_ready")

        def r_weights(h):
            b = 4 * (h % 2)
            return X[:, b:b + 4, 0:SEQ]

        def rope_items():
            return [rk[:, h, LAT:T1] for h in range(RH)] + [rq[:, h, :] for h in range(RH)]

        def pe_rope(pe, items, which, n, swap, base):
            for i in which:
                if base + i >= 2:
                    pe.wait_ge(rot_mul, base + i - 1)
                pe.matmul(wk[:, i % 2, 0:n], swap[:, :], items[i], start=True, stop=True).then_inc(rot_ready, 1)

        def dve_rope(dve, items, which, n, table, tmp, base):
            def add(i):
                dve.wait_ge(rot_mul, base + i + 1)
                dve.tensor_tensor(items[i], tmp[:, i % 2, 0, 0:n], tmp[:, i % 2, 1, 0:n], ALU.add).then_inc(rot_done, 1)
            for i in which:
                x = items[i]
                if i >= 2:
                    dve.wait_ge(rot_done, base + i - 1)
                dve.tensor_tensor(tmp[:, i % 2, 0, 0:n], x, table[:, 0, :], ALU.mult)
                dve.wait_ge(rot_ready, base + i + 1)
                dve.tensor_tensor(tmp[:, i % 2, 1, 0:n], wk[:, i % 2, 0:n], table[:, 1, :], ALU.mult).then_inc(rot_mul, 1)
                if i >= 1:
                    add(i - 1)
                if i == len(items) - 1:
                    add(i)

        def pe_ret(pe):
            def scores(h):
                if h == 0:
                    pe.wait_ge(rot_done, 2 * RH)
                    all_freed(pe, "ret_v")
                    all_freed(pe, "ret_g")
                if h >= 2:
                    pe.wait_ge(r_pt, h - 1)
                for kt in range(4):
                    mm = pe.matmul(acc[:, 2 * (h % 2) + kt // 2, (kt % 2) * 256:(kt % 2) * 256 + 256],
                                   rk[:, h, kt * P:(kt + 1) * P], rq[:, h, :], start=True, stop=True)
                mm.then_inc(r_s, 1)

            def values(h):
                pe.wait_ge(r_pt, h + 1)
                if h >= 2:
                    pe.wait_ge(r_oc, h - 1)
                for c in range(2):
                    for kt in range(4):
                        mm = pe.matmul(wk[:, h % 2, c * 256:(c + 1) * 256], rv[:, kt, h * 256 + c * P:h * 256 + (c + 1) * P],
                                       r_weights(h)[:, kt, :], start=kt == 0, stop=kt == 3)
                mm.then_inc(r_o, 1)

            def mean(h):
                pe.wait_ge(r_oc, h + 1)
                if h >= 1:
                    pe.wait_ge(r_cent, 2 * h)
                for c in range(2):
                    mm = pe.matmul(wk[:, 2, 0:256], ones[:, :], ro[:, h, c, :], start=c == 0, stop=c == 1)
                mm.then_inc(r_mean, 1)

            def variance(h):
                pe.wait_ge(r_sqd, h + 1)
                if h >= 1:
                    pe.wait_ge(r_root, h)
                for c in range(2):
                    mm = pe.matmul(wk[:, 3, 0:256], ones[:, :], r_sq[:, c, :], start=c == 0, stop=c == 1)
                mm.then_inc(r_var, 1)

            scores(0)
            for h in range(RH + 1):
                if h + 1 < RH:
                    scores(h + 1)
                if h >= 1:
                    mean(h - 1)
                if h < RH:
                    values(h)
                if h >= 1:
                    variance(h - 1)

        def act_ret(act):
            def decay(h):
                if h == 0:
                    act.wait_ge(s_decay, 5)
                if h >= 2:
                    act.wait_ge(r_pt, h - 1)
                if h >= 1:
                    act.wait_ge(r_D, 3 * h)
                d = r_dec[h % 2]
                for kt in range(2):
                    act.activation(d[:, kt, :], dist[:, :], ACT.Exp, scale=V("decay", h), bias=tiny[:, B1 + 8 * kt + h:B1 + 8 * kt + h + 1])
                    act.activation(r_e[:, kt, :], dist[:, :], ACT.Exp, scale=tiny[:, NDEC + h:NDEC + h + 1],
                                   bias=tiny[:, B2 + 8 * kt + h:B2 + 8 * kt + h + 1])
                act.wait_ge(r_arg, 2 * h + 2)
                act.activation(d[:, 2:4, :], d[:, 2:4, :], ACT.Exp).then_inc(r_exp, 1)

            def copy(h):
                act.wait_ge(r_o, h + 1)
                act.activation(ro[:, h, :, :], wk[:, h % 2, :].rearrange("p (c n) -> p c n", c=2), ACT.Copy).then_inc(r_oc, 1)

            def root_of(h):
                act.wait_ge(r_var, h + 1)
                if h >= 1:
                    act.wait_ge(r_nrm, 3 * h - 2)
                act.activation(r_rs[:, 0, :], wk[:, 3, 0:256], ACT.Sqrt, bias=V("eps"), scale=1.0 / 256).then_inc(r_root, 1)

            def square(h):
                act.wait_ge(r_cent, 2 * h + 2)
                if h >= 1:
                    act.wait_ge(r_var, h)
                act.activation(r_sq[:, :, :], ro[:, h, :, :], ACT.Square).then_inc(r_sqd, 1)

            def hi(h):
                act.wait_ge(r_mixed, 2 * h + 2)
                act.activation(H_hi[SEQ][:, 2 * h:2 * h + 2, :], r_mix[:, :, :], ACT.Copy).then_inc(r_hi, 1)

            decay(0)
            for h in range(RH + 2):
                if h + 1 < RH:
                    decay(h + 1)
                if 1 <= h <= RH:
                    square(h - 1)
                if h < RH:
                    copy(h)
                if 1 <= h <= RH:
                    root_of(h - 1)
                if h >= 2:
                    hi(h - 2)

        def pool_ret(pool):
            for h in range(RH):
                d = r_dec[h % 2]
                pool.wait_ge(r_exp, h + 1)
                pool.tensor_tensor(d[:, 0:2, :], d[:, 0:2, :], r_e[:, :, :], ALU.add).then_inc(r_D, 1)
                for kt in range(2):
                    x = d[:, 2 + kt, kt * P:(kt + 1) * P]
                    pool.tensor_tensor(x, x, ident[:, :], ALU.add).then_inc(r_D, 1)

        def dve_decays(dve):
            lg2 = V("decay", 8, 8)
            dve.tensor_scalar(tiny[:, NDEC:NDEC + 8], lg2, -1.0, None, ALU.mult).then_inc(s_decay, 1)
            for kt in range(2):
                b = 8 * kt
                dve.tensor_scalar(tiny[:, B1 + b:B1 + b + 8], V("decay", 0, 8), float(CTX - P * kt), None, ALU.mult)\
                    .then_inc(s_decay, 1)
                dve.tensor_scalar(tiny[:, B2 + b:B2 + b + 8], lg2, float(CTX + P * kt), None, ALU.mult).then_inc(s_decay, 1)
                dve.tensor_scalar(r_dist[:, 0, kt, :], dist[:, :], float(-P * kt), 0.0, ALU.add, ALU.max).then_inc(s_dist, 1)
                dve.tensor_scalar(r_dist[:, 1, kt, :], dist[:, :], float(-P * kt), 0.0, ALU.add, ALU.min).then_inc(s_dist, 1)

        def dve_ret(dve):
            def arg(h):
                d = r_dec[h % 2][:, 2:4, :]
                if h >= 2:
                    dve.wait_ge(r_pt, h - 1)
                dve.tensor_scalar(d, r_dist[:, 0, :, :], V("decay", h), None, ALU.mult).then_inc(r_arg, 1)
                dve.wait_ge(r_arg, 2 * h + 1)
                dve.scalar_tensor_tensor(d, r_dist[:, 1, :, :], tiny[:, NDEC + h:NDEC + h + 1], d, ALU.mult, ALU.add)\
                    .then_inc(r_arg, 1)

            dve.wait_ge(s_decay, 5)
            dve.wait_ge(s_dist, 4)

            def weights(h):
                dve.wait_ge(r_s, h + 1)
                dve.wait_ge(r_D, 3 * h + 3)
                if h >= 2:
                    dve.wait_ge(r_o, h - 1)
                b = 2 * (h % 2)
                dve.scalar_tensor_tensor(r_weights(h), acc[:, b:b + 2, :].rearrange("p b (k n) -> p (b k) n", k=2), P ** -0.5,
                                         r_dec[h % 2][:, :, :], ALU.mult, ALU.mult).then_inc(r_pt, 1)

            def centre(h):
                dve.wait_ge(r_mean, h + 1)
                for c in range(2):
                    dve.scalar_tensor_tensor(ro[:, h, c, :], wk[:, 2, 0:256], -1.0 / 256, ro[:, h, c, :], ALU.mult, ALU.add)\
                        .then_inc(r_cent, 1)

            def normed(h):
                dve.wait_ge(r_root, h + 1)
                dve.reciprocal(r_rs[:, 1, :], r_rs[:, 0, :]).then_inc(r_nrm, 1)
                dve.wait_ge(r_nrm, 3 * h + 1)
                for c in range(2):
                    dve.tensor_tensor(ro[:, h, c, :], ro[:, h, c, :], r_rs[:, 1, :], ALU.mult).then_inc(r_nrm, 1)
                if h == 0:
                    all_freed(dve, "ret_g")
                for c in range(2):
                    dve.wait_ge(r_nrm, 3 * h + 2 + c)
                    if h >= 1:
                        dve.wait_ge(r_lo, h)
                    dve.scalar_tensor_tensor(r_mix[:, c, :], ro[:, h, c, :], V("gn_g", 2 * h + c), rg[:, 2 * h + c, :],
                                             ALU.mult, ALU.mult).then_inc(r_mixed, 1)

            def lo(h):
                dve.wait_ge(r_hi, h + 1)
                dve.tensor_tensor(H_lo[SEQ][:, 2 * h:2 * h + 2, :], r_mix[:, :, :],
                                  H_hi[SEQ][:, 2 * h:2 * h + 2, :].bitcast(F32), ALU.subtract).then_inc(r_lo, 1)

            arg(0)
            for h in range(RH + 3):
                if h + 1 < RH:
                    arg(h + 1)
                if h < RH:
                    weights(h)
                if 1 <= h <= RH:
                    centre(h - 1)
                if h >= 3:
                    lo(h - 3)
                if 2 <= h < RH + 2:
                    normed(h - 2)

        mh_mul, mh_done = sem("mlp_products"), sem("mlp_hidden_done")

        def act_mlp_in(act, layer, half):
            p = proj[f"mlp{layer}_in{half}"]
            g0 = (2 * layer + half) * p.n

            def slot(st):
                split_hi(act, st)
                r = st.parity()
                for c in range(2):
                    act.wait_ge(acc_ready, st.tile(c))
                    if c == 0 and (st.i is not None or g0 + st.s >= 2):
                        act.wait_ge(mh_mul, 4 * st.s + 4 * (g0 - 1))
                    ins = act.activation(cgu[:, r, c, 0:T2], acc_tile(p, r, c), ACT.Relu)
                    if c == 1:
                        ins.then_inc(freed["act"], 1)
            each_slot(act, p, slot)

        def pool_mlp_in(pool, layer, half):
            p = proj[f"mlp{layer}_in{half}"]
            g0 = (2 * layer + half) * p.n

            def slot(st):
                r = st.parity()

                def part(F, c):
                    m = st.s * 2 + c
                    return F[T2][:, m, :] if st.i is None else F[T2][:, bass.ds(m, 1), :]
                pool.wait_ge(freed["act"], p.freed0 + st.s + 1)
                for c in range(2):
                    x = cgu[:, r, c, 0:T2]
                    pool.tensor_tensor(hid2[:, r, c, :], x, x, ALU.mult).then_inc(mh_mul, 1)
                    pool.tensor_tensor(part(F_hi, c), x, x, ALU.mult).then_inc(mh_mul, 1)
                pool.wait_ge(mh_mul, 4 * st.s + (4 * g0 + 4))
                for c in range(2):
                    pool.tensor_tensor(part(F_lo, c), hid2[:, r, c, :], part(F_hi, c).bitcast(F32), ALU.subtract)\
                        .then_inc(mh_done, 1)
            each_slot(pool, p, slot)

        def dve_add(dve, name, after=None, meanwhile={}):
            p = proj[name]

            def slot(st):
                split_lo(dve, st)
                if meanwhile:
                    meanwhile[st.s]()
                for c in range(p.C):
                    m = st.s * p.C + c
                    x = X[:, m, X2:T1] if st.i is None else X[:, bass.ds(m, 1), X2:T1]
                    dve.wait_ge(acc_ready, st.tile(c))
                    if after and c == 0:
                        dve.wait_ge(freed["dve"], proj[after].freed0 + st.s + 1)
                    ins = dve.tensor_tensor(x, acc_tile(p, st.parity(), c), x, ALU.add)
                    if c == p.C - 1:
                        ins.then_inc(freed["dve"], 1)
            each_slot(dve, p, slot)

        def act_mlp(act, layer):
            for half in range(2):
                act_mlp_in(act, layer, half)
                act_plain(act, f"mlp{layer}_out{half}")

        def dve_mlp(dve, layer):
            dve_plain(dve, f"mlp{layer}_in0")
            dve_add(dve, f"mlp{layer}_out0")
            dve_plain(dve, f"mlp{layer}_in1")
            dve_add(dve, f"mlp{layer}_out1", after=f"mlp{layer}_out0")

        def pe_mlp(pe, layer, j):
            for half in range(2):
                g0 = (2 * layer + half) * MLH
                project(pe, f"mlp{layer}_in{half}", lambda k: H_hi[T2][:, k, :], lambda k: H_lo[T2][:, k, :],
                        need=h_need(pe, j) if half == 0 else None)
                project(pe, f"mlp{layer}_out{half}", lambda k: F_hi[T2][:, k, :], lambda k: F_lo[T2][:, k, :],
                        need=lambda k: pe.wait_ge(mh_done, g0 + k + 1))

        def load_second(pool):
            pool.wait_ge(h_ready, 4 * DC)
            pool.dma_start(X[:, :, X2:LAT], t["meta"]).then_inc(s_meta, 16)
            pool.dma_start(lru_w[:, 0, :, :], t["lru_wr"]).then_inc(s_meta, 16)
            pool.dma_start(lru_w[:, 1, :, :], t["lru_wi"]).then_inc(s_meta, 16)
            pool.dma_start(c_mask[:, :, :], t["c_mask"]).then_inc(s_meta, 16)

        (G_I, G_F, G_ABS, G_Z, G_Y, G_Y2, G_Q, G_LF, G_CUM, G_A, G_G, G_M) = range(12)
        LRU_ABS, LRU_Z, LRU_Y, LRU_Y2, LRU_Q, LRU_POS, LRU_NEG, LRU_T = range(0, 64, 8)
        AT = 64
        s_if, s_gabs, s_gz, s_gate = sem("if_ready"), sem("gate_abs"), sem("gate_exp"), sem("gates_ready")
        s_aT, s_aTc, s_vt, s_vtc = sem("a_transposed"), sem("a_copied"), sem("v_transposed"), sem("v_copied")

        def half_log1p(dve, link, z, y, y2, q):
            half_log1p_start(dve, link, z, y, y2, q)
            half_log1p_terms(dve, link, y, y2, q, range(17, 2, -2))

        def half_log1p_start(dve, link, z, y, y2, q):
            link(dve.tensor_scalar(y, z, 2.0, None, ALU.add))
            link(dve.reciprocal(y, y))
            link(dve.tensor_tensor(y, y, z, ALU.mult))
            link(dve.tensor_tensor(y2, y, y, ALU.mult))
            link(dve.tensor_scalar(q, y2, 1.0 / 19, None, ALU.mult))

        def half_log1p_terms(dve, link, y, y2, q, terms):
            for k in terms:
                link(dve.scalar_tensor_tensor(q, q, 1.0 / k, y2, ALU.add, ALU.mult))
            if terms[-1] == 3:
                link(dve.scalar_tensor_tensor(q, q, 1.0, y, ALU.add, ALU.mult))

        def act_gates(act):
            lam = V("lru_lam", 0, 8)
            act.wait_ge(s_if, 1)
            act.activation(IF[0:4, G_ABS, :], IF[0:4, G_F, :], ACT.Abs).then_inc(s_gabs, 1)
            act.activation(tiny[:, LRU_ABS:LRU_ABS + 8], lam, ACT.Abs).then_inc(s_gabs, 1)
            act.wait_ge(s_gabs, 2)
            act.activation(IF[0:4, G_Z, :], IF[0:4, G_ABS, :], ACT.Exp, scale=-1.0).then_inc(s_gz, 1)
            act.activation(tiny[:, LRU_Z:LRU_Z + 8], tiny[:, LRU_ABS:LRU_ABS + 8], ACT.Exp, scale=-1.0).then_inc(s_gz, 1)

        def dve_gates(dve, link):
            p = proj["ab_if"]
            st = Step(p, None, 0)
            split_lo(dve, st)
            for c in range(2):
                dve.wait_ge(acc_ready, st.tile(c))
                link(dve.tensor_scalar(IF[0:4, c, :], acc_tile(p, st.parity(), c)[0:4], vec[0:4, VEC["if_bias"] + c:VEC["if_bias"] + c + 1],
                                       None, ALU.add))
            dve.tensor_copy(IF[0:4, G_LF, :], IF[0:4, G_F, :]).then_inc(freed["dve"], 1)
            link(dve.tensor_copy(IF[0:4, G_M, :], IF[0:4, G_I, :]))
            dve.tensor_copy(tiny[0:4, AT + 12:AT + 13], IF[0:4, G_F, 0:1]).then_inc(s_if, 1)

        def dve_gate_logs(dve, link, s):
            z, y, y2, q = (IF[0:4, i, :] for i in (G_Z, G_Y, G_Y2, G_Q))
            if s == 0:
                dve.wait_ge(s_gz, 2)
                half_log1p_start(dve, link, z, y, y2, q)
            else:
                half_log1p_terms(dve, link, y, y2, q, (None, (17, 15, 13), (11, 9, 7), (5, 3))[s])

        def dve_gate_sums(dve, link, s):
            def row(i):
                return IF[0:4, i, :]
            if s == 0:
                link(dve.tensor_scalar(row(G_LF), row(G_F), 0.0, None, ALU.min))
                link(dve.scalar_tensor_tensor(row(G_LF), row(G_Q), -2.0, row(G_LF), ALU.mult, ALU.add))
            if s == 1:
                link(dve.tensor_tensor_scan(row(G_CUM), one_row[0:4, :], row(G_LF), 0.0, ALU.mult, ALU.add))
                link(dve.tensor_tensor(row(G_A), row(G_I), row(G_CUM), ALU.subtract))
            if s == 2:
                link(dve.tensor_tensor_scan(row(G_G), one_row[0:4, :], row(G_A), 0.0, ALU.mult, ALU.max))
                dve.tensor_tensor(row(G_M), row(G_G), row(G_CUM), ALU.add).then_inc(s_gate, 1)

        def dve_lru_rate(dve, link):
            def col(i):
                return tiny[:, i:i + 8]
            half_log1p(dve, link, col(LRU_Z), col(LRU_Y), col(LRU_Y2), col(LRU_Q))
            link(dve.tensor_scalar(col(LRU_T), V("lru_lam", 0, 8), -1.0, 0.0, ALU.mult, ALU.max))
            link(dve.scalar_tensor_tensor(col(LRU_T), col(LRU_Q), 2.0, col(LRU_T), ALU.mult, ALU.add))
            dve.tensor_scalar(col(LRU_POS), col(LRU_T), 8.0, None, ALU.mult)
            dve.tensor_scalar(col(LRU_NEG), col(LRU_T), -8.0, None, ALU.mult).then_inc(s_gate, 1)

        def dve_gate_columns(dve):
            dve.wait_ge(s_aT, 1)
            dve.tensor_copy(tiny[:, AT:AT + 8], wk[:, 0, 0:8]).then_inc(s_aTc, 1)
            dve.tensor_copy(tiny[0:16, AT + 8:AT + 12], wk[0:16, 0, 8:12]).then_inc(s_aTc, 1)

        def pe_turn_values(pe, vF, g0, banks, turns, which=range(6)):
            for i in which:
                (t0, n), half = TILES2[i // 2], i % 2
                if i >= turns:
                    pe.wait_ge(s_vtc, g0 + i + 1 - turns)
                for c in range(4):
                    mm = pe.transpose(banks[0:n, 4 - turns + i % turns, c * P:(c + 1) * P], vF[:, 4 * half + c, t0:t0 + n], ident[:, :])
                mm.then_inc(s_vt, 1)

        def act_turn_values(act, vT, g0, banks, turns, which=range(6)):
            for i in which:
                (t0, n), half = TILES2[i // 2], i % 2
                act.wait_ge(s_vt, g0 + i + 1)
                act.activation(vT[0:n, i // 2, half * 512:half * 512 + 512], banks[0:n, 4 - turns + i % turns, :],
                               ACT.Copy).then_inc(s_vtc, 1)

        MH = 4
        m_b, m_s, m_D, m_mask = sem("mlstm_broadcast"), sem("mlstm_scores"), sem("mlstm_decay"), sem("mlstm_masked")
        m_pt, m_num, m_e, m_r = sem("mlstm_weighted"), sem("mlstm_sums"), sem("mlstm_bounds"), sem("mlstm_divisor")
        m_hh, m_sq, m_var, m_root = sem("mlstm_h"), sem("mlstm_square"), sem("mlstm_square_sum"), sem("mlstm_root")
        m_out, m_hi, m_lo = sem("mlstm_out"), sem("mlstm_hi"), sem("mlstm_lo")

        def pe_mlstm(pe):
            pe.wait_ge(s_gate, 2)
            for st, (t0, n) in enumerate(TILES2):
                mm = pe.transpose(wk[0:n, 0, 4 * st:4 * st + 4], IF[0:4, G_A, t0:t0 + n], ident[0:4, 0:4])
            mm.then_inc(s_aT, 1)
            for name in ("ab_qk", "ab_v", "ab_o", "ab_xb", "ab_gate"):
                all_freed(pe, name)
            pe.wait_ge(s_vtc, 6)
            pe.wait_ge(s_aTc, 2)
            for h in range(MH):
                if h >= 1:
                    pe.wait_ge(m_e, 2 * h)
                    pe.wait_ge(m_D, 3 * h)
                pe.matmul(wk[:, 0, 0:T2], head_sel[0:4, h, :], IF[0:4, G_G, :], start=True, stop=True)
                pe.matmul(wk[:, 1, 0:T2], head_sel[0:4, h, :], IF[0:4, G_M, :], start=True, stop=True).then_inc(m_b, 1)
                for st, (t0, n) in enumerate(TILES2):
                    if h >= 1:
                        pe.wait_ge(m_pt, 3 * (h - 1) + st + 1)
                    for c in range(2):
                        mm = pe.matmul(acc[0:n, st, t0:T2], qk[:, 8 + 2 * h + c, t0:t0 + n], qk[:, 2 * h + c, t0:T2],
                                       start=c == 0, stop=c == 1)
                    mm.then_inc(m_s, 1)
                if h >= 1:
                    pe.wait_ge(m_root, h)
                    pe.wait_ge(m_hh, 4 * h)
                for st, (t0, n) in enumerate(TILES2):
                    pe.wait_ge(m_pt, 3 * h + st + 1)
                    pe.matmul(acc[:, 3, t0:T2], ones[0:n, :], m_P[0:n, st, t0:T2], start=st == 0, stop=st == 2)
                for c in range(2):
                    for st, (t0, n) in enumerate(TILES2):
                        mm = pe.matmul(wk[:, 2 + c, t0:T2], vT[0:n, st, h * 256 + c * P:h * 256 + (c + 1) * P],
                                       m_P[0:n, st, t0:T2], start=st == 0, stop=st == 2)
                mm.then_inc(m_num, 1)
                pe.wait_ge(m_sq, h + 1)
                pe.wait_ge(m_e, 2 * h + 2)
                for c in range(2):
                    mm = pe.matmul(acc[:, 3, 0:T2], ones[:, :], m_sqr[:, c, :], start=c == 0, stop=c == 1)
                mm.then_inc(m_var, 1)

        def act_mlstm(act):
            act.wait_ge(s_aTc, 2)
            for h in range(MH):
                act.wait_ge(m_b, h + 1)
                for st, (t0, n) in enumerate(TILES2):
                    if h >= 1:
                        act.wait_ge(m_pt, 3 * (h - 1) + st + 1)
                    act.activation(m_Dk[0:n, st, t0:T2], wk[0:n, 0, t0:T2], ACT.Exp, scale=-1.0,
                                   bias=tiny[0:n, AT + 4 * st + h:AT + 4 * st + h + 1]).then_inc(m_D, 1)
                if h >= 1:
                    act.wait_ge(m_r, 2 * h)
                act.activation(m_E[:, :], wk[:, 1, 0:T2], ACT.Exp, scale=-1.0).then_inc(m_e, 1)
                act.wait_ge(m_num, h + 1)
                act.activation(m_ad[:, :], acc[:, 3, 0:T2], ACT.Abs).then_inc(m_e, 1)
                act.wait_ge(m_hh, 4 * h + 4)
                act.activation(m_sqr[:, :, :], m_h[:, :, :], ACT.Square).then_inc(m_sq, 1)
                act.wait_ge(m_var, h + 1)
                act.activation(m_rt[:, 0, :], acc[:, 3, 0:T2], ACT.Sqrt, bias=V("eps"), scale=1.0 / 256).then_inc(m_root, 1)
                act.wait_ge(m_out, 2 * h + 2)
                act.activation(H_hi[T2][:, 2 * h:2 * h + 2, :], m_h[:, :, :], ACT.Copy).then_inc(m_hi, 1)

        def pool_mlstm(pool):
            for h in range(MH):
                for st, (t0, n) in enumerate(TILES2):
                    pool.wait_ge(m_D, 3 * h + st + 1)
                    x = m_Dk[0:n, st, t0:t0 + n]
                    pool.affine_select(out=x, in_=x, compare_op=ALU.is_ge, fill=0.0, base=0, pattern=[[1, n]],
                                       channel_multiplier=-1).then_inc(m_mask, 1)

        def dve_mlstm(dve, link):
            for h in range(MH):
                for st, (t0, n) in enumerate(TILES2):
                    dve.wait_ge(m_s, 3 * h + st + 1)
                    dve.wait_ge(m_mask, 3 * h + st + 1)
                    if h >= 1:
                        dve.wait_ge(m_num, h)
                    dve.scalar_tensor_tensor(m_P[0:n, st, t0:T2], acc[0:n, st, t0:T2], 1.0 / 16, m_Dk[0:n, st, t0:T2],
                                             ALU.mult, ALU.mult).then_inc(m_pt, 1)
                lru_conv(dve, h)
                dve.wait_ge(m_e, 2 * h + 2)
                dve.tensor_tensor(m_ad[:, :], m_ad[:, :], m_E[:, :], ALU.max).then_inc(m_r, 1)
                dve.wait_ge(m_r, 2 * h + 1)
                if h == 0:
                    all_freed(dve, "ab_o")
                dve.reciprocal(m_ad[:, :], m_ad[:, :]).then_inc(m_r, 1)
                dve.wait_ge(m_r, 2 * h + 2)
                for c in range(2):
                    dve.tensor_tensor(m_h[:, c, :], wk[:, 2 + c, 0:T2], m_ad[:, :], ALU.mult).then_inc(m_hh, 1)
                for c in range(2):
                    dve.wait_ge(m_hh, 4 * h + c + 1)
                    dve.tensor_tensor(m_h[:, c, :], m_h[:, c, :], og[:, 2 * h + c, :], ALU.mult).then_inc(m_hh, 1)
                dve.wait_ge(m_root, h + 1)
                link(dve.reciprocal(m_rt[:, 1, :], m_rt[:, 0, :]))
                dve.wait_ge(m_hh, 4 * h + 4)
                for c in range(2):
                    dve.scalar_tensor_tensor(m_h[:, c, :], m_h[:, c, :], V("mlstm_norm", 2 * h + c), m_rt[:, 1, :],
                                             ALU.mult, ALU.mult).then_inc(m_out, 1)
                dve.wait_ge(m_hi, h + 1)
                dve.tensor_tensor(H_lo[T2][:, 2 * h:2 * h + 2, :], m_h[:, :, :], H_hi[T2][:, 2 * h:2 * h + 2, :].bitcast(F32),
                                  ALU.subtract).then_inc(m_lo, 1)
                if h + 1 < MH:
                    dve.wait_ge(m_lo, h + 1)

        l_conv, l_gate, l_act, l_tanh, l_dec = sem("lru_conv"), sem("lru_gate_sums"), sem("lru_gates"), sem("lru_tanh"), sem("lru_decay")
        l_arg, l_root, l_h, l_hi, l_lo = sem("lru_root_arg"), sem("lru_root"), sem("lru_out"), sem("lru_hi"), sem("lru_lo")
        l_in = sem("lru_input")
        R, I, XC, TT = qk[:, 0:8, :], qk[:, 8:16, :], vF, l_t

        def pe_lru(pe):
            for i in range(16):
                c, which = i // 2, i % 2
                pe.wait_ge(l_conv, 25 + c)
                if i >= 3:
                    pe.wait_ge(l_act, i - 2)
                pe.matmul(acc[:, i % 3, 0:T2], lru_w[:, which, c, :], XC[:, c, :], start=True, stop=True).then_inc(l_gate, 1)

        def act_lru(act):
            for i in range(16):
                c, which = i // 2, i % 2
                act.wait_ge(l_gate, i + 1)
                act.activation((R, I)[which][:, c, :], acc[:, i % 3, 0:T2], ACT.Sigmoid,
                               bias=V("lru_b_i" if which else "lru_b_r", c)).then_inc(l_act, 1)

            def tanhs():
                act.wait_ge(l_act, 16)
                for c in range(8):
                    act.activation(TT[:, c, :], R[:, c, :], ACT.Tanh, scale=tiny[:, LRU_POS + c:LRU_POS + c + 1]).then_inc(l_tanh, 1)

            def decays():
                for c in range(8):
                    act.activation(R[:, c, :], R[:, c, :], ACT.Exp, scale=tiny[:, LRU_NEG + c:LRU_NEG + c + 1]).then_inc(l_dec, 1)

            def roots():
                act.wait_ge(l_arg, 1)
                act.activation(TT[:, :, :], TT[:, :, :], ACT.Sqrt, scale=2.0).then_inc(l_root, 1)

            act_plain(act, "ab_out0", meanwhile={0: tanhs, 1: decays, 2: roots, 3: lambda: None})
            act.wait_ge(l_h, 9)
            act.activation(H_hi[T2][:, 8:16, :], XC[:, :, :], ACT.Copy).then_inc(l_hi, 1)

        def lru_conv(dve, j):
            if j == 0:
                all_freed(dve, "ab_xb")
                dve.wait_ge(s_vt, 6)
            for c in range(8):
                if j == 0:
                    dve.tensor_scalar(XC[:, c, :], xb[:, c, :], V("lru_conv_w", 24 + c), V("lru_conv_b", c), ALU.mult, ALU.add)\
                        .then_inc(l_conv, 1)
                else:
                    dve.wait_ge(l_conv, 8 * (j - 1) + c + 1)
                    dve.scalar_tensor_tensor(XC[:, c, j:T2], xb[:, c, 0:T2 - j], V("lru_conv_w", 8 * (3 - j) + c),
                                             XC[:, c, j:T2], ALU.mult, ALU.add).then_inc(l_conv, 1)

        def dve_lru(dve, link):
            def inputs():
                dve.wait_ge(l_act, 16)
                dve.wait_ge(l_conv, 32)
                dve.tensor_tensor(I[:, :, :], I[:, :, :], XC[:, :, :], ALU.mult).then_inc(l_in, 1)
                dve.wait_ge(l_tanh, 8)
                link(dve.tensor_scalar(xb[:, :, :], TT[:, :, :], 1.0, None, ALU.add))
                link(dve.reciprocal(xb[:, :, :], xb[:, :, :]))
                dve.tensor_tensor(TT[:, :, :], TT[:, :, :], xb[:, :, :], ALU.mult).then_inc(l_arg, 1)

            def scan(chunks):
                for c in chunks:
                    dve.tensor_tensor_scan(XC[:, c, :], R[:, c, :], I[:, c, :], 0.0, ALU.mult, ALU.add).then_inc(l_h, 1)

            def scaled():
                dve.wait_ge(l_root, 1)
                dve.wait_ge(l_in, 1)
                link(dve.tensor_tensor(I[:, :, :], I[:, :, :], TT[:, :, :], ALU.mult))
                dve.wait_ge(l_dec, 8)
                scan(range(4))

            def gated():
                scan(range(4, 8))
                all_freed(dve, "ab_gate")
                dve.wait_ge(l_h, 8)
                dve.tensor_tensor(XC[:, :, :], XC[:, :, :], gate[:, :, :], ALU.mult).then_inc(l_h, 1)

            dve_add(dve, "ab_out0", meanwhile={0: inputs, 1: lambda: None, 2: scaled, 3: gated})
            dve.wait_ge(l_hi, 1)
            dve.tensor_tensor(H_lo[T2][:, 8:16, :], XC[:, :, :], H_hi[T2][:, 8:16, :].bitcast(F32), ALU.subtract).then_inc(l_lo, 1)

        CH = 8
        LAMBDA_INIT = 0.8 - 0.6 * math.exp(-0.3 * 1)
        CU = 3 * CH
        C_SUM, C_NLAM, C_GAIN, C_MAX = 64, 68, 69, 0
        c_s, c_scaled, c_max, c_exp = sem("diff_scores"), sem("diff_scaled"), sem("diff_max"), sem("diff_exp")
        c_rec, c_p, c_tr, c_pt, c_o = sem("diff_recip"), sem("diff_probs"), sem("diff_transposed"), sem("diff_probsT"), sem("diff_out")
        c_sq, c_var, c_root, c_fin = sem("diff_square"), sem("diff_square_sum"), sem("diff_root"), sem("diff_normed")
        c_hi, c_lo, c_lam = sem("diff_hi"), sem("diff_lo"), sem("diff_lambda")

        def unit(w):
            h, qt = w // 3, w % 3
            t0, n = TILES2[qt]
            return h, qt, t0, n, t0 + n

        def c_items():
            return [cq[:, h, :] for h in range(CH)] + [ck[:, h, :] for h in range(CH)]

        def pe_diff(pe):
            all_freed(pe, "c_v")
            pe_turn_values(pe, cvF, 6, acc, 4)
            pe.wait_ge(s_vtc, 12)
            pe.wait_ge(rot_done, 32)

            def scores(w):
                h, qt, t0, n, keys = unit(w)
                if w >= 2:
                    pe.wait_ge(c_scaled, w - 1)
                for m in range(2):
                    b = 64 * m
                    mm = pe.matmul(acc[0:n, 2 * (w % 2) + m, 0:keys], cq[b:b + 64, h, t0:t0 + n], ck[b:b + 64, h, 0:keys],
                                   start=True, stop=True)
                mm.then_inc(c_s, 1)

            def turn(w):
                h, qt, t0, n, keys = unit(w)
                pe.wait_ge(c_p, w + 1)
                if w >= 2:
                    pe.wait_ge(c_pt, w - 1)
                for kt in range(qt + 1):
                    k0, kn = TILES2[kt]
                    mm = pe.transpose(wk[0:kn, w % 2, kt * P:kt * P + n], c_sb[0:n, w % 3, 0, k0:k0 + kn], ident[0:n, 0:n])
                mm.then_inc(c_tr, 1)

            def values(h):
                pe.wait_ge(c_pt, 3 * h + 3)
                if h >= 2:
                    pe.wait_ge(c_root, h - 1)
                for kt, (k0, kn) in enumerate(TILES2):
                    mm = pe.matmul(wk[:, 2 + h % 2, k0:T2], cvT[0:kn, kt, h * P:(h + 1) * P], cP[0:kn, h % 2, kt, k0:T2],
                                   start=kt == 0, stop=kt == 2)
                mm.then_inc(c_o, 1)

            def total(h):
                pe.wait_ge(c_sq, 2 * h + 2)
                pe.matmul(wk[:, 2 + h % 2, 0:T2], ones[:, :], csq[:, h % 2, :], start=True, stop=True).then_inc(c_var, 1)

            scores(0)
            scores(1)
            for w in range(CU + 5):
                if w + 2 < CU:
                    scores(w + 2)
                if w < CU:
                    turn(w)
                if w % 3 == 2 and w >= 5:
                    values((w - 5) // 3)
                if w % 3 == 1 and w >= 7:
                    total((w - 7) // 3)

        def act_diff(act):
            act.wait_ge(c_lam, 2)
            act.activation(tiny[:, C_SUM:C_SUM + 2], tiny[:, C_SUM:C_SUM + 2], ACT.Exp).then_inc(c_lam, 1)
            act_turn_values(act, cvT, 6, acc, 4)

            def probs(w):
                h, qt, t0, n, keys = unit(w)
                act.wait_ge(c_max, w + 1)
                if w >= 3:
                    act.wait_ge(c_p, w - 2)
                o = C_MAX + 8 * (w % 3)
                for m in range(2):
                    s = c_sb[0:n, w % 3, m, 0:keys]
                    ins = act.activation(s, s, ACT.Exp, bias=tiny[0:n, o + m:o + m + 1], accum_out=tiny[0:n, o + 2 + m:o + 3 + m])
                ins.then_inc(c_exp, 1)

            def copy(w):
                h, qt, t0, n, keys = unit(w)
                act.wait_ge(c_tr, w + 1)
                if h >= 2:
                    act.wait_ge(c_o, h - 1)
                m = min(qt + 1, 2)
                ins = act.activation(cP[:, h % 2, 0:m, t0:t0 + n],
                                     wk[:, w % 2, 0:2 * P].rearrange("p (k q) -> p k q", q=P)[:, 0:m, 0:n], ACT.Copy)
                if qt == 2:
                    ins = act.activation(cP[0:16, h % 2, 2, t0:t0 + n], wk[0:16, w % 2, 2 * P:2 * P + n], ACT.Copy)
                ins.then_inc(c_pt, 1)

            def square(h):
                act.wait_ge(c_o, h + 1)
                if h >= 2:
                    act.wait_ge(c_lo, h - 1)
                act.activation(co[:, h % 2, :], wk[:, 2 + h % 2, 0:T2], ACT.Copy).then_inc(c_sq, 1)
                act.activation(csq[:, h % 2, :], wk[:, 2 + h % 2, 0:T2], ACT.Square).then_inc(c_sq, 1)

            def root_of(h):
                act.wait_ge(c_var, h + 1)
                if h >= 1:
                    act.wait_ge(c_fin, 2 * h)
                act.activation(crt[:, 0, :], wk[:, 2 + h % 2, 0:T2], ACT.Sqrt, bias=V("eps"), scale=1.0 / P).then_inc(c_root, 1)

            def hi(h):
                act.wait_ge(c_fin, 2 * h + 2)
                act.activation(H_hi[T2][:, h, :], co[:, h % 2, :], ACT.Copy).then_inc(c_hi, 1)

            for w in range(CU + 7):
                if w < CU:
                    probs(w)
                if 2 <= w < CU + 2:
                    copy(w - 2)
                if w % 3 == 0 and 6 <= w < CU + 6:
                    square((w - 6) // 3)
                if w % 3 == 2 and w >= 8:
                    root_of((w - 8) // 3)
                if w % 3 == 0 and w >= 9:
                    hi((w - 9) // 3)

        def dve_diff(dve, link):
            lam = V("lambda", 0, 256).rearrange("p (a b d) -> p a b d", a=2, b=2)
            link(dve.tensor_tensor(csq[:, 0, 0:128].rearrange("p (a d) -> p a d", a=2), lam[:, :, 0, :], lam[:, :, 1, :], ALU.mult))
            for i in range(2):
                dve.tensor_reduce(tiny[:, C_SUM + i:C_SUM + i + 1], csq[:, 0, 64 * i:64 * i + 64], AX.X, ALU.add).then_inc(c_lam, 1)
            dve.wait_ge(c_lam, 3)
            link(dve.tensor_tensor(tiny[:, C_NLAM:C_NLAM + 1], tiny[:, C_SUM + 1:C_SUM + 2], tiny[:, C_SUM:C_SUM + 1], ALU.subtract))
            link(dve.tensor_scalar(tiny[:, C_NLAM:C_NLAM + 1], tiny[:, C_NLAM:C_NLAM + 1], -LAMBDA_INIT, None, ALU.add))
            link(dve.tensor_scalar(tiny[:, C_GAIN:C_GAIN + 1], V("subln"), 1.0 - LAMBDA_INIT, None, ALU.mult))

            def scale(w):
                h, qt, t0, n, keys = unit(w)
                dve.wait_ge(c_s, w + 1)
                if w >= 3:
                    dve.wait_ge(c_tr, w - 2)
                s = c_sb[0:n, w % 3, :, 0:keys]
                mask = c_mask[0:n, qt:qt + 1, 0:keys].to_broadcast([n, 2, keys])
                b = 2 * (w % 2)
                dve.scalar_tensor_tensor(s, acc[0:n, b:b + 2, 0:keys], 0.125, mask, ALU.mult, ALU.add).then_inc(c_scaled, 1)
                dve.wait_ge(c_scaled, w + 1)
                o = C_MAX + 8 * (w % 3)
                dve.tensor_reduce(tiny[0:n, o:o + 2], s, AX.X, ALU.max, negate=True).then_inc(c_max, 1)

            def norm(w):
                h, qt, t0, n, keys = unit(w)
                o = C_MAX + 8 * (w % 3)
                dve.wait_ge(c_exp, w + 1)
                dve.reciprocal(tiny[0:n, o + 4:o + 6], tiny[0:n, o + 2:o + 4]).then_inc(c_rec, 1)
                dve.wait_ge(c_rec, 2 * w + 1)
                s = c_sb[0:n, w % 3, :, 0:keys]
                dve.tensor_scalar(s[:, 1, :], s[:, 1, :], tiny[0:n, o + 5:o + 6], tiny[0:n, C_NLAM:C_NLAM + 1], ALU.mult, ALU.mult)\
                    .then_inc(c_rec, 1)
                dve.wait_ge(c_rec, 2 * w + 2)
                dve.scalar_tensor_tensor(s[:, 0, :], s[:, 0, :], tiny[0:n, o + 4:o + 5], s[:, 1, :], ALU.mult, ALU.add)\
                    .then_inc(c_p, 1)

            def finish(h):
                dve.wait_ge(c_root, h + 1)
                dve.reciprocal(crt[:, 1, :], crt[:, 0, :]).then_inc(c_fin, 1)
                dve.wait_ge(c_fin, 2 * h + 1)
                dve.scalar_tensor_tensor(co[:, h % 2, :], co[:, h % 2, :], tiny[:, C_GAIN:C_GAIN + 1], crt[:, 1, :],
                                         ALU.mult, ALU.mult).then_inc(c_fin, 1)

            def lo(h):
                dve.wait_ge(c_hi, h + 1)
                dve.tensor_tensor(H_lo[T2][:, h, :], co[:, h % 2, :], H_hi[T2][:, h, :].bitcast(F32), ALU.subtract).then_inc(c_lo, 1)

            for w in range(CU + 8):
                if w < CU:
                    scale(w)
                if 1 <= w <= CU:
                    norm(w - 1)
                if w % 3 == 0 and w >= 9:
                    finish((w - 9) // 3)
                if w % 3 == 1 and w >= 10:
                    lo((w - 10) // 3)

        def act_ffn(act, layer, r):
            act_ffn_in(act, layer, 0)
            act_plain(act, ffn_name(layer, 0, "out"))
            act_ffn_in(act, layer, 1)
            act_y_squares(act, ffn_name(layer, 1, "out"), r)
            act_residual(act, r)

        def dve_ffn(dve, layer, r):
            dve_ffn_in(dve, layer, 0)
            dve_y(dve, ffn_name(layer, 0, "out"))
            dve_ffn_in(dve, layer, 1)
            dve_y(dve, ffn_name(layer, 1, "out"), add=ffn_name(layer, 0, "out"))
            dve_residual(dve, r)

        def pool_ffn(pool, layer, r):
            pool_ffn_in(pool, layer, 0)
            pool_ffn_in(pool, layer, 1)
            pool_y_sum(pool, r)

        def pe_ffn_halves(pe, layer, j):
            pe_ffn(pe, layer, 0, j)
            pe_ffn(pe, layer, 1, j)
            if layer == 0:
                pe_ada_ring(pe, 76, 80)
            pe_residual(pe, j)


        def store_out(sp):
            for c in range(DC):
                sp.wait_ge(n32_ready, DC * FINAL + c + 1)
                sp.dma_start(out[:, c, :], n32[:, c % 2, META:T2]).then_inc(s_out[c % 2], 16)
            for s in s_out:
                sp.wait_ge(s, 16 * DC // 2)

        TURNS = ((0, 1), (2, 3), (4,), (5,))
        block = ctx.enter_context(nc.Block())

        @block.sync
        def _(sp):
            load_ada_first(sp)
            stream_weights(sp)
            store_out(sp)

        @block.scalar
        def _(act):
            load_constants(act)
            act_c(act)
            act_norm(act, 0, meanwhile=lambda: split_first(act))
            act_rpb(act, 0, 3)
            act_gelu(act, "hyb_g", g_sb)
            act_rpb(act, 3, 6)
            act_gelu(act, "hyb_u", u_sb)
            for name in ("hyb_v", "hyb_k", "hyb_q"):
                act_plain(act, name)
            act_sgu(act)
            act_attn(act)
            act_y_squares(act, "hyb_out", 0)
            act_residual(act, 0)
            act_norm(act, 1)
            act_ffn(act, 0, 1)
            act_norm(act, 2)
            for name in ("ret_k", "ret_v", "ret_q"):
                act_plain(act, name)
            act_gelu(act, "ret_g", rg, ACT.Silu)
            act_ret(act)
            act_y_squares(act, "ret_out", 2)
            act_residual(act, 2)
            act_norm(act, 3)
            act_ffn(act, 1, 3)
            act_norm(act, 4)
            act_plain(act, "ab_if")
            act_gates(act)
            act_plain(act, "ab_qk")
            act_plain(act, "ab_v")
            act_gelu(act, "ab_o", og, ACT.Sigmoid, after=lambda s: act_turn_values(act, vT, 0, wk, 2, TURNS[s]))
            act_plain(act, "ab_xb")
            act_gelu(act, "ab_gate", gate)
            act_mlstm(act)
            act_lru(act)
            act_plain(act, "ab_out1")
            act_norm(act, 5)
            act_mlp(act, 0)
            act_norm(act, 6)
            for name in ("c_q", "c_k", "c_v"):
                act_plain(act, name)
            act_diff(act)
            act_plain(act, "c_out")
            act_norm(act, 7)
            act_mlp(act, 1)
            act_norm(act, 8)

        @block.vector
        def _(dve):
            link = chain(dve, "dve")
            dve_norm(dve, 0, meanwhile=lambda: (split_first(dve), [dve_ada(dve, j) for j in range(4)], dve_mod_first(dve, link)))
            dve_plain(dve, "hyb_g", after=lambda s: dve_ada(dve, 4) if s == 1 else None)
            dve_plain(dve, "hyb_u", after=lambda s: dve_ada(dve, 5 + s))
            dve_copy_tokens(dve, "hyb_v", v_sb, after=lambda s: dve_ada(dve, 7 + s))
            dve_copy(dve, "hyb_k", k_sb, after=lambda s: dve_ada(dve, 9 + s))
            dve_copy(dve, "hyb_q", q_sb, after=lambda s: dve_ada(dve, 11) if s == 0 else None)
            dve_sgu(dve, link)
            dve_attn(dve, link)
            dve_y(dve, "hyb_out")
            dve_residual(dve, 0)
            dve_norm(dve, 1)
            dve_ffn(dve, 0, 1)
            dve_norm(dve, 2, meanwhile=lambda: dve_mod_rest(dve, link, 1))
            dve_copy(dve, "ret_k", rk)
            dve_copy_tokens(dve, "ret_v", rv, after=lambda s: dve_rope(dve, rope_items(), [s], SEQ, rope_ret, r_rope, 0))
            dve_decays(dve)
            dve_copy(dve, "ret_q", rq)
            dve_plain(dve, "ret_g", after=lambda s: dve_rope(dve, rope_items(), [RH + s], SEQ, rope_ret, r_rope, 0))
            dve_ret(dve)
            dve_y(dve, "ret_out")
            dve_residual(dve, 2)
            dve_norm(dve, 3)
            dve_ffn(dve, 1, 3)
            dve_norm(dve, 4)
            dve_gates(dve, link)
            dve_copy(dve, "ab_qk", qk)
            dve_copy(dve, "ab_v", vF, after=lambda s: dve_gate_logs(dve, link, s))
            dve_plain(dve, "ab_o", after=lambda s: dve_gate_sums(dve, link, s))
            dve_copy(dve, "ab_xb", xb)
            dve_plain(dve, "ab_gate", after=lambda s: dve_lru_rate(dve, link) if s == 1 else None)
            dve_gate_columns(dve)
            dve_mlstm(dve, link)
            dve_lru(dve, link)
            dve_add(dve, "ab_out1", after="ab_out0")
            dve_norm(dve, 5)
            dve_mlp(dve, 0)
            dve_norm(dve, 6)
            dve_copy(dve, "c_q", cq)
            dve_copy(dve, "c_k", ck, after=lambda s: dve_rope(dve, c_items(), (2 * s, 2 * s + 1), T2, rope_c, c_rope, 16))
            dve_copy(dve, "c_v", cvF, after=lambda s: dve_rope(dve, c_items(), (8 + 2 * s, 9 + 2 * s), T2, rope_c, c_rope, 16))
            dve_diff(dve, link)
            dve_add(dve, "c_out")
            dve_norm(dve, 7)
            dve_mlp(dve, 1)
            dve_norm(dve, 8)

        @block.gpsimd
        def _(pool):
            link = chain(pool, "pool")
            load_biases(pool)
            load_late_constants(pool)
            pool_rpb(pool, link)
            load_ada_ring(pool)
            load_ada_pairs(pool, 2, 34)
            pool_y_sum(pool, 0)
            load_ada_pairs(pool, 34, 40)
            pool_ffn(pool, 0, 1)
            pool_ret(pool)
            pool_y_sum(pool, 2)
            pool_ffn(pool, 1, 3)
            load_second(pool)
            pool_mlstm(pool)
            pool_mlp_in(pool, 0, 0)
            pool_mlp_in(pool, 0, 1)
            pool_mlp_in(pool, 1, 0)
            pool_mlp_in(pool, 1, 1)

        @block.tensor
        def _(pe):
            pe_norm(pe, 0)
            pe_ada_first(pe)
            pe_rpb(pe, 0, 3)
            hyb = (lambda k: H_hi[T1][:, k, :], lambda k: H_lo[T1][:, k, :])
            for i, name in enumerate(("hyb_g", "hyb_u", "hyb_v", "hyb_k", "hyb_q")):
                project(pe, name, *hyb, need=h_need(pe, 0) if i == 0 else None,
                        after=(lambda s, i=i: pe_ada_sum(pe, 2 + 2 * i + s)) if i else
                        lambda s: pe_rpb(pe, 3, 6) if s == 0 else None)
            pe_sgu(pe)
            pe_attn(pe)
            project(pe, "hyb_out", *hyb, need=lambda k: pe.wait_ge(at_lo, NU // 2) if k < 4 else pe.wait_ge(sgu_lo, k - 3))
            pe_ada_ring(pe, 64, 68)
            pe_residual(pe, 0)
            pe_ada_ring(pe, 68, 72)
            pe_norm(pe, 1)
            pe_ada_ring(pe, 72, 76)
            pe_ffn_halves(pe, 0, 1)
            pe_norm(pe, 2)
            ret = (lambda k: H_hi[T1][:, k, LAT:T1], lambda k: H_lo[T1][:, k, LAT:T1])
            project(pe, "ret_k", *hyb, need=h_need(pe, 2))
            all_freed(pe, "ret_k")
            project(pe, "ret_v", *hyb, after=lambda s: pe_rope(pe, rope_items(), [s], SEQ, swap_ret, 0))
            project(pe, "ret_q", *ret)
            all_freed(pe, "ret_q")
            project(pe, "ret_g", *ret, after=lambda s: pe_rope(pe, rope_items(), [RH + s], SEQ, swap_ret, 0))
            pe_ret(pe)
            project(pe, "ret_out", lambda k: H_hi[SEQ][:, k, :], lambda k: H_lo[SEQ][:, k, :],
                    need=lambda k: pe.wait_ge(r_lo, k // 2 + 1))
            pe_residual(pe, 2)
            pe_norm(pe, 3)
            pe_ffn_halves(pe, 1, 3)
            pe_norm(pe, 4)
            second = (lambda k: H_hi[T2][:, k, :], lambda k: H_lo[T2][:, k, :])
            project(pe, "ab_if", *second, need=h_need(pe, 4))
            project(pe, "ab_qk", *second)
            project(pe, "ab_v", *second)
            all_freed(pe, "ab_v")
            project(pe, "ab_o", *second, after=lambda s: pe_turn_values(pe, vF, 0, wk, 2, TURNS[s]))
            project(pe, "ab_xb", *second)
            project(pe, "ab_gate", *second)
            pe_mlstm(pe)
            pe_lru(pe)
            pe.wait_ge(l_act, 16)
            project(pe, "ab_out0", *second, need=lambda k: pe.wait_ge(m_lo, k // 2 + 1))
            project(pe, "ab_out1", lambda k: H_hi[T2][:, 8 + k, :], lambda k: H_lo[T2][:, 8 + k, :],
                    need=lambda k: pe.wait_ge(l_lo, 1))
            pe_norm(pe, 5)
            pe_mlp(pe, 0, 5)
            pe_norm(pe, 6)
            project(pe, "c_q", *second, need=h_need(pe, 6))
            all_freed(pe, "c_q")
            project(pe, "c_k", *second, after=lambda s: pe_rope(pe, c_items(), (2 * s, 2 * s + 1), T2, swap_c, 16))
            all_freed(pe, "c_k")
            project(pe, "c_v", *second, after=lambda s: pe_rope(pe, c_items(), (8 + 2 * s, 9 + 2 * s), T2, swap_c, 16))
            pe_diff(pe)
            project(pe, "c_out", *second, need=lambda k: pe.wait_ge(c_lo, k + 1))
            pe_norm(pe, 7)
            pe_mlp(pe, 1, 7)
            pe_norm(pe, 8)


def _slots(w, cols=256):
    rows, m = w.shape
    return np.ascontiguousarray(w.reshape(rows // P, P, m // cols, cols).transpose(2, 1, 0, 3)
                                .reshape(m // cols, P, rows // P * cols))


def _chunks(v):
    return np.ascontiguousarray(v.reshape(-1, P).T)


def _packed(a):
    cols = np.zeros((P, NVEC), np.float32)

    def put(name, block):
        cols[:block.shape[0], VEC[name]:VEC[name] + block.shape[1]] = block
    both = np.stack([a["c"][0], a["c_ctx"]])
    put("c", both.reshape(2, DC, P).transpose(2, 1, 0).reshape(P, 2 * DC))
    for name, v in [("norm_g", a["norm_g"]), ("ada_b", a["ada_b"]), ("conv_w", a["ffn_conv_w"]), ("conv_b", a["ffn_conv_b"]),
                    ("gn_g", a["ret_gn_g"]), ("norm_mix", a["norm_mix_2"]), ("norm_mlp", a["norm_mlp_2"]),
                    ("norm_final", a["norm_final_2"]), ("mlstm_norm", a["mlstm_norm_2"]), ("lru_conv_w", a["lru_conv_w_2"]),
                    ("lru_conv_b", a["lru_conv_b_2"]), ("lru_b_r", a["lru_b_r_2"]), ("lru_b_i", a["lru_b_i_2"]),
                    ("lru_lam", a["lru_lambda_2"]), ("subln", a["c_subln_2"])]:
        put(name, _chunks(v))
    put("decay", np.broadcast_to(a["ret_log_decay"].reshape(1, 16), (P, 16)))
    put("lambda", np.broadcast_to(a["c_lambda_2"].reshape(1, 256), (P, 256)))
    put("if_bias", a["ab_if_bias_2"].reshape(2, 4).T)
    put("eps", np.full((P, 1), EPS, np.float32))
    return cols


def _swap(pairs):
    m = np.zeros((P, P), np.float32)
    for i, j in pairs:
        m[j, i] = -1.0
        m[i, j] = 1.0
    return m


def _constants():
    c = {"ident": np.eye(P, dtype=np.float32), "ones": np.ones((P, P), np.float32), "one_row": np.ones((P, T2), np.float32)}
    flip = np.zeros((P, P), np.float32)
    flip[np.arange(P), np.concatenate([np.arange(64)[::-1], 64 + np.arange(64)[::-1]])] = 1.0
    c["flip"] = flip
    c["swap_ret"] = _swap([(i, i + 64) for i in range(64)])
    c["swap_c"] = _swap([(b + i, b + i + 8) for b in (0, 64) for i in range(8)])
    sel = np.zeros((P, 4, P), np.float32)
    for h in range(4):
        sel[h, h, :] = 1.0
    c["head_sel"] = sel
    tok = np.arange(SEQ)
    inv = (np.float32(10000.0) ** (-np.arange(32, dtype=np.float32) / np.float32(32))).astype(np.float32)
    ang = np.concatenate([(tok // GRID_W).astype(np.float32)[:, None] * inv, (tok % GRID_W).astype(np.float32)[:, None] * inv], -1)
    ang = np.concatenate([ang, ang], -1).T
    c["rope_ret"] = np.stack([np.cos(ang), np.sin(ang)], 1).astype(np.float32)
    inv2 = (np.float32(500000.0) ** (-np.arange(0, 16, 2, dtype=np.float32) / np.float32(16))).astype(np.float32)
    ang2 = np.arange(T2, dtype=np.float32)[None, :] * inv2[:, None]
    cs, sn = np.ones((P, T2), np.float32), np.zeros((P, T2), np.float32)
    for b in (0, 8, 64, 72):
        cs[b:b + 8], sn[b:b + 8] = np.cos(ang2), np.sin(ang2)
    c["rope_c"] = np.stack([cs, sn], 1)
    c["dist"] = (np.arange(SEQ)[None, :] - np.arange(P)[:, None]).astype(np.float32)
    mask = np.zeros((P, 3, T2), np.float32)
    for i, (t0, n) in enumerate(TILES2):
        mask[:, i, :] = np.where(np.arange(T2)[None, :] <= t0 + np.arange(P)[:, None], 0.0, NEG)
    c["c_mask"] = mask
    return c


def _weights(a):
    w = {"ada": np.concatenate([_slots(a["ada_w"][i]) for i in range(2)])}
    for i in range(2):
        win, wout = a["ffn_w_in"][i], a["ffn_w_out"][i]
        pair = win.reshape(D, 2, 22, P).transpose(0, 2, 1, 3).reshape(D, 2 * 22 * P)
        for half in range(2):
            w[f"ffn{i}_in{half}"] = _slots(pair[:, half * 2816:(half + 1) * 2816])
            w[f"ffn{i}_out{half}"] = _slots(wout[half * 1408:(half + 1) * 1408], P)
            w[f"mlp{i}_in{half}"] = _slots(a["mlp_w1_2"][i][:, half * 2048:(half + 1) * 2048])
            w[f"mlp{i}_out{half}"] = _slots(a["mlp_w2_2"][i][half * 2048:(half + 1) * 2048], P)
    hyb = a["hyb_w_in"][0]
    for j, name in enumerate("qkvug"):
        w["hyb_" + name] = _slots(hyb[:, j * 512:(j + 1) * 512])
    w["hyb_out"] = _slots(a["hyb_w_out"][0])
    ret = a["ret_w_in"][0]
    for name, x, y in [("q", 0, 1024), ("k", 1024, 2048), ("v", 2048, 4096), ("g", 4096, 6144)]:
        w["ret_" + name] = _slots(ret[:, x:y])
    w["ret_out"] = _slots(a["ret_w_out"][0], P)
    ab = a["ab_w_in_2"][0]
    gates = np.zeros((D, 256), np.float32)
    gates[:, 0:4], gates[:, 128:132] = ab[:, 4096:4100], ab[:, 4100:4104]
    w["ab_if"] = _slots(gates)
    for name, x, y in [("qk", 0, 2048), ("v", 2048, 3072), ("o", 3072, 4096), ("xb", 4104, 5128), ("gate", 5128, 6152)]:
        w["ab_" + name] = _slots(ab[:, x:y])
    for half in range(2):
        w[f"ab_out{half}"] = _slots(a["ab_w_out_2"][0][half * D:(half + 1) * D])
    for j, name in enumerate("qkv"):
        w["c_" + name] = _slots(a["c_w_in_2"][0][:, j * D:(j + 1) * D])
    w["c_out"] = _slots(a["c_w_out_2"][0])
    return w


def kernel(**inputs):
    import concourse.bacc as _bacc
    from concourse.bass_utils import run_bass_kernel_spmd as _run

    a = {k: np.asarray(v) for k, v in inputs.items()}
    arrays = {"w_" + k: v for k, v in _weights(a).items() if k in {p.name for p in PROJ} | {"ada"}}
    arrays.update(_constants())
    arrays["vec"] = _packed(a)
    arrays["x"] = np.concatenate([a["ctx"][0], a["x"][0]]).T.reshape(DC, P, T1).transpose(1, 0, 2)
    arrays["meta"] = a["meta_tokens_2"].T.reshape(DC, P, META).transpose(1, 0, 2)
    arrays["na_rpb"] = a["na_rpb"].reshape(-1)
    arrays["sgu_w"] = a["sgu_w"][0].transpose(2, 0, 1)
    arrays["sgu_b"] = np.repeat(a["sgu_b"][0].reshape(4, 2, P), 64, axis=1).transpose(1, 0, 2)
    for name, w in (("lru_wr", a["lru_w_r_2"]), ("lru_wi", a["lru_w_i_2"])):
        arrays[name] = w[0].transpose(1, 0, 2)
    arrays = {k: np.ascontiguousarray(v) for k, v in arrays.items()}
    nc = _bacc.Bacc("TRN2", target_bir_lowering=False, num_devices=1)
    t = {k: nc.dram_tensor("in_" + k, v.shape, F32, kind="ExternalInput").ap() for k, v in arrays.items()}
    out = nc.dram_tensor("out_0", (P, DC, SEQ), F32, kind="ExternalOutput").ap()
    stack_kernel(nc, t, out, PROJ)
    r = _run(nc, [{"in_" + k: v for k, v in arrays.items()}], core_ids=[0])
    got = r.results[0]["out_0"]
    return np.ascontiguousarray(got.transpose(2, 1, 0)).reshape(1, SEQ, D)
```
